# Optimizing a Trainium2 kernel written in Bass

```python
import math
import jax
import jax.numpy as jnp
from jax import lax
import numpy as np

D_MODEL = 1024
BATCH = 1
SEQ = 512
DEPTH = 2

HEAD_DIM = 64
D_MIX = D_MODEL
M_HEADS = 4
M_CHUNK = 64
G_HEADS = 4
G_CHUNK = 64
CONV_K = 4
N_HEADS = 8
N_KV_HEADS = 2
N_GROUP = N_HEADS // N_KV_HEADS
CMP_BLOCK = 32
CMP_STRIDE = 16
CMP_HIDDEN = 256
SLC_BLOCK = 64
N_SELECTED = 16
WINDOW = 512
Q_BLOCK = 128
ROPE_THETA = 10000.0
D_FF = 2816
EPS = 1e-6
NEG = -1e30
BIG = 1e30

M_WIDTH = M_HEADS * HEAD_DIM
G_WIDTH = G_HEADS * HEAD_DIM
N_WIDTH = N_HEADS * HEAD_DIM
KV_WIDTH = N_KV_HEADS * HEAD_DIM
M_IN = 4 * M_WIDTH + 2 * M_HEADS
G_IN = 4 * G_WIDTH + 2 * G_HEADS
N_IN = N_WIDTH + 6 * KV_WIDTH + 3 * N_HEADS
IN_WIDTH = M_IN + G_IN + N_IN

kernel_name = 'hybrid_mlstm_gdn_nsa_macaron'

def rms_norm(x, w):
    xf = x.astype(jnp.float32)
    y = xf * lax.rsqrt(jnp.mean(xf * xf, axis=-1, keepdims=True) + EPS)
    return y * w.astype(jnp.float32)

def l2_normalize(x):
    return x * lax.rsqrt(jnp.sum(x * x, axis=-1, keepdims=True) + EPS)

def rope(x, pos):
    half = HEAD_DIM // 2
    inv_freq = jnp.power(ROPE_THETA, -jnp.arange(half, dtype=jnp.float32) / half)
    ang = pos.astype(jnp.float32)[:, None] * inv_freq[None, :]
    cos, sin = jnp.cos(ang), jnp.sin(ang)
    x1, x2 = x[..., :half], x[..., half:]
    return jnp.concatenate([x1 * cos - x2 * sin, x1 * sin + x2 * cos], axis=-1)

def to_heads(x, n_heads):
    b, t, _ = x.shape
    return x.reshape(b, t, n_heads, HEAD_DIM).transpose(0, 2, 1, 3)

def from_heads(x):
    b, h, t, d = x.shape
    return x.transpose(0, 2, 1, 3).reshape(b, t, h * d)

def adaln(x, w, shift, scale):
    return (rms_norm(x, w) * (1.0 + scale) + shift).astype(x.dtype)

def swiglu(h, w_up, w_down):
    gate, up = jnp.split(h @ w_up, 2, axis=-1)
    return (jax.nn.silu(gate) * up) @ w_down

def mlstm_group(p, gate_b, norm_w):
    b, t, _ = p.shape
    nc = t // M_CHUNK
    w = M_WIDTH
    q = to_heads(p[..., 0:w], M_HEADS) * (HEAD_DIM ** -0.5)
    k = to_heads(p[..., w:2 * w], M_HEADS)
    v = to_heads(p[..., 2 * w:3 * w], M_HEADS)
    o_gate = jax.nn.sigmoid(p[..., 3 * w:4 * w])
    gates = p[..., 4 * w:] + gate_b.reshape(-1)
    log_i = gates[..., :M_HEADS].transpose(0, 2, 1)
    log_f = jax.nn.log_sigmoid(gates[..., M_HEADS:]).transpose(0, 2, 1)
    ch = lambda a: a.reshape(b, M_HEADS, nc, M_CHUNK, *a.shape[3:])
    q, k, v, log_i, log_f = ch(q), ch(k), ch(v), ch(log_i), ch(log_f)
    cum = jnp.cumsum(log_f, axis=-1)
    g_tot = cum[..., -1]
    a = g_tot[..., None] - cum + log_i
    m_loc = jnp.max(a, axis=-1)
    wgt = jnp.exp(a - m_loc[..., None])
    c_loc = jnp.einsum('bhcl,bhcld,bhcle->bhcde', wgt, k, v)
    n_loc = jnp.einsum('bhcl,bhcld->bhcd', wgt, k)

    def step(carry, inp):
        c_st, n_st, m_st = carry
        g_c, m_l, c_l, n_l = inp
        m_new = jnp.maximum(g_c + m_st, m_l)
        s_old = jnp.exp(g_c + m_st - m_new)
        s_new = jnp.exp(m_l - m_new)
        c_next = s_old[..., None, None] * c_st + s_new[..., None, None] * c_l
        n_next = s_old[..., None] * n_st + s_new[..., None] * n_l
        return (c_next, n_next, m_new), (c_st, n_st, m_st)

    init = (jnp.zeros((b, M_HEADS, HEAD_DIM, HEAD_DIM), jnp.float32),
            jnp.zeros((b, M_HEADS, HEAD_DIM), jnp.float32),
            jnp.zeros((b, M_HEADS), jnp.float32))
    xs = (jnp.moveaxis(g_tot, 2, 0), jnp.moveaxis(m_loc, 2, 0),
          jnp.moveaxis(c_loc, 2, 0), jnp.moveaxis(n_loc, 2, 0))
    _, (c_prev, n_prev, m_prev) = lax.scan(step, init, xs)
    c_prev = jnp.moveaxis(c_prev, 0, 2)
    n_prev = jnp.moveaxis(n_prev, 0, 2)
    m_prev = jnp.moveaxis(m_prev, 0, 2)

    causal = jnp.tril(jnp.ones((M_CHUNK, M_CHUNK), dtype=bool))
    d = jnp.where(causal, cum[..., :, None] - cum[..., None, :] + log_i[..., None, :], -jnp.inf)
    m_inter = cum + m_prev[..., None]
    m_t = jnp.maximum(m_inter, jnp.max(d, axis=-1))
    s = jnp.einsum('bhctd,bhcjd->bhctj', q, k) * jnp.exp(d - m_t[..., None])
    inter = jnp.exp(m_inter - m_t)
    num = (jnp.einsum('bhctj,bhcje->bhcte', s, v)
           + inter[..., None] * jnp.einsum('bhctd,bhcde->bhcte', q, c_prev))
    den = jnp.sum(s, axis=-1) + inter * jnp.einsum('bhctd,bhcd->bhct', q, n_prev)
    den = jnp.maximum(jnp.abs(den), jnp.exp(-m_t))
    h = (num / den[..., None]).reshape(b, M_HEADS, t, HEAD_DIM)
    return o_gate * from_heads(rms_norm(h, norm_w))

def causal_depthwise_conv(x, w):
    c = x.shape[-1]
    return lax.conv_general_dilated(x, w[:, None, :], window_strides=(1,), padding=[(CONV_K - 1, 0)],
                                    dimension_numbers=('NWC', 'WIO', 'NWC'), feature_group_count=c)

def gdn_group(p, conv_w, a_log, dt_bias, norm_w):
    b, t, _ = p.shape
    nc = t // G_CHUNK
    w = G_WIDTH
    qkv = jax.nn.silu(causal_depthwise_conv(p[..., :3 * w], conv_w.astype(jnp.float32)))
    q = l2_normalize(to_heads(qkv[..., :w], G_HEADS)) * (HEAD_DIM ** -0.5)
    k = l2_normalize(to_heads(qkv[..., w:2 * w], G_HEADS))
    v = to_heads(qkv[..., 2 * w:3 * w], G_HEADS)
    z = p[..., 3 * w:4 * w]
    a_pre = p[..., 4 * w:4 * w + G_HEADS].transpose(0, 2, 1)
    beta = jax.nn.sigmoid(p[..., 4 * w + G_HEADS:]).transpose(0, 2, 1)
    log_alpha = -jnp.exp(a_log.astype(jnp.float32))[None, :, None] * jax.nn.softplus(a_pre + dt_bias[None, :, None])
    ch = lambda a: a.reshape(b, G_HEADS, nc, G_CHUNK, *a.shape[3:])
    q, k, v, beta, log_alpha = ch(q), ch(k), ch(v), ch(beta), ch(log_alpha)
    gam = jnp.cumsum(log_alpha, axis=-1)
    idx = jnp.arange(G_CHUNK)
    strict = idx[:, None] > idx[None, :]
    incl = idx[:, None] >= idx[None, :]
    diff = gam[..., :, None] - gam[..., None, :]
    kk = jnp.einsum('bhctd,bhcjd->bhctj', k, k)
    a_mat = beta[..., None] * kk * jnp.exp(jnp.where(strict, diff, -jnp.inf))
    eye = jnp.eye(G_CHUNK, dtype=jnp.float32)
    rhs = jnp.concatenate([beta[..., None] * v, (beta * jnp.exp(gam))[..., None] * k], axis=-1)
    sol = lax.linalg.triangular_solve(eye + a_mat, rhs, left_side=True, lower=True, unit_diagonal=True)
    u0, w_mat = sol[..., :HEAD_DIM], sol[..., HEAD_DIM:]
    p_mat = jnp.einsum('bhctd,bhcjd->bhctj', q, k) * jnp.exp(jnp.where(incl, diff, -jnp.inf))
    q_g = q * jnp.exp(gam)[..., None]
    k_d = k * jnp.exp(gam[..., -1:] - gam)[..., None]
    g_last = jnp.exp(gam[..., -1])

    def step(s, inp):
        u0_c, w_c, qg_c, p_c, kd_c, gl_c = inp
        u = u0_c - jnp.einsum('bhld,bhde->bhle', w_c, s)
        o = jnp.einsum('bhld,bhde->bhle', qg_c, s) + jnp.einsum('bhlj,bhje->bhle', p_c, u)
        s_next = gl_c[..., None, None] * s + jnp.einsum('bhld,bhle->bhde', kd_c, u)
        return s_next, o

    xs = (jnp.moveaxis(u0, 2, 0), jnp.moveaxis(w_mat, 2, 0), jnp.moveaxis(q_g, 2, 0),
          jnp.moveaxis(p_mat, 2, 0), jnp.moveaxis(k_d, 2, 0), jnp.moveaxis(g_last, 2, 0))
    _, o = lax.scan(step, jnp.zeros((b, G_HEADS, HEAD_DIM, HEAD_DIM), jnp.float32), xs)
    o = jnp.moveaxis(o, 0, 2).reshape(b, G_HEADS, t, HEAD_DIM)
    return from_heads(rms_norm(o, norm_w)) * jax.nn.silu(z)

def compress(blocks, pos_emb, w1, w2):
    b, h, n = blocks.shape[:3]
    flat = (blocks + pos_emb).reshape(b, h, n, CMP_BLOCK * HEAD_DIM)
    return jax.nn.silu(flat @ w1) @ w2

def nsa_group(p, qk_norm, cmp_pos, cmp_w1, cmp_w2):
    b, t, _ = p.shape
    scale = HEAD_DIM ** -0.5
    pos = jnp.arange(t, dtype=jnp.int32)
    q = rope(rms_norm(to_heads(p[..., :N_WIDTH], N_HEADS), qk_norm[0]), pos)
    kv = p[..., N_WIDTH:N_WIDTH + 6 * KV_WIDTH]
    k_cmp, v_cmp, k_slc, v_slc, k_win, v_win = [
        to_heads(kv[..., i * KV_WIDTH:(i + 1) * KV_WIDTH], N_KV_HEADS) for i in range(6)]
    gates = jax.nn.sigmoid(p[..., N_WIDTH + 6 * KV_WIDTH:])
    k_slc = rope(rms_norm(k_slc, qk_norm[2]), pos)
    k_win = rope(rms_norm(k_win, qk_norm[3]), pos)

    n_cmp = (t - CMP_BLOCK) // CMP_STRIDE + 1
    cmp_start = jnp.arange(n_cmp) * CMP_STRIDE
    cmp_idx = cmp_start[:, None] + jnp.arange(CMP_BLOCK)[None, :]
    cmp_end = cmp_start + CMP_BLOCK - 1
    kc = compress(k_cmp[:, :, cmp_idx], cmp_pos[0], cmp_w1[0], cmp_w2[0])
    kc = rope(rms_norm(kc, qk_norm[1]), cmp_end)
    vc = compress(v_cmp[:, :, cmp_idx], cmp_pos[1], cmp_w1[1], cmp_w2[1])

    n_slc = t // SLC_BLOCK
    n_sel = min(N_SELECTED, n_slc)
    ks_blocks = k_slc.reshape(b, N_KV_HEADS, n_slc, SLC_BLOCK, HEAD_DIM)
    vs_blocks = v_slc.reshape(b, N_KV_HEADS, n_slc, SLC_BLOCK, HEAD_DIM)
    slc_start = jnp.arange(n_slc) * SLC_BLOCK
    overlap = jnp.maximum(jnp.minimum(cmp_start[:, None] + CMP_BLOCK, slc_start[None, :] + SLC_BLOCK)
                          - jnp.maximum(cmp_start[:, None], slc_start[None, :]), 0).astype(jnp.float32) / CMP_BLOCK

    kw_pad = jnp.pad(k_win, ((0, 0), (0, 0), (WINDOW, 0), (0, 0)))
    vw_pad = jnp.pad(v_win, ((0, 0), (0, 0), (WINDOW, 0), (0, 0)))

    n_qb = t // Q_BLOCK
    q_blocks = jnp.moveaxis(q.reshape(b, N_KV_HEADS, N_GROUP, n_qb, Q_BLOCK, HEAD_DIM), 3, 0)
    g_blocks = gates.reshape(b, t, 3, N_KV_HEADS, N_GROUP).transpose(0, 3, 4, 1, 2)
    g_blocks = jnp.moveaxis(g_blocks.reshape(b, N_KV_HEADS, N_GROUP, n_qb, Q_BLOCK, 3), 3, 0)
    starts = jnp.arange(n_qb, dtype=jnp.int32) * Q_BLOCK
    bi = jnp.arange(b)[:, None, None, None]
    hi = jnp.arange(N_KV_HEADS)[None, :, None, None]
    blk = jnp.arange(n_slc)
    tok = jnp.arange(SLC_BLOCK)
    win_off = jnp.arange(Q_BLOCK + WINDOW)

    def attend_block(args):
        qb, gb, start = args
        tq = start + jnp.arange(Q_BLOCK)
        s_c = jnp.einsum('bhgqd,bhnd->bhgqn', qb, kc) * scale
        valid_c = cmp_end[None, :] <= tq[:, None]
        p_c = jax.nn.softmax(jnp.where(valid_c, s_c, NEG), axis=-1)
        p_c = p_c * jnp.any(valid_c, axis=-1)[:, None].astype(jnp.float32)
        o_c = jnp.einsum('bhgqn,bhnd->bhgqd', p_c, vc)
        imp = jnp.einsum('bhgqn,ns->bhqs', p_c, overlap)
        cur = tq // SLC_BLOCK
        forced = (blk[None, :] == 0) | (blk[None, :] == cur[:, None]) | (blk[None, :] == cur[:, None] - 1)
        imp = jnp.where(forced, BIG, imp)
        imp = jnp.where(slc_start[None, :] <= tq[:, None], imp, NEG)
        _, sel = lax.top_k(imp, n_sel)
        ks = ks_blocks[bi, hi, sel]
        vs = vs_blocks[bi, hi, sel]
        s_s = jnp.einsum('bhgqd,bhqnpd->bhgqnp', qb, ks) * scale
        tok_pos = sel[..., None] * SLC_BLOCK + tok
        valid_s = (tok_pos <= tq[:, None, None])[:, :, None]
        s_s = jnp.where(valid_s, s_s, NEG).reshape(b, N_KV_HEADS, N_GROUP, Q_BLOCK, n_sel * SLC_BLOCK)
        p_s = jax.nn.softmax(s_s, axis=-1).reshape(b, N_KV_HEADS, N_GROUP, Q_BLOCK, n_sel, SLC_BLOCK)
        o_s = jnp.einsum('bhgqnp,bhqnpd->bhgqd', p_s, vs)
        kw = lax.dynamic_slice_in_dim(kw_pad, start, Q_BLOCK + WINDOW, axis=2)
        vw = lax.dynamic_slice_in_dim(vw_pad, start, Q_BLOCK + WINDOW, axis=2)
        kpos = start - WINDOW + win_off
        dist = tq[:, None] - kpos[None, :]
        valid_w = (dist >= 0) & (dist < WINDOW) & (kpos[None, :] >= 0)
        s_w = jnp.einsum('bhgqd,bhkd->bhgqk', qb, kw) * scale
        p_w = jax.nn.softmax(jnp.where(valid_w, s_w, NEG), axis=-1)
        o_w = jnp.einsum('bhgqk,bhkd->bhgqd', p_w, vw)
        return gb[..., 0:1] * o_c + gb[..., 1:2] * o_s + gb[..., 2:3] * o_w

    out = lax.map(attend_block, (q_blocks, g_blocks, starts))
    out = jnp.moveaxis(out, 0, 3).reshape(b, N_HEADS, t, HEAD_DIM)
    return from_heads(out)

def hybrid_mixer(h, w_in, w_out, m_gate_b, m_norm_w, g_conv_w, g_a_log, g_dt_bias, g_norm_w,
                 n_qk_norm, n_cmp_pos, n_cmp_w1, n_cmp_w2):
    proj = (h @ w_in).astype(jnp.float32)
    y_m = mlstm_group(proj[..., :M_IN], m_gate_b, m_norm_w)
    y_g = gdn_group(proj[..., M_IN:M_IN + G_IN], g_conv_w, g_a_log, g_dt_bias, g_norm_w)
    y_n = nsa_group(proj[..., M_IN + G_IN:], n_qk_norm, n_cmp_pos, n_cmp_w1, n_cmp_w2)
    y = jnp.concatenate([y_m, y_g, y_n], axis=-1).astype(h.dtype)
    return y @ w_out

def setup_inputs(seed: int = 0) -> dict:
    key = jax.random.key(seed)
    ks = jax.random.split(key, 20)
    f32 = jnp.float32
    nrm = lambda k, shape, s: jax.random.normal(k, shape, f32) * s
    x = nrm(ks[0], (BATCH, SEQ, D_MODEL), 1.0)
    c = nrm(ks[1], (BATCH, D_MODEL), 1.0)
    ada_w = nrm(ks[2], (DEPTH, D_MODEL, 9 * D_MODEL), 0.5 * D_MODEL ** -0.5)
    ada_b = nrm(ks[3], (DEPTH, 9 * D_MODEL), 0.01)
    norm_w = 1.0 + nrm(ks[4], (DEPTH, 3, D_MODEL), 0.02)
    ffn_w_up = nrm(ks[5], (DEPTH, 2, D_MODEL, 2 * D_FF), D_MODEL ** -0.5)
    ffn_w_down = nrm(ks[6], (DEPTH, 2, D_FF, D_MODEL), D_FF ** -0.5)
    w_in = nrm(ks[7], (DEPTH, D_MODEL, IN_WIDTH), D_MODEL ** -0.5)
    w_out = nrm(ks[8], (DEPTH, D_MIX, D_MODEL), D_MIX ** -0.5)
    i_b = nrm(ks[9], (DEPTH, 1, M_HEADS), 0.01)
    f_b = 3.0 + nrm(ks[10], (DEPTH, 1, M_HEADS), 0.1)
    mlstm_gate_b = jnp.concatenate([i_b, f_b], axis=1)
    mlstm_norm_w = 1.0 + nrm(ks[11], (DEPTH, HEAD_DIM), 0.02)
    gdn_conv_w = nrm(ks[12], (DEPTH, CONV_K, 3 * G_WIDTH), CONV_K ** -0.5)
    gdn_a_log = jnp.log(jax.random.uniform(ks[13], (DEPTH, G_HEADS), f32, 1.0, 16.0))
    dt = jnp.exp(jax.random.uniform(ks[14], (DEPTH, G_HEADS), f32, math.log(1e-3), math.log(1e-1)))
    gdn_dt_bias = dt + jnp.log(-jnp.expm1(-dt))
    gdn_norm_w = 1.0 + nrm(ks[15], (DEPTH, HEAD_DIM), 0.02)
    nsa_qk_norm = 1.0 + nrm(ks[16], (DEPTH, 4, HEAD_DIM), 0.02)
    nsa_cmp_pos = nrm(ks[17], (DEPTH, 2, CMP_BLOCK, HEAD_DIM), 0.02)
    nsa_cmp_w1 = nrm(ks[18], (DEPTH, 2, CMP_BLOCK * HEAD_DIM, CMP_HIDDEN), (CMP_BLOCK * HEAD_DIM) ** -0.5)
    nsa_cmp_w2 = nrm(ks[19], (DEPTH, 2, CMP_HIDDEN, HEAD_DIM), CMP_HIDDEN ** -0.5)
    return {'x': x, 'c': c, 'ada_w': ada_w, 'ada_b': ada_b, 'norm_w': norm_w,
            'ffn_w_up': ffn_w_up, 'ffn_w_down': ffn_w_down, 'w_in': w_in, 'w_out': w_out,
            'mlstm_gate_b': mlstm_gate_b, 'mlstm_norm_w': mlstm_norm_w,
            'gdn_conv_w': gdn_conv_w, 'gdn_a_log': gdn_a_log, 'gdn_dt_bias': gdn_dt_bias,
            'gdn_norm_w': gdn_norm_w, 'nsa_qk_norm': nsa_qk_norm, 'nsa_cmp_pos': nsa_cmp_pos,
            'nsa_cmp_w1': nsa_cmp_w1, 'nsa_cmp_w2': nsa_cmp_w2}

def reference(x, c, ada_w, ada_b, norm_w, ffn_w_up, ffn_w_down, w_in, w_out,
              mlstm_gate_b, mlstm_norm_w, gdn_conv_w, gdn_a_log, gdn_dt_bias, gdn_norm_w,
              nsa_qk_norm, nsa_cmp_pos, nsa_cmp_w1, nsa_cmp_w2):
    b = x.shape[0]
    c_act = jax.nn.silu(c)
    for l in range(DEPTH):
        mod = (c_act @ ada_w[l] + ada_b[l]).reshape(b, 9, 1, D_MODEL)
        h = adaln(x, norm_w[l, 0], mod[:, 0], mod[:, 1])
        x = x + 0.5 * mod[:, 2] * swiglu(h, ffn_w_up[l, 0], ffn_w_down[l, 0])
        h = adaln(x, norm_w[l, 1], mod[:, 3], mod[:, 4])
        x = x + mod[:, 5] * hybrid_mixer(h, w_in[l], w_out[l], mlstm_gate_b[l], mlstm_norm_w[l],
                                         gdn_conv_w[l], gdn_a_log[l], gdn_dt_bias[l], gdn_norm_w[l],
                                         nsa_qk_norm[l], nsa_cmp_pos[l], nsa_cmp_w1[l], nsa_cmp_w2[l])
        h = adaln(x, norm_w[l, 2], mod[:, 6], mod[:, 7])
        x = x + 0.5 * mod[:, 8] * swiglu(h, ffn_w_up[l, 1], ffn_w_down[l, 1])
    return x


_drawn_inputs = setup_inputs


def setup_inputs(seed=0):
    import zlib

    import numpy as np

    out = dict(_drawn_inputs(seed))
    spreads = {}
    factors = {'ada_b': 4.539,
     'norm_w': 5.795,
     'mlstm_norm_w': 58.288,
     'gdn_a_log': 2.956,
     'gdn_norm_w': 8.0,
     'nsa_qk_norm': 8.0,
     'nsa_cmp_pos': 8.0}
    for name, (base, spread) in spreads.items():
        noise = np.random.default_rng([zlib.crc32(name.encode()), seed]).standard_normal(out[name].shape)
        drawn = base * np.exp(spread * noise) if base else spread * noise
        out[name] = jnp.asarray(drawn.astype(out[name].dtype))
    for name, factor in factors.items():
        out[name] = (out[name] * factor).astype(out[name].dtype)
    return out
```

```python
from contextlib import ExitStack

import numpy as np

import concourse.bass as bass
import concourse.mybir as mybir
from concourse.alu_op_type import AluOpType as ALU

F32 = mybir.dt.float32
ACT = mybir.ActivationFunctionType
AX = mybir.AxisListType

P = 128
D_MODEL, SEQ, DEPTH = 1024, 512, 2
D_FF = 2816
HD = 64
KT = D_MODEL // P
TT = SEQ // P
FT = D_FF // P
EPS = 1e-6
NEG = -1e30

M_HEADS, G_HEADS, N_HEADS, N_KV = 4, 4, 8, 2
GROUP = N_HEADS // N_KV
CMP_BLOCK, CMP_STRIDE, CMP_HIDDEN = 32, 16, 256
N_CMP = (SEQ - CMP_BLOCK) // CMP_STRIDE + 1
SCALE = HD ** -0.5

M_W, KV_W = M_HEADS * HD, N_KV * HD
C_MQ, C_MK, C_MV, C_MO, C_MG = 0, M_W, 2 * M_W, 3 * M_W, 4 * M_W
C_Z = C_MG + 2 * M_HEADS
C_GA = C_Z + G_HEADS * HD
C_GB = C_GA + G_HEADS
C_Q = C_GB + G_HEADS
C_KC = C_Q + N_HEADS * HD
C_VC = C_KC + KV_W
C_KS = C_VC + KV_W
C_VS = C_KS + KV_W
C_KWN = C_VS + KV_W
C_VWN = C_KWN + KV_W
C_NG = C_VWN + KV_W
TOK_W = C_NG + 3 * N_HEADS
N_PG = 8
PG = TOK_W // N_PG
N_CONV = 3 * G_HEADS * HD // P
CONV_K = 4
FIRST_SEM = 110
LEVELS = 6

ADA_CH = 18
ADA_SLOTS = 3

CONST_PARTS = [("ident", P), ("ones", P), ("upper", P), ("decay_sel", 2 * P), ("ident2", 2 * P),
               ("causal", SEQ), ("causal_t", P), ("level0", P), ("levels", LEVELS * P),
               ("cos", TT * HD), ("sin", TT * HD), ("cmp_cos", HD), ("cmp_sin", HD),
               ("cmp_mask", TT * N_CMP), ("cmp_any", TT)]
CONST_AT, CONST_W = {}, 0
for _n, _w in CONST_PARTS:
    CONST_AT[_n] = (CONST_W, _w)
    CONST_W += _w


def constants():
    p, f = np.arange(P)[:, None], np.arange(P)[None, :]
    c = {}
    c["ident"] = (p == f)
    c["ones"] = np.ones((P, P))
    c["upper"] = (p <= f)
    c["decay_sel"] = np.concatenate([(p > f), -1.0 * (p <= f)], 1)
    c["ident2"] = np.concatenate([(p == f), (p == f)], 1)
    c["causal"] = np.concatenate([np.zeros((P, SEQ - P)), np.where(f <= p, 0.0, NEG)], 1)
    c["causal_t"] = np.where(p <= f, 0.0, NEG)

    def level(s):
        return (p // (2 * s) == f // (2 * s)) & (p % (2 * s) < s) & (f % (2 * s) >= s)

    c["level0"] = level(1)
    c["levels"] = np.concatenate([level(2 << n) for n in range(LEVELS)], 1)
    half = HD // 2
    inv = np.power(np.float32(10000.0), -np.arange(half, dtype=np.float32) / np.float32(half)).astype(np.float32)

    def tables(pos):
        ang = pos.astype(np.float32)[:, None] * inv[None, :]
        cos, sin = np.cos(ang).astype(np.float32), np.sin(ang).astype(np.float32)
        return np.concatenate([cos, cos], 1), np.concatenate([-sin, sin], 1)

    cos, sin = tables(np.arange(SEQ))
    c["cos"] = cos.reshape(TT, P, HD).transpose(1, 0, 2).reshape(P, -1)
    c["sin"] = sin.reshape(TT, P, HD).transpose(1, 0, 2).reshape(P, -1)
    end = np.arange(N_CMP) * CMP_STRIDE + CMP_BLOCK - 1
    cc, cs = tables(end)
    pad = np.zeros((P - N_CMP, HD))
    c["cmp_cos"], c["cmp_sin"] = np.concatenate([cc, pad]), np.concatenate([cs, pad])
    t = (np.arange(TT)[None, :, None] * P + np.arange(P)[:, None, None])
    valid = end[None, None, :] <= t
    c["cmp_mask"] = np.where(valid, 0.0, NEG).reshape(P, -1)
    c["cmp_any"] = valid.any(-1)
    return np.ascontiguousarray(np.concatenate([np.asarray(c[n], np.float32) for n, _ in CONST_PARTS], 1))


class Env:
    pass


def at(t, i):
    dims = " ".join("xyz"[:len(t.shape) - 2])
    return t[:, bass.ds(i, 1)].rearrange(f"p a {dims} -> p (a {dims.split()[0]}) {' '.join(dims.split()[1:])}")


def dram(t, *idx):
    n = len(idx)
    v = t[tuple(bass.ds(i, 1) for i in idx)]
    lead = " ".join("abc"[:n])
    return v.rearrange(f"{lead} p n -> ({lead} p) n")


class Stage:

    def __init__(self, nc):
        self.nc, self.ctx, self.nums = nc, ExitStack(), []

    def __enter__(self):
        self.ctx.__enter__()
        return self

    def sem(self, name):
        s = self.ctx.enter_context(self.nc.semaphore(name, num=FIRST_SEM + len(self.nums)))
        self.nums.append(s.num)
        return s

    def sems(self, names):
        return [self.sem(n) for n in names.split()]

    def sb(self, name, shape):
        return self.ctx.enter_context(self.nc.sbuf_tensor(name, shape, F32))

    def __exit__(self, *a):
        if a[0] is None:
            self.nc.all_engine_barrier(sems_to_clear=range(min(self.nums), max(self.nums) + 1))
        return self.ctx.__exit__(*a)


def load_stage(nc, e, x_t, c_t, const):
    with Stage(nc) as st:
        loaded, = st.sems("loaded")
        with nc.Block() as block:
            @block.sync
            def _(sp):
                sp.dma_start(e.x[:], x_t).then_inc(loaded, 16)
                sp.dma_start(e.const[:], const).then_inc(loaded, 16)
                sp.dma_start(e.c[:], c_t).then_inc(loaded, 16)
                sp.wait_ge(loaded, 48)

            @block.vector
            def _(dve):
                nc.vector.memset(e.eps[:], EPS)


def ada_stage(nc, e, L, tag, ada_w, ada_b, norm_w):
    with Stage(nc) as st:
        loaded = [st.sem(f"ada_loaded{b}{tag}") for b in range(ADA_SLOTS)]
        small, c_ready, acc_ready, acc_free, summed, mod_ready, chain = st.sems(
            " ".join(f"{n}{tag}" for n in "ada_small c_ready acc_ready acc_free summed mod_ready ada_chain".split()))
        w = st.sb("ada_w_sb", [P, ADA_SLOTS, KT, 512])
        acc = st.sb("ada_acc", [P, ADA_SLOTS, 512])
        bias = st.sb("ada_bias", [P, 9 * KT])
        nw = st.sb("norm_w_sb", [P, 3 * KT])
        mod, csil = e.mod, e.csil
        cols = e.bank[0]
        with nc.Block() as block:
            @block.sync
            def _(sp):
                sp.dma_start(bias[:], dram(ada_b, L)).then_inc(small, 16)
                sp.dma_start(nw[:], dram(norm_w, L)).then_inc(small, 16)
                with sp.Fori(0, ADA_CH // ADA_SLOTS) as i:
                    for b in range(ADA_SLOTS):
                        sp.wait_ge(acc_ready, i * ADA_SLOTS + b + 1)
                        sp.dma_start(w[:, b].rearrange("p k n -> p (k n)"),
                                     dram(ada_w, L, i * ADA_SLOTS + b)).then_inc(loaded[b], 16)

            @block.scalar
            def _(act):
                nc.scalar.activation(csil[:], e.c[:], ACT.Silu).then_inc(c_ready, 1)

            @block.vector
            def _(dve):
                dve.sem_inc(acc_ready, ADA_SLOTS)
                dve.wait_ge(c_ready, 1)
                with dve.Fori(0, ADA_CH // ADA_SLOTS) as i:
                    for b in range(ADA_SLOTS):
                        dve.wait_ge(loaded[b], i * 16 + 16)
                        dve.wait_ge(acc_free, i * ADA_SLOTS + b + 1)
                        nc.vector.tensor_scalar(acc[:, b], w[:, b, 0], csil[:, 0:1], None, ALU.mult)
                        for k in range(1, KT):
                            dve.drain()
                            last = nc.vector.scalar_tensor_tensor(acc[:, b], w[:, b, k], csil[:, k:k + 1], acc[:, b],
                                                                  ALU.mult, ALU.add)
                        last.then_inc(acc_ready, 1)
                dve.wait_ge(small, 32)
                dve.wait_ge(summed, 1)
                nc.vector.tensor_tensor(mod[:], cols[:, 0:9 * KT], bias[:], ALU.add)
                dve.drain()
                for s in range(3):
                    v = mod[:, (3 * s + 1) * KT:(3 * s + 2) * KT]
                    nc.vector.scalar_tensor_tensor(e.coef[:, s], v, 1.0, nw[:, s * KT:(s + 1) * KT], ALU.add, ALU.mult)
                    g = mod[:, (3 * s + 2) * KT:(3 * s + 3) * KT]
                    nc.vector.tensor_scalar(e.gate[:, s], g, 1.0 if s == 1 else 0.5, None, ALU.mult)

            @block.tensor
            def _(pe):
                pe.sem_inc(acc_free, ADA_SLOTS)
                with pe.Fori(0, ADA_CH // ADA_SLOTS) as i:
                    for b in range(ADA_SLOTS):
                        pe.wait_ge(acc_ready, i * ADA_SLOTS + b + 1 + ADA_SLOTS)
                        for m in range(4):
                            last = nc.tensor.matmul(cols[:, bass.ds((i * ADA_SLOTS + b) * 4 + m, 1)],
                                                    acc[:, b, m * P:(m + 1) * P], e.k("ones")[:, 0:1],
                                                    start=True, stop=True)
                        last.then_inc(acc_free, 1)
                pe.drain().then_inc(summed, 1)


class Norm:

    def __init__(self, nc, e, st, sub, tag):
        self.nc, self.e, self.sub = nc, e, sub
        (self.squared, self.summed, self.rooted, self.scaled, self.ready) = st.sems(
            " ".join(f"{n}{tag}" for n in "squared sumsq_ready root_ready scaled h_ready".split()))
        self.rstd = st.sb("rstd" + tag, [P, SEQ])
        self.root = st.sb("root" + tag, [P, SEQ])

    def scalar(self, act):
        nc, e = self.nc, self.e
        for k in range(KT):
            nc.scalar.activation(e.h[:, k], e.x[:, k], ACT.Square).then_inc(self.squared, 1)
        act.wait_ge(self.summed, 1)
        nc.scalar.activation(self.root[:], e.bank[7][:], ACT.Sqrt, bias=e.eps[:, 0:1], scale=1.0 / D_MODEL).then_inc(self.rooted, 1)
        for k in range(KT):
            act.wait_ge(self.scaled, k + 1)
            nc.scalar.activation(e.h[:, k], e.h[:, k], ACT.Identity, scale=e.coef[:, self.sub, k:k + 1],
                                 bias=e.mod[:, 3 * self.sub * KT + k:3 * self.sub * KT + k + 1]).then_inc(self.ready, 1)

    def tensor(self, pe):
        for k in range(KT):
            pe.wait_ge(self.squared, k + 1)
            last = self.nc.tensor.matmul(self.e.bank[7][:], self.e.k("ones"), self.e.h[:, k], start=k == 0, stop=k == KT - 1)
        last.then_inc(self.summed, 1)

    def vector(self, dve):
        nc, e = self.nc, self.e
        dve.wait_ge(self.rooted, 1)
        nc.vector.reciprocal(self.rstd[:], self.root[:])
        dve.drain()
        for k in range(KT):
            nc.vector.tensor_tensor(e.h[:, k], e.x[:, k], self.rstd[:], ALU.mult).then_inc(self.scaled, 1)


def ffn_stage(nc, e, L, which, w_up, w_down):
    sub, tag = 2 * which, f"_f{which}"
    names = lambda text: " ".join(n + tag for n in text.split())
    with Stage(nc) as st:
        up_loaded = [st.sem(f"up_loaded{b}{tag}") for b in range(2)]
        down_loaded = [st.sem(f"down_loaded{b}{tag}") for b in range(2)]
        gate_ready, up_ready, silu_ready, hidden_ready, down_ready, down_free = st.sems(
            names("gate_ready up_ready silu_ready hidden_ready down_ready down_free"))
        norm = Norm(nc, e, st, sub, tag)
        hidden = st.sb("hidden" + tag, [P, FT, SEQ])
        wu = st.sb("w_up_sb" + tag, [P, 2, KT, 2, P])
        wd = st.sb("w_down_sb" + tag, [P, 2, FT, P])
        sg = st.sb("silu_sb" + tag, [P, 2, SEQ])
        with nc.Block() as block:
            @block.sync
            def _(sp):
                def load_up(n, b):
                    sp.dma_start(wu[:, b].rearrange("p k g m -> p (k g m)"), dram(w_up, L * 2 + which, n)).then_inc(up_loaded[b], 16)

                def load_down(m, b):
                    sp.dma_start(wd[:, b].rearrange("p f m -> p (f m)"), dram(w_down, L * 2 + which, m)).then_inc(down_loaded[b], 16)

                for b in range(2):
                    load_up(b, b)
                with sp.Fori(1, FT // 2) as i:
                    for b in range(2):
                        sp.wait_ge(up_ready, i * 2 + b - 1)
                        load_up(i * 2 + b, b)
                for b in range(2):
                    load_down(b, b)
                with sp.Fori(1, KT // 2) as i:
                    for b in range(2):
                        sp.wait_ge(down_ready, i * 2 + b - 1)
                        load_down(i * 2 + b, b)

            @block.tensor
            def _(pe):
                norm.tensor(pe)
                pe.wait_ge(norm.ready, KT)
                with pe.Fori(0, FT // 2) as i:
                    for b in range(2):
                        pe.wait_ge(up_loaded[b], i * 16 + 16)
                        pe.wait_ge(hidden_ready, i * 2 + b + 1)
                        for side, done in ((0, gate_ready), (1, up_ready)):
                            for k in range(KT):
                                last = nc.tensor.matmul(e.bank[2 * b + side][:], wu[:, b, k, side], e.h[:, k],
                                                        start=k == 0, stop=k == KT - 1)
                            last.then_inc(done, 1)
                pe.wait_ge(hidden_ready, FT + 2)
                with pe.Fori(0, KT // 2) as i:
                    for b in range(2):
                        pe.wait_ge(down_loaded[b], i * 16 + 16)
                        pe.wait_ge(down_free, i * 2 + b + 1)
                        for f in range(FT):
                            last = nc.tensor.matmul(e.bank[4 + b][:], wd[:, b, f], hidden[:, f],
                                                    start=f == 0, stop=f == FT - 1)
                        last.then_inc(down_ready, 1)

            @block.scalar
            def _(act):
                norm.scalar(act)
                with act.Fori(0, FT // 2) as i:
                    for b in range(2):
                        act.wait_ge(gate_ready, i * 2 + b + 1)
                        act.wait_ge(hidden_ready, i * 2 + b + 1)
                        nc.scalar.activation(sg[:, b], e.bank[2 * b][:], ACT.Silu).then_inc(silu_ready, 1)

            @block.vector
            def _(dve):
                dve.sem_inc(hidden_ready, 2)
                dve.sem_inc(down_free, 2)
                norm.vector(dve)
                with dve.Fori(0, FT // 2) as i:
                    for b in range(2):
                        dve.wait_ge(up_ready, i * 2 + b + 1)
                        dve.wait_ge(silu_ready, i * 2 + b + 1)
                        nc.vector.tensor_tensor(at(hidden, i * 2 + b), e.bank[2 * b + 1][:], sg[:, b], ALU.mult).then_inc(hidden_ready, 1)
                with dve.Fori(0, KT // 2) as i:
                    for b in range(2):
                        dve.wait_ge(down_ready, i * 2 + b + 1)
                        xm = at(e.x, i * 2 + b)
                        nc.vector.scalar_tensor_tensor(xm, e.bank[4 + b][:], e.gate[:, sub, bass.ds(i * 2 + b, 1)], xm,
                                                       ALU.mult, ALU.add).then_inc(down_free, 1)


def proj_stage(nc, e, L, w_tok, w_conv, conv_w):
    with Stage(nc) as st:
        tok_loaded = [st.sem(f"tok_loaded{b}") for b in range(2)]
        ch_loaded = [st.sem(f"ch_loaded{b}") for b in range(2)]
        small, tok_ready, even_free, odd_free, ch_ready, padded, convolved, conv_out, pad_zero = st.sems(
            "taps_loaded tok_ready even_free odd_free ch_ready padded convolved conv_out pad_zero")
        norm = Norm(nc, e, st, 1, "_p")
        wt = st.sb("w_tok_sb", [P, 2, KT, PG])
        wc = st.sb("w_conv_sb", [P, 2, KT, P])
        taps = st.sb("taps", [P, N_CONV, CONV_K])
        pad = st.sb("conv_pad", [P, 2, SEQ + CONV_K - 1])
        acc = st.sb("conv_acc", [P, 2, SEQ])
        with nc.Block() as block:
            @block.sync
            def _(sp):
                def load_tok(n, b):
                    sp.dma_start(wt[:, b].rearrange("p k n -> p (k n)"), dram(w_tok, L, n)).then_inc(tok_loaded[b], 16)

                def load_ch(n, b):
                    sp.dma_start(wc[:, b].rearrange("p k n -> p (k n)"), dram(w_conv, L, n)).then_inc(ch_loaded[b], 16)

                for b in range(2):
                    load_tok(b, b)
                sp.dma_start(taps[:].rearrange("p n k -> p (n k)"), dram(conv_w, L)).then_inc(small, 16)
                for b in range(2):
                    load_ch(b, b)
                with sp.Fori(1, N_PG // 2) as i:
                    for b in range(2):
                        sp.wait_ge(tok_ready, (i * 2 + b - 1) * TT)
                        load_tok(i * 2 + b, b)
                with sp.Fori(1, N_CONV // 2) as i:
                    for b in range(2):
                        sp.wait_ge(ch_ready, i * 2 + b - 1)
                        load_ch(i * 2 + b, b)

            @block.tensor
            def _(pe):
                norm.tensor(pe)
                pe.wait_ge(norm.ready, KT)
                with pe.Fori(0, N_PG // 2) as i:
                    for b in range(2):
                        pe.wait_ge(tok_loaded[b], i * 16 + 16)
                        for t in range(TT):
                            pe.wait_ge(odd_free if t % 2 else even_free, i * 4 + b * 2 + t // 2 + 1)
                            for k in range(KT):
                                last = nc.tensor.matmul(e.bank[t][:, 0:PG], e.h[:, k, t * P:(t + 1) * P], wt[:, b, k],
                                                        start=k == 0, stop=k == KT - 1)
                            last.then_inc(tok_ready, 1)
                with pe.Fori(0, N_CONV // 2) as i:
                    for b in range(2):
                        pe.wait_ge(ch_loaded[b], i * 16 + 16)
                        pe.wait_ge(padded, i * 2 + b + 1)
                        for k in range(KT):
                            last = nc.tensor.matmul(e.bank[4 + b][:], wc[:, b, k], e.h[:, k], start=k == 0, stop=k == KT - 1)
                        last.then_inc(ch_ready, 1)

            @block.scalar
            def _(act):
                act.sem_inc(even_free, 2)
                act.sem_inc(padded, 2)
                act.sem_inc(conv_out, 2)
                norm.scalar(act)
                with act.Fori(0, N_PG // 2) as i:
                    for b in range(2):
                        for t in (0, 2):
                            act.wait_ge(tok_ready, i * 8 + b * 4 + t + 1)
                            nc.scalar.activation(e.proj[:, t, bass.ds((i * 2 + b) * PG, PG)], e.bank[t][:, 0:PG],
                                                 ACT.Copy).then_inc(even_free, 1)
                act.wait_ge(pad_zero, 1)
                with act.Fori(0, N_CONV // 2) as i:
                    for b in range(2):
                        act.wait_ge(ch_ready, i * 2 + b + 1)
                        act.wait_ge(convolved, i * 2 + b + 1)
                        nc.scalar.activation(pad[:, b, CONV_K - 1:], e.bank[4 + b][:], ACT.Copy).then_inc(padded, 1)
                        act.wait_ge(convolved, i * 2 + b + 3)
                        nc.scalar.activation(at(e.conv, i * 2 + b), acc[:, b], ACT.Silu).then_inc(conv_out, 1)

            @block.vector
            def _(dve):
                dve.sem_inc(odd_free, 2)
                dve.sem_inc(convolved, 2)
                nc.vector.memset(pad[:, :, 0:CONV_K - 1], 0.0).then_inc(pad_zero, 1)
                norm.vector(dve)
                with dve.Fori(0, N_PG // 2) as i:
                    for b in range(2):
                        for t in (1, 3):
                            dve.wait_ge(tok_ready, i * 8 + b * 4 + t + 1)
                            nc.vector.tensor_copy(e.proj[:, t, bass.ds((i * 2 + b) * PG, PG)], e.bank[t][:, 0:PG]).then_inc(odd_free, 1)
                dve.wait_ge(small, 16)
                with dve.Fori(0, N_CONV // 2) as i:
                    for b in range(2):
                        dve.wait_ge(padded, i * 2 + b + 3)
                        dve.wait_ge(conv_out, i * 2 + b + 1)
                        tap = at(taps, i * 2 + b)
                        nc.vector.tensor_scalar(acc[:, b], pad[:, b, 0:SEQ], tap[:, 0:1], None, ALU.mult)
                        for j in range(1, CONV_K):
                            dve.drain()
                            last = nc.vector.scalar_tensor_tensor(acc[:, b], pad[:, b, j:j + SEQ], tap[:, j:j + 1], acc[:, b],
                                                                  ALU.mult, ALU.add)
                        last.then_inc(convolved, 1)


def out_stage(nc, e, L, w_out):
    with Stage(nc) as st:
        w_loaded = [st.sem(f"wo_loaded{b}") for b in range(2)]
        turned, y_even, y_odd, out_ready, out_free = st.sems("turned y_even y_odd out_ready out_free")
        wo = st.sb("w_out_sb", [P, 2, KT, P])
        yt = st.sb("y_t", [P, KT, SEQ])
        with nc.Block() as block:
            @block.sync
            def _(sp):
                for b in range(2):
                    sp.dma_start(wo[:, b].rearrange("p k n -> p (k n)"), dram(w_out, L, b)).then_inc(w_loaded[b], 16)
                with sp.Fori(1, KT // 2) as i:
                    for b in range(2):
                        sp.wait_ge(out_ready, i * 2 + b - 1)
                        sp.dma_start(wo[:, b].rearrange("p k n -> p (k n)"), dram(w_out, L, i * 2 + b)).then_inc(w_loaded[b], 16)

            @block.tensor
            def _(pe):
                for k in range(KT):
                    if k >= 4:
                        pe.wait_ge(y_odd if k % 2 else y_even, (k - 4) // 2 + 1)
                    for t in range(TT):
                        last = nc.tensor.transpose(e.bank[k % 4][:, t * P:(t + 1) * P], e.y[:, t, k * P:(k + 1) * P], e.k("ident"))
                    last.then_inc(turned, 1)
                pe.wait_ge(y_even, KT // 2)
                pe.wait_ge(y_odd, KT // 2)
                with pe.Fori(0, KT // 2) as i:
                    for b in range(2):
                        pe.wait_ge(w_loaded[b], i * 16 + 16)
                        pe.wait_ge(out_free, i * 2 + b + 1)
                        for k in range(KT):
                            last = nc.tensor.matmul(e.bank[4 + b][:], wo[:, b, k], yt[:, k], start=k == 0, stop=k == KT - 1)
                        last.then_inc(out_ready, 1)

            @block.scalar
            def _(act):
                for k in range(0, KT, 2):
                    act.wait_ge(turned, k + 1)
                    nc.scalar.activation(yt[:, k], e.bank[k % 4][:], ACT.Copy).then_inc(y_even, 1)

            @block.vector
            def _(dve):
                dve.sem_inc(out_free, 2)
                for k in range(1, KT, 2):
                    dve.wait_ge(turned, k + 1)
                    nc.vector.tensor_copy(yt[:, k], e.bank[k % 4][:]).then_inc(y_odd, 1)
                with dve.Fori(0, KT // 2) as i:
                    for b in range(2):
                        dve.wait_ge(out_ready, i * 2 + b + 1)
                        xm = at(e.x, i * 2 + b)
                        nc.vector.scalar_tensor_tensor(xm, e.bank[4 + b][:], e.gate[:, 1, bass.ds(i * 2 + b, 1)], xm,
                                                       ALU.mult, ALU.add).then_inc(out_free, 1)


def bc(ap, n):
    return ap.broadcast_to(list(ap.shape[:-1]) + [n])


def mlstm_stage(nc, e, L, gate_b, head_norm_w):
    H = M_HEADS
    with Stage(nc) as st:
        (small, gates_in, absed, e_ready, ln_ready, forget_ready, cum_ready, cum_out, offsets_ready,
         qk_turned, qk_act, qk_dve, bcast_ready, head_copied, e_rows, e_out, rows_done, w_ready, score_ready, weighted,
         w_turned, w_copied_a, w_copied_v, pv_ready, head_done, exp_m, ssq_ready, root_ready, o_ready, e_free) = st.sems(
            "m_small gates_in absed e_ready ln_ready forget_ready cum_ready cum_out offsets_ready "
            "qk_turned qk_act qk_dve bcast_ready head_copied e_rows e_out rows_done w_ready score_ready weighted "
            "w_turned w_copied_a w_copied_v pv_ready head_done exp_m ssq_ready root_ready o_ready e_free")
        sb = lambda n, s: st.sb("m_" + n, s)
        gb = sb("gate_b", [P, 2 * H])
        nw = sb("norm_w", [P, 2 * HD])
        g = sb("gates", [P, TT, 2 * H])
        ga, ge = sb("gate_abs", [P, TT, H]), sb("gate_exp", [P, TT, H])
        lf = sb("log_f", [P, TT, H])
        cum, tot = sb("cum", [P, TT, H]), sb("tot", [P, TT, H])
        off = sb("off", [P, H, TT, TT])
        start = sb("start", [P, H, TT])
        qT, kT = sb("qT", [HD, H, SEQ]), sb("kT", [HD, H, SEQ])
        qs = sb("q_head", [HD, SEQ])
        lfb, lib = sb("lf_rows", [P, TT, P]), sb("li_rows", [P, TT, P])
        eo, ed = sb("e_off", [P, TT, P]), sb("e_diag", [P, TT, P])
        emax, dmax, cand = sb("emax", [P, TT]), sb("dmax", [P, TT]), sb("cand", [P, TT, TT])
        m1, rows = sb("m1", [P, TT]), sb("rows", [P, TT])
        nb, nd = sb("neg_b", [P, TT, TT]), sb("neg_d", [P, TT])
        w = sb("w", [P, TT, SEQ])
        sw = sb("sw", [P, TT, SEQ])
        swT = sb("swT", [P, 2, SEQ])
        num, den, mm = sb("num", [P, H, TT, HD]), sb("den", [P, H, TT]), sb("m", [P, H, TT])
        sq = sb("sq", [P, H, TT, HD])
        ss, rs = sb("ss", [P, H, TT]), sb("rs", [P, H, TT])
        og = sb("og", [P, TT, H * HD])
        causal = e.k("causal")
        tri = causal[:, SEQ - P:]
        with nc.Block() as block:
            @block.sync
            def _(sp):
                sp.dma_start(gb[:], dram(gate_b, L).broadcast_to([P, 2 * H])).then_inc(small, 16)
                sp.dma_start(nw[:], dram(head_norm_w, L).broadcast_to([P, 2 * HD])).then_inc(small, 16)

            @block.gpsimd
            def _(pool):
                nc.gpsimd.memset(off[:], 0.0)
                nc.gpsimd.memset(start[:], 0.0)
                pool.drain()
                for b in range(TT):
                    for i in range(b + 1):
                        nc.gpsimd.memset(off[:, :, i, b], NEG)
                pool.wait_ge(cum_out, 1)
                pool.drain()
                T = lambda u: tot[:, u, :]
                nc.gpsimd.tensor_copy(off[:, :, 2, 0], T(1))
                nc.gpsimd.tensor_copy(off[:, :, 3, 1], T(2))
                nc.gpsimd.tensor_tensor(off[:, :, 3, 0], T(1), T(2), ALU.add)
                nc.gpsimd.tensor_copy(start[:, :, 1], T(0))
                nc.gpsimd.tensor_tensor(start[:, :, 2], T(0), T(1), ALU.add)
                pool.drain()
                nc.gpsimd.tensor_tensor(start[:, :, 3], start[:, :, 2], T(2), ALU.add).then_inc(offsets_ready, 1)
                pool.wait_ge(qk_act, H)
                pool.wait_ge(qk_dve, H)
                with pool.Fori(0, H) as h:
                    pool.wait_ge(head_done, h)
                    nc.gpsimd.tensor_copy(lfb[:], bc(lf[:, :, bass.ds(h, 1)], P))
                    nc.gpsimd.tensor_copy(lib[:], bc(g[:, :, bass.ds(h, 1)], P)).then_inc(bcast_ready, 1)
                    nc.gpsimd.tensor_copy(qs[:], at(qT, h)).then_inc(head_copied, 1)

            @block.scalar
            def _(act):
                nc.scalar.activation(og[:], e.proj[:, :, C_MO:C_MO + H * HD], ACT.Sigmoid).then_inc(o_ready, 1)
                act.wait_ge(absed, 1)
                nc.scalar.activation(ge[:], ga[:], ACT.Exp, scale=-1.0).then_inc(e_ready, 1)
                act.wait_ge(e_ready, 1)
                nc.scalar.activation(ga[:], ge[:], ACT.Ln, bias=1.0).then_inc(ln_ready, 1)
                for h in range(H):
                    act.wait_ge(qk_turned, 2 * h + 1)
                    nc.scalar.activation(qT[:, h], e.bank[(2 * h) % 8][0:HD], ACT.Copy).then_inc(qk_act, 1)
                with act.Fori(0, H) as h:
                    act.wait_ge(rows_done, h + 1)
                    act.wait_ge(head_done, h)
                    for i in range(TT):
                        for b in range(i):
                            nc.scalar.activation(w[:, i, b * P:(b + 1) * P], eo[:, b], ACT.Exp, bias=nb[:, i, b:b + 1])
                        nc.scalar.activation(w[:, i, i * P:(i + 1) * P], ed[:, i], ACT.Exp, bias=nd[:, i:i + 1]).then_inc(w_ready, 1)
                    for i in (1, 3):
                        act.wait_ge(w_turned, h * TT + i + 1)
                        if i == 3:
                            act.wait_ge(pv_ready, h * TT + 2)
                        nc.scalar.activation(swT[:, 1, 0:(i + 1) * P], e.bank[5][:, 0:(i + 1) * P], ACT.Copy).then_inc(w_copied_a, 1)
                act.wait_ge(absed, 2)
                nc.scalar.activation(ss[:], mm[:], ACT.Exp, scale=-1.0).then_inc(exp_m, 1)
                act.wait_ge(ssq_ready, 1)
                nc.scalar.activation(rs[:], ss[:], ACT.Sqrt, bias=e.eps[:, 0:1], scale=1.0 / HD).then_inc(root_ready, 1)

            @block.tensor
            def _(pe):
                for h in range(H):
                    for n, c0 in ((0, C_MQ), (1, C_MK)):
                        for t in range(TT):
                            last = nc.tensor.transpose(e.bank[2 * h + n][0:HD, t * P:(t + 1) * P],
                                                       e.proj[:, t, c0 + h * HD:c0 + (h + 1) * HD], e.k("ident"))
                        last.then_inc(qk_turned, 1)
                pe.wait_ge(qk_act, 1)
                pe.wait_ge(forget_ready, 1)
                nc.tensor.matmul(e.bank[0][:, 0:TT * H], e.k("upper"), lf[:], start=True, stop=True)
                nc.tensor.matmul(e.bank[0][:, TT * H:2 * TT * H], e.k("ones"), lf[:], start=True, stop=True).then_inc(cum_ready, 1)
                pe.wait_ge(cum_out, 1)
                with pe.Fori(0, H) as h:
                    pe.wait_ge(bcast_ready, h + 1)
                    for b in range(TT):
                        r = e.bank[6 + b // 2][:, (b % 2) * 2 * P:(b % 2 + 1) * 2 * P]
                        nc.tensor.matmul(r, lfb[:, b], e.k("decay_sel"), start=True, stop=False)
                        last = nc.tensor.matmul(r, lib[:, b], e.k("ident2"), start=False, stop=True)
                    last.then_inc(e_rows, 1)
                    pe.wait_ge(head_copied, h + 1)
                    for i in range(TT):
                        n = (i + 1) * P
                        nc.tensor.matmul(e.bank[i][:, 0:n], qs[:, i * P:n], kT[:, bass.ds(h, 1), 0:n].rearrange("p a n -> p (a n)"),
                                         start=True, stop=True).then_inc(score_ready, 1)

                    def turn(i):
                        pe.wait_ge(weighted, h * TT + i + 1)
                        if i >= 2:
                            pe.wait_ge(w_copied_a if i % 2 else w_copied_v, h * 2 + 1)
                        for b in range(i + 1):
                            last = nc.tensor.transpose(e.bank[4 + i % 2][:, b * P:(b + 1) * P], sw[:, i, b * P:(b + 1) * P], e.k("ident"))
                        last.then_inc(w_turned, 1)

                    def values(i):
                        pe.wait_ge(w_copied_a if i % 2 else w_copied_v, h * 2 + i // 2 + 1)
                        if i == 0:
                            pe.wait_ge(e_out, h + 1)
                        for b in range(i + 1):
                            last = nc.tensor.matmul(e.bank[6][:, i * HD:(i + 1) * HD], swT[:, i % 2, b * P:(b + 1) * P],
                                                    e.proj[:, b, bass.ds(h * HD + C_MV, HD)], start=b == 0, stop=b == i)
                        last.then_inc(pv_ready, 1)

                    turn(0)
                    turn(1)
                    values(0)
                    turn(2)
                    values(1)
                    turn(3)
                    values(2)
                    values(3)
                    pe.wait_ge(head_done, h + 1)

            @block.vector
            def _(dve):
                v = nc.vector
                dve.wait_ge(small, 32)
                v.tensor_tensor(g[:], e.proj[:, :, C_MG:C_MG + 2 * H], gb[:].unsqueeze(1).broadcast_to([P, TT, 2 * H]), ALU.add)
                dve.drain()
                v.tensor_scalar(lf[:], g[:, :, H:], 0.0, None, ALU.min)
                v.scalar_tensor_tensor(ga[:], g[:, :, H:], -1.0, g[:, :, H:], ALU.mult, ALU.max).then_inc(absed, 1)
                for h in range(H):
                    dve.wait_ge(qk_turned, 2 * h + 2)
                    v.tensor_copy(kT[:, h], e.bank[2 * h + 1][0:HD]).then_inc(qk_dve, 1)
                dve.wait_ge(ln_ready, 1)
                v.tensor_tensor(lf[:], lf[:], ga[:], ALU.subtract).then_inc(forget_ready, 1)
                dve.wait_ge(cum_ready, 1)
                v.tensor_copy(cum[:].rearrange("p t h -> p (t h)"), e.bank[0][:, 0:TT * H])
                v.tensor_copy(tot[:].rearrange("p t h -> p (t h)"), e.bank[0][:, TT * H:2 * TT * H]).then_inc(cum_out, 1)
                dve.wait_ge(offsets_ready, 1)
                with dve.Fori(0, H) as h:
                    dve.wait_ge(e_rows, h + 1)
                    for b in range(TT):
                        v.tensor_tensor(ed[:, b], e.bank[6 + b // 2][:, (b % 2) * 256 + P:(b % 2) * 256 + 2 * P], tri, ALU.add)
                        last = v.tensor_copy(eo[:, b], e.bank[6 + b // 2][:, (b % 2) * 256:(b % 2) * 256 + P])
                    last.then_inc(e_out, 1)
                    dve.drain()
                    v.tensor_reduce(emax[:], eo[:], AX.X, ALU.max)
                    v.tensor_reduce(dmax[:], ed[:], AX.X, ALU.max)
                    dve.drain()
                    oh = at(off, h)
                    v.tensor_tensor(cand[:], oh, emax[:].unsqueeze(1).broadcast_to([P, TT, TT]), ALU.add)
                    v.tensor_tensor(dmax[:], dmax[:], start[:, bass.ds(h, 1), :].rearrange("p a t -> p (a t)"), ALU.max)
                    dve.drain()
                    v.tensor_reduce(m1[:], cand[:], AX.X, ALU.max)
                    dve.drain()
                    v.tensor_tensor(m1[:], m1[:], dmax[:], ALU.max)
                    dve.drain()
                    v.tensor_tensor(nb[:], oh, bc(m1[:].unsqueeze(2), TT), ALU.subtract)
                    v.tensor_tensor(mm[:, bass.ds(h, 1), :].rearrange("p a t -> p (a t)"), m1[:],
                                    cum[:, :, bass.ds(h, 1)].rearrange("p t a -> p (t a)"), ALU.add)
                    v.tensor_scalar(nd[:], m1[:], -1.0, None, ALU.mult).then_inc(rows_done, 1)
                    for i in range(TT):
                        n = (i + 1) * P
                        dve.wait_ge(score_ready, h * TT + i + 1)
                        dve.wait_ge(w_ready, h * TT + i + 1)
                        v.tensor_tensor_reduce(sw[:, i, 0:n], e.bank[i][:, 0:n], w[:, i, 0:n], SCALE, 0.0, ALU.mult, ALU.add,
                                               rows[:, i:i + 1]).then_inc(weighted, 1)
                    dve.drain()
                    v.tensor_copy(den[:, bass.ds(h, 1), :].rearrange("p a t -> p (a t)"), rows[:])
                    for i in (0, 2):
                        dve.wait_ge(w_turned, h * TT + i + 1)
                        if i == 2:
                            dve.wait_ge(pv_ready, h * TT + 1)
                        v.tensor_copy(swT[:, 0, 0:(i + 1) * P], e.bank[4][:, 0:(i + 1) * P]).then_inc(w_copied_v, 1)
                    dve.wait_ge(pv_ready, h * TT + TT)
                    v.tensor_copy(at(num, h), e.bank[6][:, 0:TT * HD].rearrange("p (t d) -> p t d", t=TT)).then_inc(head_done, 1)
                dve.drain()
                v.scalar_tensor_tensor(den[:], den[:], -1.0, den[:], ALU.mult, ALU.max).then_inc(absed, 1)
                dve.wait_ge(exp_m, 1)
                dve.drain()
                v.tensor_tensor(den[:], den[:], ss[:], ALU.max)
                dve.drain()
                v.reciprocal(den[:], den[:])
                dve.drain()
                v.tensor_tensor(num[:], num[:], bc(den[:].unsqueeze(3), HD), ALU.mult)
                dve.drain()
                v.tensor_tensor(sq[:], num[:], num[:], ALU.mult)
                dve.drain()
                v.tensor_reduce(ss[:], sq[:], AX.X, ALU.add).then_inc(ssq_ready, 1)
                dve.wait_ge(root_ready, 1)
                v.reciprocal(rs[:], rs[:])
                dve.drain()
                v.tensor_tensor(num[:], num[:], bc(rs[:].unsqueeze(3), HD), ALU.mult)
                dve.drain()
                v.tensor_tensor(sq[:].rearrange("p h t d -> p (h t) d"), num[:].rearrange("p h t d -> p (h t) d"),
                                nw[:, 0:HD].unsqueeze(1).broadcast_to([P, H * TT, HD]), ALU.mult)
                dve.wait_ge(o_ready, 1)
                dve.drain()
                for h in range(H):
                    v.tensor_tensor(e.y[:, :, h * HD:(h + 1) * HD], sq[:, h], og[:, :, h * HD:(h + 1) * HD], ALU.mult)


def delta_stage(nc, e, L, g_decay, head_norm_w):
    H = G_HEADS
    W = H * P
    with Stage(nc) as st:
        (small, decay_ready, beta_ready, a_exp, a_ln, alpha_ready, staged, raw_turned, raw_out, ssq_ready, root_ready, gam_ready, gam_out,
         gam_exp, normed, kq_turned, kq_out_v, kq_out_a, grams_ready, dec_arg, dec_ready, gram_out, x0_turned, prepared,
         masked, t1_ready, t1_out, dx_ready, inverted, w_ready, w_out, u_ready, u_out, o_ready, o_out, s_ready, z_ready,
         ssq2_ready, root2_ready, rows_ready, sq_done, s_out) = st.sems(
            "g_small decay_ready beta_ready a_exp a_ln alpha_ready staged raw_turned raw_out g_ssq_ready g_root_ready gam_ready gam_out "
            "gam_exp normed kq_turned kq_out_v kq_out_a grams_ready dec_arg dec_ready gram_out x0_turned prepared "
            "masked t1_ready t1_out dx_ready inverted wt_ready wt_out u_ready u_out g_o_ready g_o_out s_ready z_ready "
            "ssq2_ready root2_ready gam_rows_ready sq_done s_out")
        sb = lambda n, s: st.sb("g_" + n, s)
        gd = sb("decay", [P, 2 * H])
        nw = sb("norm_w", [P, 2 * HD])
        beta = sb("beta", [P, TT, H])
        la = sb("log_alpha", [P, TT, H])
        t1a, t1b = sb("t1a", [P, TT, H]), sb("t1b", [P, TT, H])
        stage = sb("stage", [P, N_CONV, P])
        raw = sb("raw", [P, 3 * H, HD])
        sq = sb("sq", [P, 2 * H, HD])
        ss, rt = sb("ss", [P, 2 * H]), sb("rt", [P, 2 * H])
        lac = sb("la_c", [P, H])
        lar = sb("la_rows", [P, H, P])
        gam, eg, egl = sb("gam", [P, H]), sb("eg", [P, H]), sb("egl", [P, H])
        qk = sb("qk", [P, 4, H, HD])
        qkT = sb("qkT", [HD, 3, H, P])
        dec = sb("dec", [P, H, P])
        at0 = sb("at0", [P, H, P])
        qgT = sb("qgT", [HD, TT, H, P])
        vb, kbg, kd = sb("vb", [P, TT, H, HD]), sb("kbg", [P, TT, H, HD]), sb("kd", [P, TT, H, HD])
        gl = sb("gl", [HD, TT, H])
        aT, pT = sb("aT", [P, TT, W]), sb("pT", [P, TT, W])
        xT, xn = sb("xT", [P, TT, W]), sb("xn", [P, TT, W])
        am, t1 = sb("am", [P, TT, W]), sb("t1", [P, TT, W])
        nwT = sb("nwT", [HD, TT, H, P])
        u = sb("u", [P, 2, H, HD])
        s = sb("s", [HD, H, HD])
        o = sb("o", [P, TT, H, HD])
        osq = am[:].rearrange("p t n -> p (t n)")[:, 0:TT * H * HD].rearrange("p (t h d) -> p t h d", t=TT, h=H)
        so, ro = sb("so", [P, TT, H]), sb("ro", [P, TT, H])
        zs = e.proj[:, :, C_Z:C_Z + H * HD]
        h4 = lambda b: b.rearrange("p (h n) -> p h n", h=H)
        odd_even = lambda t, half: t.rearrange("p (g b) n -> p g b n", b=2)[:, :, half]
        ident = e.k("ident")
        with nc.Block() as block:
            @block.sync
            def _(sp):
                sp.dma_start(gd[:], dram(g_decay, L).broadcast_to([P, 2 * H])).then_inc(small, 16)
                sp.dma_start(nw[:], dram(head_norm_w, L).broadcast_to([P, 2 * HD])).then_inc(small, 16)

            @block.gpsimd
            def _(pool):
                pool.wait_ge(prepared, TT)
                for n in range(LEVELS):
                    for c in range(TT):
                        pool.wait_ge(t1_ready, n * TT + c)
                        m = e.k("levels")[:, n * P:(n + 1) * P].unsqueeze(1)
                        nc.gpsimd.tensor_tensor(h4(am[:, c]), h4(aT[:, c]), m.broadcast_to([P, H, P]), ALU.mult).then_inc(masked, 1)

            @block.scalar
            def _(act):
                a = nc.scalar.activation
                a(zs, zs, ACT.Silu).then_inc(z_ready, 1)
                a(beta[:], e.proj[:, :, C_GB:C_GB + H], ACT.Sigmoid).then_inc(beta_ready, 1)
                act.wait_ge(small, 32)
                a(gd[:, 0:H], gd[:, 0:H], ACT.Exp).then_inc(decay_ready, 1)
                act.wait_ge(a_exp, 1)
                a(t1b[:], t1b[:], ACT.Exp, scale=-1.0).then_inc(a_ln, 1)
                act.wait_ge(a_ln, 1)
                a(t1b[:], t1b[:], ACT.Ln, bias=1.0).then_inc(a_ln, 1)
                with act.Fori(0, TT) as c:
                    act.wait_ge(raw_turned, c)
                    a(stage[:], e.conv[:, :, bass.ds(c * P, P)], ACT.Copy).then_inc(staged, 1)
                    act.wait_ge(ssq_ready, c + 1)
                    a(rt[:], ss[:], ACT.Sqrt, bias=e.eps[:, 0:1]).then_inc(root_ready, 1)
                    act.wait_ge(gam_out, c + 1)
                    a(eg[:], gam[:], ACT.Exp)
                    a(egl[:], egl[:], ACT.Exp)
                    act.wait_ge(rows_ready, c + 1)
                    a(gl[:, bass.ds(c, 1), :].rearrange("p a h -> p (a h)"), h4(e.bank[2][0:HD])[:, :, P - 1], ACT.Exp).then_inc(gam_exp, 1)
                    for n in (1, 3):
                        act.wait_ge(kq_turned, c * 4 + n + 1)
                        dst = qkT[:, 1] if n == 1 else qgT[:, bass.ds(c, 1)].rearrange("p a h n -> p (a h) n")
                        for half in range(2):
                            last = a(odd_even(dst, half), e.bank[4 + n][half * HD:(half + 1) * HD, 0:2 * P].rearrange("p (g n) -> p g n", g=2), ACT.Copy)
                        last.then_inc(kq_out_a, 1)
                    act.wait_ge(dec_arg, c + 1)
                    a(dec[:], dec[:], ACT.Exp).then_inc(dec_ready, 1)
                with act.Fori(0, LEVELS) as n:
                    for c in range(TT):
                        act.wait_ge(t1_ready, n * TT + c + 1)
                        a(t1[:, c], e.bank[c % 2][:], ACT.Copy).then_inc(t1_out, 1)
                for c in range(TT):
                    act.wait_ge(w_ready, c + 1)
                    a(nwT[:, c].rearrange("p h n -> p (h n)"), e.bank[c % 2][0:HD], ACT.Copy, scale=-1.0).then_inc(w_out, 1)
                for c in range(TT):
                    act.wait_ge(o_ready, c + 1)
                    a(o[:, c].rearrange("p h d -> p (h d)"), e.bank[4][:, 0:H * HD], ACT.Copy).then_inc(o_out, 1)
                act.wait_ge(ssq2_ready, 1)
                a(ro[:], so[:], ACT.Sqrt, bias=e.eps[:, 0:1], scale=1.0 / HD).then_inc(root2_ready, 1)

            @block.tensor
            def _(pe):
                mm = nc.tensor.matmul
                pe.wait_ge(alpha_ready, 1)
                with pe.Fori(0, TT) as c:
                    pe.wait_ge(staged, c + 1)
                    pe.wait_ge(prepared, c)
                    for n in range(N_CONV):
                        last = nc.tensor.transpose(e.bank[n // 4][:, (n % 4) * P:(n % 4 + 1) * P], stage[:, n], ident)
                    last.then_inc(raw_turned, 1)
                    pe.wait_ge(normed, c * 3 + 1)
                    mm(e.bank[3][:, 0:H], e.k("upper"), lac[:], start=True, stop=True).then_inc(gam_ready, 1)
                    for h in range(H):
                        last = mm(h4(e.bank[2][:])[:, h], lar[:, h], e.k("upper"), start=True, stop=True)
                    last.then_inc(rows_ready, 1)
                    pe.wait_ge(normed, c * 3 + 2)
                    for n in range(3):
                        for h in range(0, H, 2):
                            last = nc.tensor.transpose(e.bank[4 + n][:, h * HD:(h + 2) * HD], qk[:, n, h:h + 2].rearrange("p h d -> p (h d)"), ident)
                        last.then_inc(kq_turned, 1)
                    pe.wait_ge(normed, c * 3 + 3)
                    for h in range(0, H, 2):
                        last = nc.tensor.transpose(e.bank[7][:, h * HD:(h + 2) * HD], qk[:, 3, h:h + 2].rearrange("p h d -> p (h d)"), ident)
                    last.then_inc(kq_turned, 1)
                    pe.wait_ge(kq_out_v, c * 2 + 2)
                    pe.wait_ge(kq_out_a, c * 2 + 2)
                    for n, b in ((1, 0), (2, 1)):
                        for h in range(H):
                            last = mm(h4(e.bank[b][:])[:, h], qkT[:, 0, h], qkT[:, n, h], start=True, stop=True)
                    last.then_inc(grams_ready, 1)
                    pe.wait_ge(gram_out, c + 1)
                    for h in range(H):
                        last = nc.tensor.transpose(e.bank[5][:, h * P:(h + 1) * P], at0[:, h], ident)
                    last.then_inc(x0_turned, 1)
                pe.wait_ge(prepared, TT)
                with pe.Fori(0, LEVELS) as n:
                    def below(c):
                        pe.wait_ge(masked, n * TT + c + 1)
                        if c >= 2:
                            pe.wait_ge(t1_out, n * TT + c - 1)
                        for h in range(H):
                            last = mm(h4(e.bank[c % 2][:])[:, h], am[:, c, h * P:(h + 1) * P], xn[:, c, h * P:(h + 1) * P], start=True, stop=True)
                        last.then_inc(t1_ready, 1)

                    def join(c):
                        pe.wait_ge(t1_out, n * TT + c + 1)
                        if c >= 2:
                            pe.wait_ge(inverted, n * TT + c - 1)
                        for h in range(H):
                            hs = slice(h * P, (h + 1) * P)
                            mm(h4(e.bank[2 + 2 * (c % 2)][:])[:, h], t1[:, c, hs], xT[:, c, hs], start=True, stop=True)
                            last = mm(h4(e.bank[3 + 2 * (c % 2)][:])[:, h], xT[:, c, hs], t1[:, c, hs], start=True, stop=True)
                        last.then_inc(dx_ready, 1)

                    pe.wait_ge(inverted, n * TT)
                    below(0)
                    below(1)
                    join(0)
                    below(2)
                    join(1)
                    below(3)
                    join(2)
                    join(3)
                pe.wait_ge(inverted, LEVELS * TT)
                for c in range(TT):
                    if c >= 2:
                        pe.wait_ge(w_out, c - 1)
                    for h in range(H):
                        last = mm(e.bank[c % 2][0:HD, h * P:(h + 1) * P], kbg[:, c, h], xT[:, c, h * P:(h + 1) * P], start=True, stop=True)
                    last.then_inc(w_ready, 1)
                for c in range(TT):
                    pe.wait_ge(w_out, c + 1)
                    pe.wait_ge(s_out, c + 1)
                    for h in range(H):
                        b = e.bank[3][:, h * HD:(h + 1) * HD]
                        mm(b, xT[:, c, h * P:(h + 1) * P], vb[:, c, h], start=True, stop=False)
                        last = mm(b, nwT[:, c, h], s[:, h], start=False, stop=True)
                    last.then_inc(u_ready, 1)
                    pe.wait_ge(u_out, c + 1)
                    if c:
                        pe.wait_ge(o_out, c)
                    for h in range(H):
                        b = e.bank[4][:, h * HD:(h + 1) * HD]
                        mm(b, qgT[:, c, h], s[:, h], start=True, stop=False)
                        last = mm(b, pT[:, c, h * P:(h + 1) * P], u[:, c % 2, h], start=False, stop=True)
                    last.then_inc(o_ready, 1)
                    for h in range(H):
                        last = mm(e.bank[5][0:HD, h * HD:(h + 1) * HD], kd[:, c, h], u[:, c % 2, h], start=True, stop=True)
                    last.then_inc(s_ready, 1)

            @block.vector
            def _(dve):
                v = nc.vector
                bh = lambda x, n=HD: bc(x.unsqueeze(2), n)
                v.memset(s[:], 0.0)
                dve.wait_ge(small, 32)
                v.tensor_tensor(t1a[:], e.proj[:, :, C_GA:C_GA + H], gd[:, H:].unsqueeze(1).broadcast_to([P, TT, H]), ALU.add)
                dve.drain()
                v.scalar_tensor_tensor(t1b[:], t1a[:], -1.0, t1a[:], ALU.mult, ALU.max).then_inc(a_exp, 1)
                v.tensor_scalar(t1a[:], t1a[:], 0.0, None, ALU.max)
                dve.drain()
                dve.wait_ge(a_ln, 2)
                v.tensor_tensor(t1a[:], t1a[:], t1b[:], ALU.add)
                dve.drain()
                dve.wait_ge(decay_ready, 1)
                v.scalar_tensor_tensor(la[:], t1a[:], -1.0, gd[:, 0:H].unsqueeze(1).broadcast_to([P, TT, H]), ALU.mult, ALU.mult).then_inc(alpha_ready, 1)
                dve.wait_ge(beta_ready, 1)
                with dve.Fori(0, TT) as c:
                    dve.drain()
                    v.tensor_copy(lac[:], la[:, bass.ds(c, 1), :].rearrange("p a h -> p (a h)"))
                    v.tensor_copy(lar[:], bc(la[:, bass.ds(c, 1), :].rearrange("p a h -> p (a h)").unsqueeze(2), P)).then_inc(normed, 1)
                    dve.wait_ge(raw_turned, c + 1)
                    v.tensor_copy(raw[:, 0:8].rearrange("p h d -> p (h d)"), e.bank[0][:])
                    v.tensor_copy(raw[:, 8:12].rearrange("p h d -> p (h d)"), e.bank[1][:, 0:H * HD])
                    dve.drain()
                    v.tensor_tensor(sq[:], raw[:, 0:8], raw[:, 0:8], ALU.mult)
                    dve.drain()
                    v.tensor_reduce(ss[:], sq[:], AX.X, ALU.add).then_inc(ssq_ready, 1)
                    dve.wait_ge(gam_ready, c + 1)
                    dve.wait_ge(rows_ready, c + 1)
                    v.tensor_copy(gam[:], e.bank[3][:, 0:H])
                    dve.drain()
                    v.tensor_tensor(egl[:], h4(e.bank[2][:])[:, :, P - 1], gam[:], ALU.subtract).then_inc(gam_out, 1)
                    dve.wait_ge(root_ready, c + 1)
                    v.reciprocal(ss[:], rt[:])
                    dve.drain()
                    k_, kb_, q_, qg_ = (qk[:, n] for n in range(4))
                    bt = beta[:, bass.ds(c, 1), :].rearrange("p a h -> p (a h)")
                    v.tensor_tensor(k_, raw[:, 4:8], bh(ss[:, 4:8]), ALU.mult)
                    v.tensor_tensor(q_, raw[:, 0:4], bh(ss[:, 0:4]), ALU.mult)
                    dve.drain()
                    v.tensor_tensor(kb_, k_, bh(bt), ALU.mult)
                    v.tensor_scalar(q_, q_, SCALE, None, ALU.mult).then_inc(normed, 1)
                    dve.drain()
                    dve.wait_ge(gam_exp, c + 1)
                    col = lambda t: t[:, bass.ds(c, 1)].rearrange("p a h n -> p (a h) n")
                    v.tensor_tensor(qg_, q_, bh(eg[:]), ALU.mult).then_inc(normed, 1)
                    v.tensor_tensor(col(kbg), kb_, bh(eg[:]), ALU.mult)
                    v.tensor_tensor(col(kd), k_, bh(egl[:]), ALU.mult)
                    v.tensor_tensor(col(vb), raw[:, 8:12], bh(bt), ALU.mult)
                    v.tensor_tensor(dec[:], h4(e.bank[2][:]), bh(gam[:], P), ALU.subtract)
                    dve.drain()
                    v.tensor_tensor(dec[:], dec[:], e.k("causal_t").unsqueeze(1).broadcast_to([P, H, P]), ALU.add).then_inc(dec_arg, 1)
                    for n in (0, 2):
                        dve.wait_ge(kq_turned, c * 4 + n + 1)
                        for half in range(2):
                            last = v.tensor_copy(odd_even(qkT[:, n], half), e.bank[4 + n][half * HD:(half + 1) * HD, 0:2 * P].rearrange("p (g n) -> p g n", g=2))
                        last.then_inc(kq_out_v, 1)
                    dve.wait_ge(dec_ready, c + 1)
                    dve.wait_ge(grams_ready, c + 1)
                    row = lambda t: h4(t[:, bass.ds(c, 1)].rearrange("p a n -> p (a n)"))
                    v.tensor_tensor(at0[:], h4(e.bank[0][:]), dec[:], ALU.mult)
                    v.tensor_tensor(row(pT), h4(e.bank[1][:]), dec[:], ALU.mult)
                    dve.drain()
                    v.tensor_copy(row(aT), at0[:])
                    dve.drain()
                    v.tensor_tensor(at0[:], at0[:], e.k("level0").unsqueeze(1).broadcast_to([P, H, P]), ALU.mult)
                    dve.drain()
                    v.tensor_tensor(at0[:], ident.unsqueeze(1).broadcast_to([P, H, P]), at0[:], ALU.subtract).then_inc(gram_out, 1)
                    dve.drain()
                    v.tensor_copy(row(xT), at0[:])
                    dve.wait_ge(x0_turned, c + 1)
                    v.tensor_copy(row(xn), h4(e.bank[5][:])).then_inc(prepared, 1)
                with dve.Fori(0, LEVELS) as n:
                    for c in range(TT):
                        dve.wait_ge(dx_ready, n * TT + c + 1)
                        v.tensor_tensor(xT[:, c], xT[:, c], e.bank[2 + 2 * (c % 2)][:], ALU.subtract)
                        v.tensor_tensor(xn[:, c], xn[:, c], e.bank[3 + 2 * (c % 2)][:], ALU.subtract).then_inc(inverted, 1)
                v.memset(so[:], 0.0).then_inc(s_out, 1)
                for c in range(TT):
                    dve.wait_ge(u_ready, c + 1)
                    v.tensor_copy(u[:, c % 2].rearrange("p h d -> p (h d)"), e.bank[3][:, 0:H * HD]).then_inc(u_out, 1)
                    dve.wait_ge(o_ready, c + 1)
                    v.tensor_tensor(s[:], s[:], bh(gl[:, c]), ALU.mult)
                    dve.drain()
                    dve.wait_ge(s_ready, c + 1)
                    v.tensor_tensor(s[:], s[:], e.bank[5][0:HD, 0:H * HD].rearrange("p (h d) -> p h d", h=H), ALU.add).then_inc(s_out, 1)
                dve.wait_ge(o_out, TT)
                v.tensor_tensor(osq, o[:], o[:], ALU.mult)
                dve.drain()
                v.tensor_reduce(so[:], osq, AX.X, ALU.add).then_inc(ssq2_ready, 1)
                dve.wait_ge(root2_ready, 1)
                v.reciprocal(ro[:], ro[:])
                dve.drain()
                v.tensor_tensor(o[:], o[:], bc(ro[:].unsqueeze(3), HD), ALU.mult)
                dve.drain()
                th = lambda x: x.rearrange("p t h d -> p (t h) d")
                v.tensor_tensor(th(osq), th(o[:]), nw[:, HD:].unsqueeze(1).broadcast_to([P, TT * H, HD]), ALU.mult)
                dve.drain()
                dve.wait_ge(z_ready, 1)
                v.tensor_tensor(e.y[:, :, M_W:M_W + H * HD], osq.rearrange("p t h d -> p t (h d)"), zs, ALU.mult)


def nsa_stage(nc, e, L, qk_norm, cmp_pos, cmp_w1, cmp_w2):
    NQ, NK = N_HEADS, 2 * N_KV
    NH = NQ + NK
    NC = N_CMP
    PAIRS = CMP_BLOCK // 2
    HT = CMP_HIDDEN // P
    with Stage(nc) as st:
        (small, w1_loaded, w2_loaded, gates_ready, ss_ready, root_ready, roped, q_turned, qk_out_v, qk_out_a, c_turned, blocks_ready,
         hid_ready, hid_out, kc_ready, kc_ss, kc_root, kc_roped, kc_turned, kc_out, vc_ready, cs_ready, cs_masked, cp_ready, cp_scaled,
         cp_turned, cp_out, co_ready, co_out, q_copied, score_ready, tile_taken, max_ready, prob_ready, turned, t_out_v, t_out_a,
         pv_ready, combined, squared, blk_zero, masked) = st.sems(
            "n_small w1_loaded w2_loaded n_gates_ready n_ss_ready n_root_ready roped q_turned qk_out_v qk_out_a c_turned blocks_ready "
            "hid_ready hid_out kc_ready kc_ss kc_root kc_roped kc_turned kc_out vc_ready cs_ready cs_masked cp_ready cp_scaled "
            "cp_turned cp_out co_ready co_out q_copied n_score_ready tile_taken max_ready prob_ready n_turned t_out_v t_out_a "
            "n_pv_ready combined n_squared blk_zero n_masked")
        sb = lambda n, s: st.sb("n_" + n, s)
        qw = sb("qk_norm", [P, 4, HD])
        wt = sb("norm_rows", [P, NH, HD])
        pos = sb("pos", [P, 2, PAIRS])
        w1 = sb("w1", [P, 2, PAIRS, CMP_HIDDEN])
        w2 = sb("w2", [P, 2, HT, HD])
        ng = sb("gates", [P, TT, 3 * NQ])
        ss, rs = sb("ss", [P, TT, NH]), sb("rs", [P, TT, NH])
        qn = e.conv[:].rearrange("p n s -> p (n s)").rearrange("p (t h d) -> p t h d", t=TT, h=NH)
        qT, kT = sb("qT", [HD, NQ, SEQ]), sb("kT", [HD, NK, SEQ])
        blk = sb("blocks", [P, 2, PAIRS, N_KV * NC])
        hidT = sb("hidT", [P, 2, HT, N_KV * NC])
        kc, kc1, kc2 = sb("kc", [NC, N_KV, HD]), sb("kc1", [NC, N_KV, HD]), sb("kc2", [NC, N_KV, HD])
        ks, kr = sb("kc_ss", [NC, N_KV]), sb("kc_rs", [NC, N_KV])
        kcT = sb("kcT", [HD, N_KV, 32])
        vcb = sb("vc_blocks", [P, N_KV, GROUP, HD])
        cp = sb("cp", [P, TT, NQ, 32])
        cm, cs = sb("cmp_max", [P, TT, NQ]), sb("cmp_sum", [P, TT, NQ])
        cpT = sb("cpT", [P, 2, P])
        qs = sb("q_head", [HD, N_KV, SEQ])
        sm = sb("masked_s", [P, 2, TT, SEQ])
        r1, r2 = (sm[:, n].rearrange("p t s -> p (t s)")[:, 0:NH * HD].rearrange("p (h d) -> p h d", h=NH) for n in range(2))
        pr = w1[:].rearrange("p a b c -> p (a b c)")[:, 0:2 * TT * SEQ].rearrange("p (a t s) -> p a t s", a=2, t=TT)
        pt = sb("probs_t", [P, 2, SEQ])
        mx, nm, rsum = sb("mx", [P, 2, TT]), sb("neg_max", [P, 2, TT]), sb("row_sum", [P, 2, TT])
        cf, om = sb("coef_o", [P, TT]), sb("o_scaled", [P, TT, HD])
        causal, ident = e.k("causal"), e.k("ident")
        Y0 = M_W + G_HEADS * HD
        prep = ((0, NQ, C_Q), (NQ, N_KV, C_KS), (NQ + N_KV, N_KV, C_KWN))
        half = HD // 2
        v_cols = (C_VS, C_VWN)

        def compressed(pe, mm, i):
            t, kv = i // N_KV, i % N_KV
            pe.wait_ge(cp_out, i + 1)
            if i >= 2:
                pe.wait_ge(co_out, i - 1)
            mm(e.bank[6 + i % 2][:, 0:GROUP * HD], cpT[:, i % 2], vcb[:, kv].rearrange("p g d -> p (g d)"), start=True, stop=True).then_inc(co_ready, 1)

        def take(dve, v, i):
            t, kv = i // N_KV, i % N_KV
            dve.wait_ge(co_ready, i + 1)
            v.tensor_copy(e.y[:, t, Y0 + kv * GROUP * HD:Y0 + (kv + 1) * GROUP * HD], e.bank[6 + i % 2][:, 0:GROUP * HD]).then_inc(co_out, 1)

        with nc.Block() as block:
            @block.sync
            def _(sp):
                sp.dma_start(qw[:].rearrange("p a d -> p (a d)"), dram(qk_norm, L).broadcast_to([P, 4 * HD])).then_inc(small, 16)
                sp.dma_start(pos[:].rearrange("p a b -> p (a b)"), dram(cmp_pos, L)).then_inc(small, 16)
                sp.dma_start(w1[:].rearrange("p a b c -> p (a b c)"), dram(cmp_w1, L)).then_inc(w1_loaded, 16)
                sp.dma_start(w2[:].rearrange("p a b c -> p (a b c)"), dram(cmp_w2, L)).then_inc(w2_loaded, 16)

            @block.gpsimd
            def _(pool):
                nc.gpsimd.memset(vcb[:], 0.0).then_inc(blk_zero, 1)
                nc.gpsimd.memset(cp[:], 0.0).then_inc(blk_zero, 1)
                pool.wait_ge(qk_out_v, NH // 2)
                pool.wait_ge(qk_out_a, NH // 2)
                with pool.Fori(0, GROUP) as g:
                    pool.wait_ge(score_ready, g * 16)
                    nc.gpsimd.tensor_copy(qs[:], qT[:].rearrange("p (k g) s -> p k g s", k=N_KV)[:, :, bass.ds(g, 1)].rearrange("p k a s -> p k (a s)")).then_inc(q_copied, 1)

            @block.scalar
            def _(act):
                a = nc.scalar.activation
                act.sem_inc(prob_ready, 8)
                a(ng[:], e.proj[:, :, C_NG:C_NG + 3 * NQ], ACT.Sigmoid).then_inc(gates_ready, 1)
                act.wait_ge(ss_ready, TT)
                a(rs[:], ss[:], ACT.Sqrt, bias=e.eps[:, 0:1], scale=1.0 / HD).then_inc(root_ready, 1)
                act.wait_ge(hid_ready, 1)
                a(hidT[:], e.bank[7][:, 0:2 * HT * 64].rearrange("p (a b n) -> p a b n", a=2, b=HT)[:, :, :, 0:N_KV * NC], ACT.Silu).then_inc(hid_out, 1)
                act.wait_ge(kc_ss, 1)
                a(kr[:], ks[:], ACT.Sqrt, bias=e.eps[0:NC, 0:1], scale=1.0 / HD).then_inc(kc_root, 1)
                for n in range(NH // 2):
                    act.wait_ge(q_turned, n + 1)
                    hh = 2 * n + 1
                    act.wait_ge(qk_out_v, n + 1)
                    a(qT[:, hh] if hh < NQ else kT[:, hh - NQ], e.bank[n % 4][HD:P], ACT.Copy).then_inc(qk_out_a, 1)
                act.wait_ge(cs_masked, 1)
                a(cp[:, :, :, 0:NC], cp[:, :, :, 0:NC], ACT.Exp, scale=SCALE).then_inc(cp_ready, 1)
                with act.Fori(0, GROUP) as g:
                    def probs(j):
                        act.wait_ge(combined, g * 4 + j + 1)
                        act.wait_ge(turned, g * 16 + j * 4 + 4)
                        act.wait_ge(max_ready, g * 4 + j + 1)
                        for t in range(TT):
                            n = (t + 1) * P
                            a(pr[:, j % 2, t, 0:n], sm[:, j % 2, t, 0:n], ACT.Exp, bias=nm[:, j % 2, t:t + 1], scale=SCALE,
                              accum_out=rsum[:, j % 2, t:t + 1]).then_inc(prob_ready, 1)

                    def last_tile(j):
                        act.wait_ge(turned, g * 16 + j * 4 + 4 + 8)
                        act.wait_ge(pv_ready, g * 16 + j * 4 + 6)
                        a(pt[:, 1], e.bank[5][:], ACT.Copy).then_inc(t_out_a, 1)

                    probs(0)
                    for j in range(1, 4):
                        probs(j)
                        last_tile(j - 1)
                    last_tile(3)

            @block.tensor
            def _(pe):
                mm, tr = nc.tensor.matmul, nc.tensor.transpose
                pe.sem_inc(turned, 8)
                pe.sem_inc(pv_ready, 4)
                for n, c0 in ((0, C_KC), (1, C_VC)):
                    for t in range(TT):
                        last = tr(e.bank[5 + n][:, t * P:(t + 1) * P], e.proj[:, t, c0:c0 + P], ident)
                    last.then_inc(c_turned, 1)
                pe.wait_ge(w1_loaded, 16)
                for n in range(2):
                    pe.wait_ge(blocks_ready, n + 1)
                    for ht in range(HT):
                        for a_ in range(PAIRS):
                            last = mm(e.bank[7][:, (n * HT + ht) * 64:(n * HT + ht) * 64 + N_KV * NC],
                                      w1[:, n, a_, ht * P:(ht + 1) * P], blk[:, n, a_], start=a_ == 0, stop=a_ == PAIRS - 1)
                last.then_inc(hid_ready, 1)
                pe.wait_ge(w2_loaded, 16)
                pe.wait_ge(hid_out, 1)
                for n in range(2):
                    for kv in range(N_KV):
                        for ht in range(HT):
                            last = mm(e.bank[4][0:NC, (n * N_KV + kv) * HD:(n * N_KV + kv + 1) * HD],
                                      hidT[:, n, ht, kv * NC:(kv + 1) * NC], w2[:, n, ht], start=ht == 0, stop=ht == HT - 1)
                last.then_inc(kc_ready, 1)
                for n in range(NH // 2):
                    pe.wait_ge(roped, TT)
                    if n >= 4:
                        pe.wait_ge(qk_out_a, n - 3)
                    for t in range(TT):
                        last = tr(e.bank[n % 4][:, t * P:(t + 1) * P], qn[:, t, 2 * n:2 * n + 2].rearrange("p h d -> p (h d)"), ident)
                    last.then_inc(q_turned, 1)
                pe.wait_ge(kc_roped, 1)
                for kv in range(N_KV):
                    last = tr(e.bank[5][0:HD, kv * 32:kv * 32 + NC], kc2[:, kv], ident[0:NC, 0:NC])
                last.then_inc(kc_turned, 1)
                pe.wait_ge(kc_out, 1)
                pe.wait_ge(qk_out_a, NH // 2)
                pe.wait_ge(qk_out_v, NH // 2)
                for t in range(TT):
                    for h in range(NQ):
                        last = mm(e.bank[t // 2][:, ((t % 2) * NQ + h) * 32:((t % 2) * NQ + h) * 32 + NC],
                                  qT[:, h, t * P:(t + 1) * P], kcT[:, h // GROUP, 0:NC], start=True, stop=True)
                last.then_inc(cs_ready, 1)
                pe.wait_ge(cp_scaled, 1)
                pe.wait_ge(vc_ready, 1)
                for i in range(TT * N_KV):
                    t, kv = i // N_KV, i % N_KV
                    if i >= 2:
                        pe.wait_ge(cp_out, i - 1)
                    tr(e.bank[2 + i % 2][:, 0:P], cp[:, t, kv * GROUP:(kv + 1) * GROUP].rearrange("p h n -> p (h n)"), ident).then_inc(cp_turned, 1)
                    if i >= 1:
                        compressed(pe, mm, i - 1)
                compressed(pe, mm, TT * N_KV - 1)
                pe.wait_ge(co_out, TT * N_KV)

                with pe.Fori(0, GROUP) as g:
                    pe.wait_ge(q_copied, g + 1)

                    def scores(j):
                        kv, br = j // 2, j % 2
                        for t in range(TT):
                            n = (t + 1) * P
                            pe.wait_ge(masked, g * 16 + j * 4 + t + 1)
                            mm(e.bank[t][:, 0:n], qs[:, kv, t * P:n], kT[:, br * N_KV + kv, 0:n], start=True, stop=True).then_inc(score_ready, 1)

                    def turn(j, t):
                        u = g * 4 + j
                        pe.wait_ge(prob_ready, g * 16 + j * 4 + t + 1 + 8)
                        if t == 1:
                            pe.wait_ge(t_out_a, u)
                        else:
                            pe.wait_ge(t_out_v, g * 12 + j * 3 + (0, 0, 1, 2)[t])
                        for b in range(t + 1):
                            last = tr(e.bank[4 + t % 2][:, b * P:(b + 1) * P], pr[:, j % 2, t, b * P:(b + 1) * P], ident)
                        last.then_inc(turned, 1)

                    def values(j, t):
                        kv, br = j // 2, j % 2
                        if t == 0:
                            pe.wait_ge(combined, g * 4 + j + 1)
                        if t == 3:
                            pe.wait_ge(t_out_a, g * 4 + j + 1)
                        else:
                            pe.wait_ge(t_out_v, g * 12 + j * 3 + t + 1)
                        for b in range(t + 1):
                            last = mm(e.bank[6 + j % 2][:, t * HD:(t + 1) * HD], pt[:, t % 2, b * P:(b + 1) * P],
                                      e.proj[:, b, v_cols[br] + kv * HD:v_cols[br] + (kv + 1) * HD], start=b == 0, stop=b == t)
                        last.then_inc(pv_ready, 1)

                    def outputs(j):
                        turn(j, 0)
                        for t in range(1, TT):
                            turn(j, t)
                            values(j, t - 1)
                        values(j, TT - 1)

                    scores(0)
                    for j in range(1, 4):
                        scores(j)
                        outputs(j - 1)
                    outputs(3)

            @block.vector
            def _(dve):
                v = nc.vector
                dve.sem_inc(masked, 4)
                dve.sem_inc(combined, 2)
                dve.wait_ge(small, 32)
                for n in range(2):
                    dve.wait_ge(c_turned, n + 1)
                    for kv in range(N_KV):
                        for par in range(2):
                            for hi in range(2):
                                rows = e.bank[5 + n][kv * HD:(kv + 1) * HD].rearrange("p (w a r) -> p r a w", r=2, a=PAIRS // 2)[:, par, :, hi:hi + NC]
                                dst = blk[par * HD:(par + 1) * HD, n, hi * 8:(hi + 1) * 8, kv * NC:(kv + 1) * NC]
                                ps_ = pos[par * HD:(par + 1) * HD, n, hi * 8:(hi + 1) * 8]
                                last = v.tensor_tensor(dst, rows, bc(ps_.unsqueeze(2), NC), ALU.add)
                    last.then_inc(blocks_ready, 1)
                for h0, nh, _c in prep:
                    row = {0: 0, NQ: 2, NQ + N_KV: 3}[h0]
                    v.tensor_copy(wt[:, h0:h0 + nh], qw[:, row].unsqueeze(1).broadcast_to([P, nh, HD]))
                with dve.Fori(0, TT) as t:
                    for h0, nh, c0 in prep:
                        x = e.proj[:, bass.ds(t, 1), c0:c0 + nh * HD].rearrange("p a n -> p (a n)").rearrange("p (h d) -> p h d", h=nh)
                        v.tensor_tensor(r1[:, h0:h0 + nh], x, x, ALU.mult)
                    dve.drain()
                    v.tensor_reduce(ss[:, bass.ds(t, 1), :].rearrange("p a h -> p (a h)"), r1, AX.X, ALU.add).then_inc(ss_ready, 1)
                    dve.drain()
                dve.wait_ge(root_ready, 1)
                v.reciprocal(rs[:], rs[:])
                with dve.Fori(0, TT) as t:
                    dve.drain()
                    for h0, nh, c0 in prep:
                        x = e.proj[:, bass.ds(t, 1), c0:c0 + nh * HD].rearrange("p a n -> p (a n)").rearrange("p (h d) -> p h d", h=nh)
                        v.tensor_tensor(r1[:, h0:h0 + nh], x, bc(rs[:, bass.ds(t, 1), h0:h0 + nh].rearrange("p a h -> p (a h)").unsqueeze(2), HD), ALU.mult)
                    dve.drain()
                    v.tensor_tensor(r1, r1, wt[:], ALU.mult)
                    dve.drain()
                    tab = lambda n: e.k(n).rearrange("p (t d) -> p t d", t=TT)[:, bass.ds(t, 1)]
                    dst = at4(qn, t)
                    v.tensor_tensor(dst, r1, tab("cos").broadcast_to([P, NH, HD]), ALU.mult)
                    v.tensor_tensor(r2[:, :, 0:half], r1[:, :, half:], tab("sin")[:, :, 0:half].broadcast_to([P, NH, half]), ALU.mult)
                    v.tensor_tensor(r2[:, :, half:], r1[:, :, 0:half], tab("sin")[:, :, half:].broadcast_to([P, NH, half]), ALU.mult)
                    dve.drain()
                    v.tensor_tensor(dst, dst, r2, ALU.add).then_inc(roped, 1)
                dve.wait_ge(kc_ready, 1)
                dve.wait_ge(blk_zero, 2)
                v.tensor_copy(kc[:].rearrange("p k d -> p (k d)"), e.bank[4][0:NC, 0:N_KV * HD])
                for kv in range(N_KV):
                    for g in range(GROUP):
                        last = v.tensor_copy(vcb[32 * g:32 * g + NC, kv, g], e.bank[4][0:NC, (N_KV + kv) * HD:(N_KV + kv + 1) * HD])
                last.then_inc(vc_ready, 1)
                dve.drain()
                v.tensor_tensor(kc1[:], kc[:], kc[:], ALU.mult)
                dve.drain()
                v.tensor_reduce(ks[:], kc1[:], AX.X, ALU.add).then_inc(kc_ss, 1)
                dve.wait_ge(kc_root, 1)
                v.reciprocal(kr[:], kr[:])
                dve.drain()
                v.tensor_tensor(kc[:], kc[:], bc(kr[:].unsqueeze(2), HD), ALU.mult)
                dve.drain()
                v.tensor_tensor(kc[:], kc[:], qw[0:NC, 1].unsqueeze(1).broadcast_to([NC, N_KV, HD]), ALU.mult)
                dve.drain()
                ctab = lambda n: e.k(n)[0:NC].unsqueeze(1)
                v.tensor_tensor(kc2[:], kc[:], ctab("cmp_cos").broadcast_to([NC, N_KV, HD]), ALU.mult)
                v.tensor_tensor(kc1[:, :, 0:half], kc[:, :, half:], ctab("cmp_sin")[:, :, 0:half].broadcast_to([NC, N_KV, half]), ALU.mult)
                v.tensor_tensor(kc1[:, :, half:], kc[:, :, 0:half], ctab("cmp_sin")[:, :, half:].broadcast_to([NC, N_KV, half]), ALU.mult)
                dve.drain()
                v.tensor_tensor(kc2[:], kc2[:], kc1[:], ALU.add).then_inc(kc_roped, 1)
                for n in range(NH // 2):
                    dve.wait_ge(q_turned, n + 1)
                    hh = 2 * n
                    v.tensor_copy(qT[:, hh] if hh < NQ else kT[:, hh - NQ], e.bank[n % 4][0:HD]).then_inc(qk_out_v, 1)
                dve.wait_ge(kc_turned, 1)
                v.tensor_copy(kcT[:, :, 0:NC], e.bank[5][0:HD, 0:64].rearrange("p (k n) -> p k n", k=N_KV)[:, :, 0:NC]).then_inc(kc_out, 1)
                dve.wait_ge(cs_ready, 1)
                for t in range(TT):
                    src = e.bank[t // 2][:].rearrange("p (u h n) -> p u h n", u=2, h=NQ)[:, t % 2, :, 0:NC]
                    v.tensor_tensor(cp[:, t, :, 0:NC], src, e.k("cmp_mask")[:, t * NC:(t + 1) * NC].unsqueeze(1).broadcast_to([P, NQ, NC]), ALU.add)
                dve.drain()
                v.tensor_reduce(cm[:], cp[:, :, :, 0:NC], AX.X, ALU.max)
                dve.drain()
                flat = cp[:].rearrange("p t h n -> p (t h) n")[:, :, 0:NC]
                v.tensor_tensor(flat, flat, bc(cm[:].rearrange("p t h -> p (t h)").unsqueeze(2), NC), ALU.subtract).then_inc(cs_masked, 1)
                dve.wait_ge(cp_ready, 1)
                v.tensor_reduce(cs[:], cp[:, :, :, 0:NC], AX.X, ALU.add)
                dve.drain()
                v.reciprocal(cs[:], cs[:])
                dve.wait_ge(gates_ready, 1)
                v.tensor_tensor(cm[:], ng[:, :, 0:NQ], bc(e.k("cmp_any").unsqueeze(2), NQ), ALU.mult)
                dve.drain()
                v.tensor_tensor(cs[:], cs[:], cm[:], ALU.mult)
                dve.drain()
                v.tensor_tensor(flat, flat, bc(cs[:].rearrange("p t h -> p (t h)").unsqueeze(2), NC), ALU.mult).then_inc(cp_scaled, 1)
                for i in range(TT * N_KV):
                    t, kv = i // N_KV, i % N_KV
                    dve.wait_ge(cp_turned, i + 1)
                    if i >= 2:
                        dve.wait_ge(co_ready, i - 1)
                    v.tensor_copy(cpT[:, i % 2], e.bank[2 + i % 2][:, 0:P]).then_inc(cp_out, 1)
                    if i >= 1:
                        take(dve, v, i - 1)
                take(dve, v, TT * N_KV - 1)

                with dve.Fori(0, GROUP) as g:
                    def mask_max(j):
                        for t in range(TT):
                            n = (t + 1) * P
                            dve.wait_ge(prob_ready, g * 16 + j * 4 + t + 1)
                            dve.wait_ge(score_ready, g * 16 + j * 4 + t + 1)
                            dve.sem_inc(tile_taken, 1)
                            v.tensor_tensor_reduce(sm[:, j % 2, t, 0:n], e.bank[t][:, 0:n], causal[:, SEQ - n:], 1.0, -3.0e38,
                                                   ALU.add, ALU.max, mx[:, j % 2, t:t + 1]).then_inc(masked, 1)
                        dve.drain()
                        v.tensor_scalar(nm[:, j % 2], mx[:, j % 2], -SCALE, None, ALU.mult).then_inc(max_ready, 1)

                    def finish(j):
                        kv, br = j // 2, j % 2
                        for t in range(3):
                            dve.wait_ge(turned, g * 16 + j * 4 + t + 1 + 8)
                            dve.wait_ge(pv_ready, g * 16 + j * 4 + 3 + t)
                            v.tensor_copy(pt[:, t % 2, 0:(t + 1) * P], e.bank[4 + t % 2][:, 0:(t + 1) * P]).then_inc(t_out_v, 1)
                        dve.wait_ge(prob_ready, g * 16 + j * 4 + 4 + 8)
                        v.reciprocal(cf[:], rsum[:, j % 2])
                        dve.drain()
                        gate = ng[:, :, bass.ds((br + 1) * NQ + kv * GROUP + g, 1)].rearrange("p t a -> p (t a)")
                        v.tensor_tensor(cf[:], cf[:], gate, ALU.mult)
                        dve.drain()
                        dve.wait_ge(pv_ready, g * 16 + j * 4 + 4 + 4)
                        v.tensor_tensor(om[:], e.bank[6 + j % 2][:, 0:TT * HD].rearrange("p (t d) -> p t d", t=TT), bc(cf[:].unsqueeze(2), HD), ALU.mult)
                        dve.drain()
                        yh = e.y[:, :, bass.ds((kv * GROUP + g) * HD + Y0, HD)]
                        v.tensor_tensor(yh, yh, om[:], ALU.add).then_inc(combined, 1)

                    mask_max(0)
                    for j in range(1, 4):
                        mask_max(j)
                        finish(j - 1)
                    finish(3)
                    dve.drain()


def at4(t, i):
    return t[:, bass.ds(i, 1)].rearrange("p a b c -> p (a b) c")


def store_stage(nc, e, out):
    with Stage(nc) as st:
        stored, = st.sems("stored")
        with nc.Block() as block:
            @block.sync
            def _(sp):
                sp.dma_start(out, e.x[:].rearrange("p k n -> p (k n)")).then_inc(stored, 16)
                sp.wait_ge(stored, 16)


def decoder_kernel(nc, x_t, c_t, const, ada_w, ada_b, norm_w, w_up, w_down, w_tok, w_conv, conv_w, w_out,
                   m_gate_b, head_norm_w, g_decay, qk_norm, cmp_pos, cmp_w1, cmp_w2, out):
    with ExitStack() as ctx:
        def sb(name, shape):
            return ctx.enter_context(nc.sbuf_tensor(name, shape, F32))

        e = Env()
        e.x = sb("x", [P, KT, SEQ])
        e.h = sb("h", [P, KT, SEQ])
        e.y = e.h[:].rearrange("p k n -> p (k n)").rearrange("p (t n) -> p t n", t=TT)
        e.const = sb("const", [P, CONST_W])
        e.k = lambda n: e.const[:, CONST_AT[n][0]:CONST_AT[n][0] + CONST_AT[n][1]]
        e.c, e.csil = sb("c", [P, KT]), sb("c_silu", [P, KT])
        e.mod, e.coef, e.gate = sb("mod", [P, 9 * KT]), sb("coef", [P, 3, KT]), sb("gate", [P, 3, KT])
        e.eps = sb("eps", [P, 1])
        e.bank = [ctx.enter_context(nc.psum_tensor(f"bank{i}", [P, 512], F32)) for i in range(8)]
        load_stage(nc, e, x_t, c_t, const)
        with nc.Fori(0, DEPTH) as L:
            ada_stage(nc, e, L, "", ada_w, ada_b, norm_w)
            ffn_stage(nc, e, L, 0, w_up, w_down)
            with ExitStack() as mix:
                e.proj = mix.enter_context(nc.sbuf_tensor("proj", [P, TT, TOK_W], F32))
                e.conv = mix.enter_context(nc.sbuf_tensor("conv", [P, N_CONV, SEQ], F32))
                proj_stage(nc, e, L, w_tok, w_conv, conv_w)
                mlstm_stage(nc, e, L, m_gate_b, head_norm_w)
                delta_stage(nc, e, L, g_decay, head_norm_w)
                nsa_stage(nc, e, L, qk_norm, cmp_pos, cmp_w1, cmp_w2)
            out_stage(nc, e, L, w_out)
            ffn_stage(nc, e, L, 1, w_up, w_down)
        store_stage(nc, e, out)


def laid_out(a):
    def kpn(w, n):
        *lead, K, N = w.shape
        v = w.reshape(*lead, K // P, P, N // n, n)
        d = len(lead)
        return v.transpose(*range(d), d + 2, d + 1, d, d + 3).reshape(*lead, N // n, P, K // P * n)

    def cols(v):
        *lead, K = v.shape
        return np.moveaxis(v.reshape(*lead, K // P, P), -1, -2)

    o = {}
    o["x_t"] = a["x"][0].T.reshape(KT, P, SEQ).transpose(1, 0, 2).reshape(P, -1)
    o["c_t"] = cols(a["c"][0])
    o["const"] = constants()
    o["ada_w"] = kpn(a["ada_w"], 512)
    o["ada_b"] = cols(a["ada_b"])
    o["norm_w"] = cols(a["norm_w"].reshape(DEPTH, 3 * D_MODEL))
    up = a["ffn_w_up"].reshape(2 * DEPTH, KT, P, 2, FT, P)
    o["w_up"] = up.transpose(0, 4, 2, 1, 3, 5).reshape(2 * DEPTH, FT, P, -1)
    o["w_down"] = kpn(a["ffn_w_down"].reshape(2 * DEPTH, D_FF, D_MODEL), P)
    w = a["w_in"]
    m_in, g_w = 4 * M_W + 2 * M_HEADS, G_HEADS * HD
    conv_cols = w[:, :, m_in:m_in + 3 * g_w]
    tok_cols = np.concatenate([w[:, :, :m_in], w[:, :, m_in + 3 * g_w:]], 2)
    o["w_tok"] = kpn(tok_cols, PG)
    o["w_conv"] = kpn(conv_cols, P)
    o["conv_w"] = a["gdn_conv_w"].transpose(0, 2, 1).reshape(DEPTH, N_CONV, P, CONV_K).transpose(0, 2, 1, 3).reshape(DEPTH, P, -1)
    o["w_out"] = kpn(a["w_out"], P)
    o["m_gate_b"] = a["mlstm_gate_b"].reshape(DEPTH, 1, -1)
    o["head_norm_w"] = np.stack([a["mlstm_norm_w"], a["gdn_norm_w"]], 1).reshape(DEPTH, 1, -1)
    o["g_decay"] = np.concatenate([a["gdn_a_log"], a["gdn_dt_bias"]], 1).reshape(DEPTH, 1, -1)
    o["qk_norm"] = a["nsa_qk_norm"].reshape(DEPTH, 1, -1)
    pos = a["nsa_cmp_pos"].reshape(DEPTH, 2, CMP_BLOCK // 2, P)
    o["cmp_pos"] = pos.transpose(0, 3, 1, 2).reshape(DEPTH, P, -1)
    w1 = a["nsa_cmp_w1"].reshape(DEPTH, 2, CMP_BLOCK // 2, P, CMP_HIDDEN)
    o["cmp_w1"] = w1.transpose(0, 3, 1, 2, 4).reshape(DEPTH, P, -1)
    o["cmp_w2"] = a["nsa_cmp_w2"].reshape(DEPTH, 2, CMP_HIDDEN // P, P, HD).transpose(0, 3, 1, 2, 4).reshape(DEPTH, P, -1)
    return {k: np.ascontiguousarray(v) for k, v in o.items()}


def kernel(**inputs):
    import concourse.bacc as bacc
    from concourse.bass_utils import run_bass_kernel_spmd

    arrays = laid_out({k: np.asarray(v) for k, v in inputs.items()})
    nc = bacc.Bacc("TRN2", target_bir_lowering=False, num_devices=1)
    args = [nc.dram_tensor(f"in_{k}", v.shape, F32, kind="ExternalInput").ap() for k, v in arrays.items()]
    out = nc.dram_tensor("out_x", (P, KT * SEQ), F32, kind="ExternalOutput").ap()
    decoder_kernel(nc, *args, out)
    got = run_bass_kernel_spmd(nc, [{f"in_{k}": v for k, v in arrays.items()}], core_ids=[0]).results[0]["out_x"]
    return np.ascontiguousarray(got.reshape(P, KT, SEQ).transpose(1, 0, 2).reshape(D_MODEL, SEQ).T)[None]
```

```python
from contextlib import ExitStack

import numpy as np

import concourse.bass as bass
import concourse.mybir as mybir
from concourse.alu_op_type import AluOpType as ALU

F32 = mybir.dt.float32
F32R = mybir.dt.float32r
ACT = mybir.ActivationFunctionType
AX = mybir.AxisListType

P = 128
D_MODEL, SEQ, DEPTH = 1024, 512, 2
D_FF = 2816
HD = 64
KT = D_MODEL // P
TT = SEQ // P
FT = D_FF // P
EPS = 1e-6
NEG = -1e30

M_HEADS, G_HEADS, N_HEADS, N_KV = 4, 4, 8, 2
GROUP = N_HEADS // N_KV
CMP_BLOCK, CMP_STRIDE, CMP_HIDDEN = 32, 16, 256
N_CMP = (SEQ - CMP_BLOCK) // CMP_STRIDE + 1
SCALE = HD ** -0.5

M_W, KV_W = M_HEADS * HD, N_KV * HD
C_MQ, C_MK, C_MV, C_MO, C_MG = 0, M_W, 2 * M_W, 3 * M_W, 4 * M_W
C_Z = C_MG + 2 * M_HEADS
C_GA = C_Z + G_HEADS * HD
C_GB = C_GA + G_HEADS
C_Q = C_GB + G_HEADS
C_KC = C_Q + N_HEADS * HD
C_VC = C_KC + KV_W
C_KS = C_VC + KV_W
C_VS = C_KS + KV_W
C_KWN = C_VS + KV_W
C_VWN = C_KWN + KV_W
C_NG = C_VWN + KV_W
TOK_W = C_NG + 3 * N_HEADS
N_PG = 8
PG = TOK_W // N_PG
N_CONV = 3 * G_HEADS * HD // P
CONV_K = 4
FIRST_SEM = 110
LEVELS = 6

ADA_SLOTS = 4
ADA_HEAD = 2 * KT
ADA_UP, ADA_DOWN = 4, 3

CONST_PARTS = [("ident", P), ("ones", P), ("upper", P), ("decay_sel", 2 * P), ("ident2", 2 * P),
               ("causal", SEQ), ("causal_t", P), ("level0", P), ("levels", LEVELS * P),
               ("cos", TT * HD), ("sin", TT * HD), ("cmp_cos", HD), ("cmp_sin", HD),
               ("cmp_mask", TT * N_CMP), ("cmp_any", TT)]
BASE_W = 2 * P
CONST_AT, CONST_W = {}, 0
for _n, _w in CONST_PARTS:
    CONST_AT[_n] = (CONST_W, _w)
    CONST_W += _w


def constants():
    p, f = np.arange(P)[:, None], np.arange(P)[None, :]
    c = {}
    c["ident"] = (p == f)
    c["ones"] = np.ones((P, P))
    c["upper"] = (p <= f)
    c["decay_sel"] = np.concatenate([(p > f), -1.0 * (p <= f)], 1)
    c["ident2"] = np.concatenate([(p == f), (p == f)], 1)
    c["causal"] = np.concatenate([np.zeros((P, SEQ - P)), np.where(f <= p, 0.0, NEG)], 1)
    c["causal_t"] = np.where(p <= f, 0.0, NEG)

    def level(s):
        return (p // (2 * s) == f // (2 * s)) & (p % (2 * s) < s) & (f % (2 * s) >= s)

    c["level0"] = level(1)
    c["levels"] = np.concatenate([level(2 << n) for n in range(LEVELS)], 1)
    half = HD // 2
    inv = np.power(10000.0, -np.arange(half) / half).astype(np.float32)

    def tables(pos):
        ang = pos.astype(np.float32)[:, None] * inv[None, :]
        cos, sin = np.cos(ang).astype(np.float32), np.sin(ang).astype(np.float32)
        return np.concatenate([cos, cos], 1), np.concatenate([-sin, sin], 1)

    cos, sin = tables(np.arange(SEQ))
    c["cos"] = cos.reshape(TT, P, HD).transpose(1, 0, 2).reshape(P, -1)
    c["sin"] = sin.reshape(TT, P, HD).transpose(1, 0, 2).reshape(P, -1)
    end = np.arange(N_CMP) * CMP_STRIDE + CMP_BLOCK - 1
    cc, cs = tables(end)
    pad = np.zeros((P - N_CMP, HD))
    c["cmp_cos"], c["cmp_sin"] = np.concatenate([cc, pad]), np.concatenate([cs, pad])
    t = (np.arange(TT)[None, :, None] * P + np.arange(P)[:, None, None])
    valid = end[None, None, :] <= t
    c["cmp_mask"] = np.where(valid, 0.0, NEG).reshape(P, -1)
    c["cmp_any"] = valid.any(-1)
    return np.ascontiguousarray(np.concatenate([np.asarray(c[n], np.float32) for n, _ in CONST_PARTS], 1))


class Env:
    pass


def at(t, i):
    dims = " ".join("xyz"[:len(t.shape) - 2])
    return t[:, bass.ds(i, 1)].rearrange(f"p a {dims} -> p (a {dims.split()[0]}) {' '.join(dims.split()[1:])}")


def dram(t, *idx):
    n = len(idx)
    v = t[tuple(bass.ds(i, 1) for i in idx)]
    lead = " ".join("abc"[:n])
    return v.rearrange(f"{lead} p n -> ({lead} p) n")


class Stage:

    def __init__(self, nc):
        self.nc, self.ctx, self.nums = nc, ExitStack(), []

    def __enter__(self):
        self.ctx.__enter__()
        return self

    def sem(self, name):
        s = self.ctx.enter_context(self.nc.semaphore(name, num=FIRST_SEM + len(self.nums)))
        self.nums.append(s.num)
        return s

    def sems(self, names):
        return [self.sem(n) for n in names.split()]

    def sb(self, name, shape, dtype=F32):
        return self.ctx.enter_context(self.nc.sbuf_tensor(name, shape, dtype))

    def __exit__(self, *a):
        if a[0] is None:
            self.nc.all_engine_barrier(sems_to_clear=range(min(self.nums), max(self.nums) + 1))
        return self.ctx.__exit__(*a)


def load_stage(nc, e, x_t, c_t, const):
    with Stage(nc) as st:
        loaded, = st.sems("loaded")
        with nc.Block() as block:
            @block.sync
            def _(sp):
                sp.dma_start(e.x[:], x_t).then_inc(loaded, 16)
                sp.dma_start(e.base[:], const[:, 0:BASE_W]).then_inc(loaded, 16)
                sp.dma_start(e.c[:], c_t).then_inc(loaded, 16)
                sp.wait_ge(loaded, 48)

            @block.vector
            def _(dve):
                nc.vector.memset(e.eps[:], EPS)


def mod_tile(nc, dve, acc, w, csil):
    nc.vector.tensor_scalar(acc, w[:, 0], csil[:, 0:1], None, ALU.mult)
    for k in range(1, KT):
        dve.drain()
        last = nc.vector.scalar_tensor_tensor(acc, w[:, k], csil[:, k:k + 1], acc, ALU.mult, ALU.add)
    return last


def ada_stage(nc, e, L, ada_w, ada_b, norm_w):
    with Stage(nc) as st:
        small, c_ready = st.sems("ada_small c_ready")
        loaded = [st.sem(f"ada_loaded{b}") for b in range(ADA_SLOTS)]
        acc_ready, acc_free = st.sems("ada_acc_ready ada_acc_free")
        w = st.sb("ada_w_sb", [P, ADA_SLOTS, 2, KT, P])
        acc = st.sb("ada_acc", [P, ADA_SLOTS, P])
        N = ADA_HEAD
        with nc.Block() as block:
            @block.sync
            def _(sp):
                sp.dma_start(e.mod_b[:], dram(ada_b, L)).then_inc(small, 16)
                sp.dma_start(e.nw[:], dram(norm_w, L)).then_inc(small, 16)
                for n in range(0, N, 2):
                    b = (n // 2) % ADA_SLOTS
                    if n // 2 >= ADA_SLOTS:
                        sp.wait_ge(acc_ready, n - 2 * ADA_SLOTS + 2)
                    sp.dma_start(w[:, b].rearrange("p t k n -> p t (k n)"),
                                 ada_w[bass.ds(L, 1), n:n + 2].rearrange("a t p n -> p (a t) n")).then_inc(loaded[b], 16)

            @block.scalar
            def _(act):
                nc.scalar.activation(e.csil[:], e.c[:], ACT.Silu).then_inc(c_ready, 1)

            @block.vector
            def _(dve):
                dve.wait_ge(c_ready, 1)
                for n in range(N):
                    b = (n // 2) % ADA_SLOTS
                    dve.wait_ge(loaded[b], (n // 2 // ADA_SLOTS) * 16 + 16)
                    if n >= ADA_SLOTS:
                        dve.wait_ge(acc_free, n - ADA_SLOTS + 1)
                    mod_tile(nc, dve, acc[:, n % ADA_SLOTS], w[:, b, n % 2], e.csil).then_inc(acc_ready, 1)
                dve.wait_ge(small, 32)
                dve.wait_ge(acc_free, N)
                nc.vector.tensor_tensor(e.mod[:, 0:N], e.bank[0][:, 0:N], e.mod_b[:, 0:N], ALU.add)
                dve.drain()
                nc.vector.scalar_tensor_tensor(e.coef[:, 0], e.mod[:, KT:2 * KT], 1.0, e.nw[:, 0:KT], ALU.add, ALU.mult)

            @block.tensor
            def _(pe):
                for n in range(N):
                    pe.wait_ge(acc_ready, n + 1)
                    nc.tensor.matmul(e.bank[0][:, n:n + 1], acc[:, n % ADA_SLOTS], e.k("ones")[:, 0:1],
                                     start=True, stop=True).then_inc(acc_free, 1)


class SplitNorm:

    def __init__(self, nc, e, st, sub, tag, scratch):
        self.nc, self.e, self.sub = nc, e, sub
        (self.squared, self.summed, self.rooted, self.scaled, self.high, self.full, self.ready) = st.sems(
            " ".join(f"{n}{tag}" for n in "squared sumsq_ready root_ready scaled h_hi_ready h_full_ready h_ready".split()))
        self.root, self.rstd = scratch
        self.hi = st.sb("h_hi" + tag, [P, KT, SEQ], F32R)
        self.lo = st.sb("h_lo" + tag, [P, KT, SEQ], F32R)

    def affine(self, k):
        return self.e.coef[:, self.sub, k:k + 1], self.e.mod[:, 3 * self.sub * KT + k:3 * self.sub * KT + k + 1]

    def scalar(self, act):
        nc, e = self.nc, self.e
        for k in range(KT):
            nc.scalar.activation(e.h[:, k], e.x[:, k], ACT.Square).then_inc(self.squared, 1)
        act.wait_ge(self.summed, 1)
        nc.scalar.activation(self.root, e.bank[7][:], ACT.Sqrt, bias=e.eps[:, 0:1], scale=1.0 / D_MODEL).then_inc(self.rooted, 1)
        for k in range(KT):
            act.wait_ge(self.scaled, k + 1)
            coef, shift = self.affine(k)
            nc.scalar.activation(self.hi[:, k], e.h[:, k], ACT.Identity, scale=coef, bias=shift).then_inc(self.high, 1)

    def gpsimd(self, pool):
        for k in range(KT):
            pool.wait_ge(self.high, k + 1)
            coef, shift = self.affine(k)
            self.nc.gpsimd.tensor_scalar(self.e.h[:, k], self.e.h[:, k], coef, shift, ALU.mult, ALU.add).then_inc(self.full, 1)

    def tensor(self, pe):
        for k in range(KT):
            pe.wait_ge(self.squared, k + 1)
            last = self.nc.tensor.matmul(self.e.bank[7][:], self.e.k("ones"), self.e.h[:, k], start=k == 0, stop=k == KT - 1)
        last.then_inc(self.summed, 1)

    def vector(self, dve):
        nc, e = self.nc, self.e
        dve.wait_ge(self.rooted, 1)
        nc.vector.reciprocal(self.rstd, self.root)
        dve.drain()
        for k in range(KT + 1):
            if k < KT:
                nc.vector.tensor_tensor(e.h[:, k], e.x[:, k], self.rstd, ALU.mult).then_inc(self.scaled, 1)
            if k:
                dve.wait_ge(self.full, k)
                nc.vector.tensor_tensor(self.lo[:, k - 1], e.h[:, k - 1], self.hi[:, k - 1].bitcast(F32), ALU.subtract).then_inc(self.ready, 1)


def product(nc, out, w_hi, w_lo, x_hi, x_lo, first, last):
    nc.tensor.matmul(out, w_hi, x_hi, start=first, stop=False)
    nc.tensor.matmul(out, w_hi, x_lo, start=False, stop=False)
    return nc.tensor.matmul(out, w_lo, x_hi, start=False, stop=last)


class Norm:

    def __init__(self, nc, e, st, sub, tag):
        self.nc, self.e, self.sub = nc, e, sub
        (self.squared, self.summed, self.rooted, self.scaled, self.ready) = st.sems(
            " ".join(f"{n}{tag}" for n in "squared sumsq_ready root_ready scaled h_ready".split()))
        self.rstd = st.sb("rstd" + tag, [P, SEQ])
        self.root = st.sb("root" + tag, [P, SEQ])

    def scalar(self, act):
        nc, e = self.nc, self.e
        for k in range(KT):
            nc.scalar.activation(e.h[:, k], e.x[:, k], ACT.Square).then_inc(self.squared, 1)
        act.wait_ge(self.summed, 1)
        nc.scalar.activation(self.root[:], e.bank[7][:], ACT.Sqrt, bias=e.eps[:, 0:1], scale=1.0 / D_MODEL).then_inc(self.rooted, 1)
        for k in range(KT):
            act.wait_ge(self.scaled, k + 1)
            nc.scalar.activation(e.h[:, k], e.h[:, k], ACT.Identity, scale=e.coef[:, self.sub, k:k + 1],
                                 bias=e.mod[:, 3 * self.sub * KT + k:3 * self.sub * KT + k + 1]).then_inc(self.ready, 1)

    def tensor(self, pe):
        for k in range(KT):
            pe.wait_ge(self.squared, k + 1)
            last = self.nc.tensor.matmul(self.e.bank[7][:], self.e.k("ones"), self.e.h[:, k], start=k == 0, stop=k == KT - 1)
        last.then_inc(self.summed, 1)

    def vector(self, dve):
        nc, e = self.nc, self.e
        dve.wait_ge(self.rooted, 1)
        nc.vector.reciprocal(self.rstd[:], self.root[:])
        dve.drain()
        for k in range(KT):
            nc.vector.tensor_tensor(e.h[:, k], e.x[:, k], self.rstd[:], ALU.mult).then_inc(self.scaled, 1)


def ffn_stage(nc, e, L, which, w_up, w_down, ada_w):
    sub, tag = 2 * which, f"_f{which}"
    names = lambda text: " ".join(n + tag for n in text.split())
    FH = FT // 2
    ada = which == 0
    UP, DOWN = FT // 2, KT // 2
    MOD_REST = 9 * KT - ADA_HEAD
    assert UP * ADA_UP + DOWN * ADA_DOWN == MOD_REST
    with Stage(nc) as st:
        raw_loaded = [st.sem(f"raw_loaded{b}{tag}") for b in range(2)]
        (high_ready, split_ready, gate_ready, up_ready, silu_ready, product_ready, hidden_high, hidden_ready,
         down_high, down_split, half_ready, down_ready) = st.sems(
            names("high_ready split_ready gate_ready up_ready silu_ready product_ready hidden_high hidden_ready "
                  "down_high down_split half_ready down_ready"))
        down_free = st.sem("down_free" + tag)
        if ada:
            mod_loaded = [st.sem(f"mod_loaded{b}") for b in range(ADA_SLOTS)]
            mod_acc, mod_sums = st.sems("mod_acc mod_sums")
            acc = st.sb("mod_acc_sb", [P, ADA_SLOTS, P])
        sg = st.sb("silu_sb" + tag, [P, 2, SEQ])
        norm = SplitNorm(nc, e, st, sub, tag, (sg[:, 0], sg[:, 1]))
        prod = st.sb("product_sb" + tag, [P, 2, SEQ])
        hid_hi = st.sb("hidden_hi" + tag, [P, FT, SEQ], F32R)
        hid_lo = st.sb("hidden_lo" + tag, [P, FT, SEQ], F32R)
        raw = st.sb("w_raw" + tag, [P, 2, FH * P])
        parts = st.sb("w_parts" + tag, [P, 4 * 2 * KT * P], F32R)
        up = parts[:].rearrange("p (b s h n) -> p b s h n", b=2, s=2, h=2)
        down = parts[:, 0:4 * FH * P].rearrange("p (b h n) -> p b h n", b=2, h=2)
        aw = e.h[:].rearrange("p k n -> p (k n)").rearrange("p (b k m) -> p b k m", b=ADA_SLOTS, k=KT)
        with nc.Block() as block:
            @block.sync
            def _(sp):
                def load_up(n, b):
                    sp.dma_start(raw[:, b, 0:KT * P], dram(w_up, L * 2 + which, n)).then_inc(raw_loaded[b], 16)

                def load_down(n, b):
                    sp.dma_start(raw[:, b], dram(w_down, L * 2 + which, n)).then_inc(raw_loaded[b], 16)

                def load_mod(n, b):
                    sp.dma_start(aw[:, b].rearrange("p k m -> p (k m)"), dram(ada_w, L, n + ADA_HEAD)).then_inc(mod_loaded[b], 16)

                for q in range(2):
                    load_up(q, q)
                for q in range(2):
                    sp.wait_ge(split_ready, q + 1)
                    load_up(2 + q, q)
                if ada:
                    sp.wait_ge(norm.ready, KT)
                    for b in range(ADA_SLOTS):
                        load_mod(b, b)
                with sp.Fori(1, UP) as i:
                    for q in range(4):
                        sp.wait_ge(split_ready, i * 4 + q - 1)
                        load_up(i * 4 + q, q % 2)
                        if ada:
                            sp.wait_ge(mod_acc, (i - 1) * ADA_UP + q + 1)
                            load_mod(i * ADA_UP + q, q)
                for q in range(2):
                    sp.wait_ge(split_ready, 4 * UP - 1 + q)
                    load_down(q, q)
                for q in range(2):
                    sp.wait_ge(down_split, q + 1)
                    load_down(2 + q, q)
                if ada:
                    for q in range(ADA_DOWN):
                        sp.wait_ge(mod_acc, UP * ADA_UP - ADA_UP + q + 1)
                        load_mod(UP * ADA_UP + q, q)
                with sp.Fori(1, DOWN) as i:
                    for q in range(4):
                        sp.wait_ge(down_split, i * 4 + q - 1)
                        load_down(i * 4 + q, q % 2)
                        if ada and q < ADA_DOWN:
                            sp.wait_ge(mod_acc, UP * ADA_UP + (i - 1) * ADA_DOWN + q + 1)
                            load_mod(UP * ADA_UP + i * ADA_DOWN + q, q)

            @block.gpsimd
            def _(pool):
                norm.gpsimd(pool)

            @block.tensor
            def _(pe):
                def mod_sum(bank, col, n, s):
                    pe.wait_ge(mod_acc, n + 1)
                    nc.tensor.matmul(bank[:, bass.ds(col, 1)], acc[:, s], e.k("ones")[:, 0:1],
                                     start=True, stop=True).then_inc(mod_sums, 1)

                pe.sem_inc(gate_ready, 2)
                pe.sem_inc(up_ready, 2)
                pe.sem_inc(half_ready, 1)
                pe.sem_inc(down_ready, 1)
                if ada:
                    pe.sem_inc(mod_sums, ADA_SLOTS)
                norm.tensor(pe)
                with pe.Fori(0, UP) as i:
                    for b in range(2):
                        n = i * 2 + b
                        pe.wait_ge(product_ready, n + 1)
                        for side, done in ((0, gate_ready), (1, up_ready)):
                            pe.wait_ge(split_ready, n * 2 + side + 1)
                            for k in range(KT):
                                if b == 0 and side == 0:
                                    pe.wait_ge(norm.ready, k + 1)
                                ks = slice(k * P, (k + 1) * P)
                                last = product(nc, e.bank[2 * b + side][:], up[:, b, side, 0, ks], up[:, b, side, 1, ks],
                                               norm.hi[:, k], norm.lo[:, k], k == 0, k == KT - 1)
                            last.then_inc(done, 1)
                        if ada:
                            for q in (2 * b, 2 * b + 1):
                                mod_sum(e.bank[6], i * ADA_UP + q, i * ADA_UP + q, q)
                with pe.Fori(0, DOWN) as i:
                    for b in range(2):
                        m = i * 2 + b
                        pe.wait_ge(down_free, m + 1)
                        for half in range(2):
                            pe.wait_ge(down_split, m * 2 + half + 1)
                            pe.wait_ge(hidden_ready, (half + 1) * FH)
                            for f in range(FH):
                                fs, ff = slice(f * P, (f + 1) * P), half * FH + f
                                last = product(nc, e.bank[4 + b][:], down[:, half, 0, fs], down[:, half, 1, fs],
                                               hid_hi[:, ff], hid_lo[:, ff], ff == 0, ff == FT - 1)
                            last.then_inc(down_ready if half else half_ready, 1)
                    if ada:
                        for q in range(ADA_DOWN):
                            mod_sum(e.bank[7], i * ADA_DOWN + q, i * ADA_DOWN + q + UP * ADA_UP, q)

            @block.scalar
            def _(act):
                norm.scalar(act)

                def round_up(n, b):
                    for side, used in ((0, gate_ready), (1, up_ready)):
                        act.wait_ge(raw_loaded[side], n * 16 + 16)
                        act.wait_ge(used, n + 1)
                        nc.scalar.activation(up[:, b, side, 0], raw[:, side, 0:KT * P], ACT.Copy).then_inc(high_ready, 1)

                def silu(n, b, hi):
                    act.wait_ge(gate_ready, n + 1 + 2)
                    act.wait_ge(product_ready, n + 1)
                    nc.scalar.activation(sg[:, b], e.bank[2 * b][:], ACT.Silu).then_inc(silu_ready, 1)
                    act.wait_ge(product_ready, n + 1 + 2)
                    nc.scalar.activation(hi, prod[:, b], ACT.Copy).then_inc(hidden_high, 1)

                def round_down(n, half, m):
                    act.wait_ge(raw_loaded[half], (m + FT + 1) * 16)
                    act.wait_ge(down_ready if half else half_ready, m + 1)
                    nc.scalar.activation(down[:, half, 0], raw[:, half], ACT.Copy).then_inc(down_high, 1)

                act.sem_inc(hidden_high, 2)
                round_up(0, 0)
                with act.Fori(0, UP - 1) as i:
                    round_up(i * 2 + 1, 1)
                    silu(i * 2, 0, at(hid_hi, i * 2))
                    round_up(i * 2 + 2, 0)
                    silu(i * 2 + 1, 1, at(hid_hi, i * 2 + 1))
                round_up(FT - 1, 1)
                for b in range(2):
                    silu(FT - 2 + b, b, hid_hi[:, FT - 2 + b])
                act.wait_ge(up_ready, FT + 2)
                with act.Fori(0, KT) as m:
                    for half in range(2):
                        round_down(m * 2 + half, half, m)

            @block.vector
            def _(dve):
                dve.sem_inc(product_ready, 2)
                dve.sem_inc(down_free, 2)
                norm.vector(dve)
                v = nc.vector

                def split_up(n, b):
                    for side in range(2):
                        dve.wait_ge(high_ready, n * 2 + side + 1)
                        v.tensor_tensor(up[:, b, side, 1], raw[:, side, 0:KT * P], up[:, b, side, 0].bitcast(F32), ALU.subtract).then_inc(split_ready, 1)

                def hidden(n, b, hi, lo):
                    dve.wait_ge(up_ready, n + 1 + 2)
                    dve.wait_ge(silu_ready, n + 1)
                    dve.wait_ge(hidden_high, n + 1)
                    v.tensor_tensor(prod[:, b], e.bank[2 * b + 1][:], sg[:, b], ALU.mult).then_inc(product_ready, 1)
                    dve.wait_ge(hidden_high, n + 1 + 2)
                    v.tensor_tensor(lo, prod[:, b], hi.bitcast(F32), ALU.subtract).then_inc(hidden_ready, 1)

                def mod(n, s, turn):
                    if ada:
                        dve.wait_ge(mod_loaded[s], turn * 16 + 16)
                        dve.wait_ge(mod_sums, n + 1)
                        mod_tile(nc, dve, acc[:, s], aw[:, s], e.csil).then_inc(mod_acc, 1)

                def split_down(n, half):
                    dve.wait_ge(down_high, n + 1)
                    v.tensor_tensor(down[:, half, 1], raw[:, half], down[:, half, 0].bitcast(F32), ALU.subtract).then_inc(down_split, 1)

                def add_to_x(m, b, xm, gate):
                    dve.wait_ge(down_ready, m + 1 + 1)
                    v.scalar_tensor_tensor(xm, e.bank[4 + b][:], gate, xm, ALU.mult, ALU.add).then_inc(down_free, 1)

                split_up(0, 0)
                with dve.Fori(0, UP - 1) as i:
                    for b in range(2):
                        n = i * 2 + b
                        split_up(n + 1, 1 - b)
                        for q in (2 * b, 2 * b + 1):
                            mod(i * ADA_UP + q, q, i)
                        hidden(n, b, at(hid_hi, n), at(hid_lo, n))
                split_up(FT - 1, 1)
                for b in range(2):
                    for q in (2 * b, 2 * b + 1):
                        mod((UP - 1) * ADA_UP + q, q, UP - 1)
                    n = FT - 2 + b
                    hidden(n, b, hid_hi[:, n], hid_lo[:, n])
                if ada:
                    done = UP * ADA_UP
                    dve.wait_ge(mod_sums, done + ADA_SLOTS)
                    v.tensor_tensor(e.mod[:, ADA_HEAD:ADA_HEAD + done], e.bank[6][:, 0:done], e.mod_b[:, ADA_HEAD:ADA_HEAD + done], ALU.add)
                    dve.drain()
                    v.tensor_scalar(e.gate[:, 0], e.mod[:, 2 * KT:3 * KT], 0.5, None, ALU.mult)
                    dve.drain()
                for half in range(2):
                    split_down(half, half)
                with dve.Fori(0, DOWN - 1) as i:
                    for b in range(2):
                        m = i * 2 + b
                        split_down(m * 2 + 2, 0)
                        add_to_x(m, b, at(e.x, m), e.gate[:, sub, bass.ds(m, 1)])
                        if b:
                            mod(i * ADA_DOWN + 1 + UP * ADA_UP + 1, 1, i + UP)
                        split_down(m * 2 + 3, 1)
                        mod(i * ADA_DOWN + 2 * b + UP * ADA_UP + 1, 2 * b, i + UP)
                m = KT - 2
                split_down(m * 2 + 2, 0)
                add_to_x(m, 0, e.x[:, m], e.gate[:, sub, m:m + 1])
                split_down(m * 2 + 3, 1)
                for q in range(ADA_DOWN):
                    mod((DOWN - 1) * ADA_DOWN + q + UP * ADA_UP + 1, q, DOWN - 1 + UP)
                add_to_x(KT - 1, 1, e.x[:, KT - 1], e.gate[:, sub, KT - 1:KT])
                if ada:
                    done = UP * ADA_UP
                    dve.wait_ge(mod_sums, MOD_REST + ADA_SLOTS)
                    v.tensor_tensor(e.mod[:, ADA_HEAD + done:], e.bank[7][:, 0:MOD_REST - done], e.mod_b[:, ADA_HEAD + done:], ALU.add)
                    dve.drain()
                    for s in (1, 2):
                        vec = lambda j: e.mod[:, (3 * s + j) * KT:(3 * s + j + 1) * KT]
                        v.scalar_tensor_tensor(e.coef[:, s], vec(1), 1.0, e.nw[:, s * KT:(s + 1) * KT], ALU.add, ALU.mult)
                        v.tensor_scalar(e.gate[:, s], vec(2), 1.0 if s == 1 else 0.5, None, ALU.mult)


def proj_stage(nc, e, L, const, w_tok, w_conv, conv_w):
    with Stage(nc) as st:
        tok_loaded = [st.sem(f"tok_loaded{b}") for b in range(2)]
        ch_loaded = [st.sem(f"ch_loaded{b}") for b in range(2)]
        const_loaded, small, tok_ready, even_free, odd_free, ch_ready, padded, convolved, conv_out, pad_zero = st.sems(
            "const_loaded taps_loaded tok_ready even_free odd_free ch_ready padded convolved conv_out pad_zero")
        norm = Norm(nc, e, st, 1, "_p")
        wt = st.sb("w_tok_sb", [P, 2, KT, PG])
        wc = st.sb("w_conv_sb", [P, 2, KT, P])
        taps = st.sb("taps", [P, N_CONV, CONV_K])
        pad = st.sb("conv_pad", [P, 2, SEQ + CONV_K - 1])
        acc = st.sb("conv_acc", [P, 2, SEQ])
        with nc.Block() as block:
            @block.sync
            def _(sp):
                def load_tok(n, b):
                    sp.dma_start(wt[:, b].rearrange("p k n -> p (k n)"), dram(w_tok, L, n)).then_inc(tok_loaded[b], 16)

                def load_ch(n, b):
                    sp.dma_start(wc[:, b].rearrange("p k n -> p (k n)"), dram(w_conv, L, n)).then_inc(ch_loaded[b], 16)

                for b in range(2):
                    load_tok(b, b)
                sp.dma_start(taps[:].rearrange("p n k -> p (n k)"), dram(conv_w, L)).then_inc(small, 16)
                for b in range(2):
                    load_ch(b, b)
                sp.dma_start(e.const[:], const[:, BASE_W:]).then_inc(const_loaded, 16)
                with sp.Fori(1, N_PG // 2) as i:
                    for b in range(2):
                        sp.wait_ge(tok_ready, (i * 2 + b - 1) * TT)
                        load_tok(i * 2 + b, b)
                with sp.Fori(1, N_CONV // 2) as i:
                    for b in range(2):
                        sp.wait_ge(ch_ready, i * 2 + b - 1)
                        load_ch(i * 2 + b, b)
                sp.wait_ge(const_loaded, 16)

            @block.tensor
            def _(pe):
                norm.tensor(pe)
                pe.wait_ge(norm.ready, KT)
                with pe.Fori(0, N_PG // 2) as i:
                    for b in range(2):
                        pe.wait_ge(tok_loaded[b], i * 16 + 16)
                        for t in range(TT):
                            pe.wait_ge(odd_free if t % 2 else even_free, i * 4 + b * 2 + t // 2 + 1)
                            for k in range(KT):
                                last = nc.tensor.matmul(e.bank[t][:, 0:PG], e.h[:, k, t * P:(t + 1) * P], wt[:, b, k],
                                                        start=k == 0, stop=k == KT - 1)
                            last.then_inc(tok_ready, 1)
                with pe.Fori(0, N_CONV // 2) as i:
                    for b in range(2):
                        pe.wait_ge(ch_loaded[b], i * 16 + 16)
                        pe.wait_ge(padded, i * 2 + b + 1)
                        for k in range(KT):
                            last = nc.tensor.matmul(e.bank[4 + b][:], wc[:, b, k], e.h[:, k], start=k == 0, stop=k == KT - 1)
                        last.then_inc(ch_ready, 1)

            @block.scalar
            def _(act):
                act.sem_inc(even_free, 2)
                act.sem_inc(padded, 2)
                act.sem_inc(conv_out, 2)
                norm.scalar(act)
                with act.Fori(0, N_PG // 2) as i:
                    for b in range(2):
                        for t in (0, 2):
                            act.wait_ge(tok_ready, i * 8 + b * 4 + t + 1)
                            nc.scalar.activation(e.proj[:, t, bass.ds((i * 2 + b) * PG, PG)], e.bank[t][:, 0:PG],
                                                 ACT.Copy).then_inc(even_free, 1)
                act.wait_ge(pad_zero, 1)
                with act.Fori(0, N_CONV // 2) as i:
                    for b in range(2):
                        act.wait_ge(ch_ready, i * 2 + b + 1)
                        act.wait_ge(convolved, i * 2 + b + 1)
                        nc.scalar.activation(pad[:, b, CONV_K - 1:], e.bank[4 + b][:], ACT.Copy).then_inc(padded, 1)
                        act.wait_ge(convolved, i * 2 + b + 3)
                        nc.scalar.activation(at(e.conv, i * 2 + b), acc[:, b], ACT.Silu).then_inc(conv_out, 1)

            @block.vector
            def _(dve):
                dve.sem_inc(odd_free, 2)
                dve.sem_inc(convolved, 2)
                nc.vector.memset(pad[:, :, 0:CONV_K - 1], 0.0).then_inc(pad_zero, 1)
                norm.vector(dve)
                with dve.Fori(0, N_PG // 2) as i:
                    for b in range(2):
                        for t in (1, 3):
                            dve.wait_ge(tok_ready, i * 8 + b * 4 + t + 1)
                            nc.vector.tensor_copy(e.proj[:, t, bass.ds((i * 2 + b) * PG, PG)], e.bank[t][:, 0:PG]).then_inc(odd_free, 1)
                dve.wait_ge(small, 16)
                with dve.Fori(0, N_CONV // 2) as i:
                    for b in range(2):
                        dve.wait_ge(padded, i * 2 + b + 3)
                        dve.wait_ge(conv_out, i * 2 + b + 1)
                        tap = at(taps, i * 2 + b)
                        nc.vector.tensor_scalar(acc[:, b], pad[:, b, 0:SEQ], tap[:, 0:1], None, ALU.mult)
                        for j in range(1, CONV_K):
                            dve.drain()
                            last = nc.vector.scalar_tensor_tensor(acc[:, b], pad[:, b, j:j + SEQ], tap[:, j:j + 1], acc[:, b],
                                                                  ALU.mult, ALU.add)
                        last.then_inc(convolved, 1)


def out_stage(nc, e, L, w_out):
    with Stage(nc) as st:
        w_loaded = [st.sem(f"wo_loaded{b}") for b in range(2)]
        turned, y_even, y_odd, out_ready, out_free = st.sems("turned y_even y_odd out_ready out_free")
        wo = st.sb("w_out_sb", [P, 2, KT, P])
        yt = st.sb("y_t", [P, KT, SEQ])
        with nc.Block() as block:
            @block.sync
            def _(sp):
                for b in range(2):
                    sp.dma_start(wo[:, b].rearrange("p k n -> p (k n)"), dram(w_out, L, b)).then_inc(w_loaded[b], 16)
                with sp.Fori(1, KT // 2) as i:
                    for b in range(2):
                        sp.wait_ge(out_ready, i * 2 + b - 1)
                        sp.dma_start(wo[:, b].rearrange("p k n -> p (k n)"), dram(w_out, L, i * 2 + b)).then_inc(w_loaded[b], 16)

            @block.tensor
            def _(pe):
                for k in range(KT):
                    if k >= 4:
                        pe.wait_ge(y_odd if k % 2 else y_even, (k - 4) // 2 + 1)
                    for t in range(TT):
                        last = nc.tensor.transpose(e.bank[k % 4][:, t * P:(t + 1) * P], e.y[:, t, k * P:(k + 1) * P], e.k("ident"))
                    last.then_inc(turned, 1)
                pe.wait_ge(y_even, KT // 2)
                pe.wait_ge(y_odd, KT // 2)
                with pe.Fori(0, KT // 2) as i:
                    for b in range(2):
                        pe.wait_ge(w_loaded[b], i * 16 + 16)
                        pe.wait_ge(out_free, i * 2 + b + 1)
                        for k in range(KT):
                            last = nc.tensor.matmul(e.bank[4 + b][:], wo[:, b, k], yt[:, k], start=k == 0, stop=k == KT - 1)
                        last.then_inc(out_ready, 1)

            @block.scalar
            def _(act):
                for k in range(0, KT, 2):
                    act.wait_ge(turned, k + 1)
                    nc.scalar.activation(yt[:, k], e.bank[k % 4][:], ACT.Copy).then_inc(y_even, 1)

            @block.vector
            def _(dve):
                dve.sem_inc(out_free, 2)
                for k in range(1, KT, 2):
                    dve.wait_ge(turned, k + 1)
                    nc.vector.tensor_copy(yt[:, k], e.bank[k % 4][:]).then_inc(y_odd, 1)
                with dve.Fori(0, KT // 2) as i:
                    for b in range(2):
                        dve.wait_ge(out_ready, i * 2 + b + 1)
                        xm = at(e.x, i * 2 + b)
                        nc.vector.scalar_tensor_tensor(xm, e.bank[4 + b][:], e.gate[:, 1, bass.ds(i * 2 + b, 1)], xm,
                                                       ALU.mult, ALU.add).then_inc(out_free, 1)


def bc(ap, n):
    return ap.broadcast_to(list(ap.shape[:-1]) + [n])


def mlstm_stage(nc, e, L, gate_b, head_norm_w):
    H = M_HEADS
    with Stage(nc) as st:
        (small, gates_in, absed, e_ready, ln_ready, forget_ready, cum_ready, cum_out, offsets_ready,
         qk_turned, qk_act, qk_dve, bcast_ready, head_copied, e_rows, e_out, rows_done, w_ready, score_ready, weighted,
         w_turned, w_copied_a, w_copied_v, pv_ready, head_done, exp_m, ssq_ready, root_ready, o_ready, e_free) = st.sems(
            "m_small gates_in absed e_ready ln_ready forget_ready cum_ready cum_out offsets_ready "
            "qk_turned qk_act qk_dve bcast_ready head_copied e_rows e_out rows_done w_ready score_ready weighted "
            "w_turned w_copied_a w_copied_v pv_ready head_done exp_m ssq_ready root_ready o_ready e_free")
        sb = lambda n, s: st.sb("m_" + n, s)
        gb = sb("gate_b", [P, 2 * H])
        nw = sb("norm_w", [P, 2 * HD])
        g = sb("gates", [P, TT, 2 * H])
        ga, ge = sb("gate_abs", [P, TT, H]), sb("gate_exp", [P, TT, H])
        lf = sb("log_f", [P, TT, H])
        cum, tot = sb("cum", [P, TT, H]), sb("tot", [P, TT, H])
        off = sb("off", [P, H, TT, TT])
        start = sb("start", [P, H, TT])
        qT, kT = sb("qT", [HD, H, SEQ]), sb("kT", [HD, H, SEQ])
        qs = sb("q_head", [HD, SEQ])
        lfb, lib = sb("lf_rows", [P, TT, P]), sb("li_rows", [P, TT, P])
        eo, ed = sb("e_off", [P, TT, P]), sb("e_diag", [P, TT, P])
        emax, dmax, cand = sb("emax", [P, TT]), sb("dmax", [P, TT]), sb("cand", [P, TT, TT])
        m1, rows = sb("m1", [P, TT]), sb("rows", [P, TT])
        nb, nd = sb("neg_b", [P, TT, TT]), sb("neg_d", [P, TT])
        w = sb("w", [P, TT, SEQ])
        sw = sb("sw", [P, TT, SEQ])
        swT = sb("swT", [P, 2, SEQ])
        num, den, mm = sb("num", [P, H, TT, HD]), sb("den", [P, H, TT]), sb("m", [P, H, TT])
        sq = sb("sq", [P, H, TT, HD])
        ss, rs = sb("ss", [P, H, TT]), sb("rs", [P, H, TT])
        og = sb("og", [P, TT, H * HD])
        causal = e.k("causal")
        tri = causal[:, SEQ - P:]
        with nc.Block() as block:
            @block.sync
            def _(sp):
                sp.dma_start(gb[:], dram(gate_b, L).broadcast_to([P, 2 * H])).then_inc(small, 16)
                sp.dma_start(nw[:], dram(head_norm_w, L).broadcast_to([P, 2 * HD])).then_inc(small, 16)

            @block.gpsimd
            def _(pool):
                nc.gpsimd.memset(off[:], 0.0)
                nc.gpsimd.memset(start[:], 0.0)
                pool.drain()
                for b in range(TT):
                    for i in range(b + 1):
                        nc.gpsimd.memset(off[:, :, i, b], NEG)
                pool.wait_ge(cum_out, 1)
                pool.drain()
                T = lambda u: tot[:, u, :]
                nc.gpsimd.tensor_copy(off[:, :, 2, 0], T(1))
                nc.gpsimd.tensor_copy(off[:, :, 3, 1], T(2))
                nc.gpsimd.tensor_tensor(off[:, :, 3, 0], T(1), T(2), ALU.add)
                nc.gpsimd.tensor_copy(start[:, :, 1], T(0))
                nc.gpsimd.tensor_tensor(start[:, :, 2], T(0), T(1), ALU.add)
                pool.drain()
                nc.gpsimd.tensor_tensor(start[:, :, 3], start[:, :, 2], T(2), ALU.add).then_inc(offsets_ready, 1)
                pool.wait_ge(qk_act, H)
                pool.wait_ge(qk_dve, H)
                with pool.Fori(0, H) as h:
                    pool.wait_ge(head_done, h)
                    nc.gpsimd.tensor_copy(lfb[:], bc(lf[:, :, bass.ds(h, 1)], P))
                    nc.gpsimd.tensor_copy(lib[:], bc(g[:, :, bass.ds(h, 1)], P)).then_inc(bcast_ready, 1)
                    nc.gpsimd.tensor_copy(qs[:], at(qT, h)).then_inc(head_copied, 1)

            @block.scalar
            def _(act):
                nc.scalar.activation(og[:], e.proj[:, :, C_MO:C_MO + H * HD], ACT.Sigmoid).then_inc(o_ready, 1)
                act.wait_ge(absed, 1)
                nc.scalar.activation(ge[:], ga[:], ACT.Exp, scale=-1.0).then_inc(e_ready, 1)
                act.wait_ge(e_ready, 1)
                nc.scalar.activation(ga[:], ge[:], ACT.Ln, bias=1.0).then_inc(ln_ready, 1)
                for h in range(H):
                    act.wait_ge(qk_turned, 2 * h + 1)
                    nc.scalar.activation(qT[:, h], e.bank[(2 * h) % 8][0:HD], ACT.Copy).then_inc(qk_act, 1)
                with act.Fori(0, H) as h:
                    act.wait_ge(rows_done, h + 1)
                    act.wait_ge(head_done, h)
                    for i in range(TT):
                        for b in range(i):
                            nc.scalar.activation(w[:, i, b * P:(b + 1) * P], eo[:, b], ACT.Exp, bias=nb[:, i, b:b + 1])
                        nc.scalar.activation(w[:, i, i * P:(i + 1) * P], ed[:, i], ACT.Exp, bias=nd[:, i:i + 1]).then_inc(w_ready, 1)
                    for i in (1, 3):
                        act.wait_ge(w_turned, h * TT + i + 1)
                        if i == 3:
                            act.wait_ge(pv_ready, h * TT + 2)
                        nc.scalar.activation(swT[:, 1, 0:(i + 1) * P], e.bank[5][:, 0:(i + 1) * P], ACT.Copy).then_inc(w_copied_a, 1)
                act.wait_ge(absed, 2)
                nc.scalar.activation(ss[:], mm[:], ACT.Exp, scale=-1.0).then_inc(exp_m, 1)
                act.wait_ge(ssq_ready, 1)
                nc.scalar.activation(rs[:], ss[:], ACT.Sqrt, bias=e.eps[:, 0:1], scale=1.0 / HD).then_inc(root_ready, 1)

            @block.tensor
            def _(pe):
                for h in range(H):
                    for n, c0 in ((0, C_MQ), (1, C_MK)):
                        for t in range(TT):
                            last = nc.tensor.transpose(e.bank[2 * h + n][0:HD, t * P:(t + 1) * P],
                                                       e.proj[:, t, c0 + h * HD:c0 + (h + 1) * HD], e.k("ident"))
                        last.then_inc(qk_turned, 1)
                pe.wait_ge(qk_act, 1)
                pe.wait_ge(forget_ready, 1)
                nc.tensor.matmul(e.bank[0][:, 0:TT * H], e.k("upper"), lf[:], start=True, stop=True)
                nc.tensor.matmul(e.bank[0][:, TT * H:2 * TT * H], e.k("ones"), lf[:], start=True, stop=True).then_inc(cum_ready, 1)
                pe.wait_ge(cum_out, 1)
                with pe.Fori(0, H) as h:
                    pe.wait_ge(bcast_ready, h + 1)
                    for b in range(TT):
                        r = e.bank[6 + b // 2][:, (b % 2) * 2 * P:(b % 2 + 1) * 2 * P]
                        nc.tensor.matmul(r, lfb[:, b], e.k("decay_sel"), start=True, stop=False)
                        last = nc.tensor.matmul(r, lib[:, b], e.k("ident2"), start=False, stop=True)
                    last.then_inc(e_rows, 1)
                    pe.wait_ge(head_copied, h + 1)
                    for i in range(TT):
                        n = (i + 1) * P
                        nc.tensor.matmul(e.bank[i][:, 0:n], qs[:, i * P:n], kT[:, bass.ds(h, 1), 0:n].rearrange("p a n -> p (a n)"),
                                         start=True, stop=True).then_inc(score_ready, 1)

                    def turn(i):
                        pe.wait_ge(weighted, h * TT + i + 1)
                        if i >= 2:
                            pe.wait_ge(w_copied_a if i % 2 else w_copied_v, h * 2 + 1)
                        for b in range(i + 1):
                            last = nc.tensor.transpose(e.bank[4 + i % 2][:, b * P:(b + 1) * P], sw[:, i, b * P:(b + 1) * P], e.k("ident"))
                        last.then_inc(w_turned, 1)

                    def values(i):
                        pe.wait_ge(w_copied_a if i % 2 else w_copied_v, h * 2 + i // 2 + 1)
                        if i == 0:
                            pe.wait_ge(e_out, h + 1)
                        for b in range(i + 1):
                            last = nc.tensor.matmul(e.bank[6][:, i * HD:(i + 1) * HD], swT[:, i % 2, b * P:(b + 1) * P],
                                                    e.proj[:, b, bass.ds(h * HD + C_MV, HD)], start=b == 0, stop=b == i)
                        last.then_inc(pv_ready, 1)

                    turn(0)
                    turn(1)
                    values(0)
                    turn(2)
                    values(1)
                    turn(3)
                    values(2)
                    values(3)
                    pe.wait_ge(head_done, h + 1)

            @block.vector
            def _(dve):
                v = nc.vector
                dve.wait_ge(small, 32)
                v.tensor_tensor(g[:], e.proj[:, :, C_MG:C_MG + 2 * H], gb[:].unsqueeze(1).broadcast_to([P, TT, 2 * H]), ALU.add)
                dve.drain()
                v.tensor_scalar(lf[:], g[:, :, H:], 0.0, None, ALU.min)
                v.scalar_tensor_tensor(ga[:], g[:, :, H:], -1.0, g[:, :, H:], ALU.mult, ALU.max).then_inc(absed, 1)
                for h in range(H):
                    dve.wait_ge(qk_turned, 2 * h + 2)
                    v.tensor_copy(kT[:, h], e.bank[2 * h + 1][0:HD]).then_inc(qk_dve, 1)
                dve.wait_ge(ln_ready, 1)
                v.tensor_tensor(lf[:], lf[:], ga[:], ALU.subtract).then_inc(forget_ready, 1)
                dve.wait_ge(cum_ready, 1)
                v.tensor_copy(cum[:].rearrange("p t h -> p (t h)"), e.bank[0][:, 0:TT * H])
                v.tensor_copy(tot[:].rearrange("p t h -> p (t h)"), e.bank[0][:, TT * H:2 * TT * H]).then_inc(cum_out, 1)
                dve.wait_ge(offsets_ready, 1)
                with dve.Fori(0, H) as h:
                    dve.wait_ge(e_rows, h + 1)
                    for b in range(TT):
                        v.tensor_tensor(ed[:, b], e.bank[6 + b // 2][:, (b % 2) * 256 + P:(b % 2) * 256 + 2 * P], tri, ALU.add)
                        last = v.tensor_copy(eo[:, b], e.bank[6 + b // 2][:, (b % 2) * 256:(b % 2) * 256 + P])
                    last.then_inc(e_out, 1)
                    dve.drain()
                    v.tensor_reduce(emax[:], eo[:], AX.X, ALU.max)
                    v.tensor_reduce(dmax[:], ed[:], AX.X, ALU.max)
                    dve.drain()
                    oh = at(off, h)
                    v.tensor_tensor(cand[:], oh, emax[:].unsqueeze(1).broadcast_to([P, TT, TT]), ALU.add)
                    v.tensor_tensor(dmax[:], dmax[:], start[:, bass.ds(h, 1), :].rearrange("p a t -> p (a t)"), ALU.max)
                    dve.drain()
                    v.tensor_reduce(m1[:], cand[:], AX.X, ALU.max)
                    dve.drain()
                    v.tensor_tensor(m1[:], m1[:], dmax[:], ALU.max)
                    dve.drain()
                    v.tensor_tensor(nb[:], oh, bc(m1[:].unsqueeze(2), TT), ALU.subtract)
                    v.tensor_tensor(mm[:, bass.ds(h, 1), :].rearrange("p a t -> p (a t)"), m1[:],
                                    cum[:, :, bass.ds(h, 1)].rearrange("p t a -> p (t a)"), ALU.add)
                    v.tensor_scalar(nd[:], m1[:], -1.0, None, ALU.mult).then_inc(rows_done, 1)
                    for i in range(TT):
                        n = (i + 1) * P
                        dve.wait_ge(score_ready, h * TT + i + 1)
                        dve.wait_ge(w_ready, h * TT + i + 1)
                        v.tensor_tensor_reduce(sw[:, i, 0:n], e.bank[i][:, 0:n], w[:, i, 0:n], SCALE, 0.0, ALU.mult, ALU.add,
                                               rows[:, i:i + 1]).then_inc(weighted, 1)
                    dve.drain()
                    v.tensor_copy(den[:, bass.ds(h, 1), :].rearrange("p a t -> p (a t)"), rows[:])
                    for i in (0, 2):
                        dve.wait_ge(w_turned, h * TT + i + 1)
                        if i == 2:
                            dve.wait_ge(pv_ready, h * TT + 1)
                        v.tensor_copy(swT[:, 0, 0:(i + 1) * P], e.bank[4][:, 0:(i + 1) * P]).then_inc(w_copied_v, 1)
                    dve.wait_ge(pv_ready, h * TT + TT)
                    v.tensor_copy(at(num, h), e.bank[6][:, 0:TT * HD].rearrange("p (t d) -> p t d", t=TT)).then_inc(head_done, 1)
                dve.drain()
                v.scalar_tensor_tensor(den[:], den[:], -1.0, den[:], ALU.mult, ALU.max).then_inc(absed, 1)
                dve.wait_ge(exp_m, 1)
                dve.drain()
                v.tensor_tensor(den[:], den[:], ss[:], ALU.max)
                dve.drain()
                v.reciprocal(den[:], den[:])
                dve.drain()
                v.tensor_tensor(num[:], num[:], bc(den[:].unsqueeze(3), HD), ALU.mult)
                dve.drain()
                v.tensor_tensor(sq[:], num[:], num[:], ALU.mult)
                dve.drain()
                v.tensor_reduce(ss[:], sq[:], AX.X, ALU.add).then_inc(ssq_ready, 1)
                dve.wait_ge(root_ready, 1)
                v.reciprocal(rs[:], rs[:])
                dve.drain()
                v.tensor_tensor(num[:], num[:], bc(rs[:].unsqueeze(3), HD), ALU.mult)
                dve.drain()
                v.tensor_tensor(sq[:].rearrange("p h t d -> p (h t) d"), num[:].rearrange("p h t d -> p (h t) d"),
                                nw[:, 0:HD].unsqueeze(1).broadcast_to([P, H * TT, HD]), ALU.mult)
                dve.wait_ge(o_ready, 1)
                dve.drain()
                for h in range(H):
                    v.tensor_tensor(e.y[:, :, h * HD:(h + 1) * HD], sq[:, h], og[:, :, h * HD:(h + 1) * HD], ALU.mult)


def delta_stage(nc, e, L, g_decay, head_norm_w):
    H = G_HEADS
    W = H * P
    with Stage(nc) as st:
        (small, decay_ready, beta_ready, a_exp, a_ln, alpha_ready, staged, raw_turned, raw_out, ssq_ready, root_ready, gam_ready, gam_out,
         gam_exp, normed, kq_turned, kq_out_v, kq_out_a, grams_ready, dec_arg, dec_ready, gram_out, x0_turned, prepared,
         masked, t1_ready, t1_out, dx_ready, inverted, w_ready, w_out, u_ready, u_out, o_ready, o_out, s_ready, z_ready,
         ssq2_ready, root2_ready, rows_ready, sq_done, s_out) = st.sems(
            "g_small decay_ready beta_ready a_exp a_ln alpha_ready staged raw_turned raw_out g_ssq_ready g_root_ready gam_ready gam_out "
            "gam_exp normed kq_turned kq_out_v kq_out_a grams_ready dec_arg dec_ready gram_out x0_turned prepared "
            "masked t1_ready t1_out dx_ready inverted wt_ready wt_out u_ready u_out g_o_ready g_o_out s_ready z_ready "
            "ssq2_ready root2_ready gam_rows_ready sq_done s_out")
        sb = lambda n, s: st.sb("g_" + n, s)
        gd = sb("decay", [P, 2 * H])
        nw = sb("norm_w", [P, 2 * HD])
        beta = sb("beta", [P, TT, H])
        la = sb("log_alpha", [P, TT, H])
        t1a, t1b = sb("t1a", [P, TT, H]), sb("t1b", [P, TT, H])
        stage = sb("stage", [P, N_CONV, P])
        raw = sb("raw", [P, 3 * H, HD])
        sq = sb("sq", [P, 2 * H, HD])
        ss, rt = sb("ss", [P, 2 * H]), sb("rt", [P, 2 * H])
        lac = sb("la_c", [P, H])
        lar = sb("la_rows", [P, H, P])
        gam, eg, egl = sb("gam", [P, H]), sb("eg", [P, H]), sb("egl", [P, H])
        qk = sb("qk", [P, 4, H, HD])
        qkT = sb("qkT", [HD, 3, H, P])
        dec = sb("dec", [P, H, P])
        at0 = sb("at0", [P, H, P])
        qgT = sb("qgT", [HD, TT, H, P])
        vb, kbg, kd = sb("vb", [P, TT, H, HD]), sb("kbg", [P, TT, H, HD]), sb("kd", [P, TT, H, HD])
        gl = sb("gl", [HD, TT, H])
        aT, pT = sb("aT", [P, TT, W]), sb("pT", [P, TT, W])
        xT, xn = sb("xT", [P, TT, W]), sb("xn", [P, TT, W])
        am, t1 = sb("am", [P, TT, W]), sb("t1", [P, TT, W])
        nwT = sb("nwT", [HD, TT, H, P])
        u = sb("u", [P, 2, H, HD])
        s = sb("s", [HD, H, HD])
        o = sb("o", [P, TT, H, HD])
        osq = am[:].rearrange("p t n -> p (t n)")[:, 0:TT * H * HD].rearrange("p (t h d) -> p t h d", t=TT, h=H)
        so, ro = sb("so", [P, TT, H]), sb("ro", [P, TT, H])
        zs = e.proj[:, :, C_Z:C_Z + H * HD]
        h4 = lambda b: b.rearrange("p (h n) -> p h n", h=H)
        odd_even = lambda t, half: t.rearrange("p (g b) n -> p g b n", b=2)[:, :, half]
        ident = e.k("ident")
        with nc.Block() as block:
            @block.sync
            def _(sp):
                sp.dma_start(gd[:], dram(g_decay, L).broadcast_to([P, 2 * H])).then_inc(small, 16)
                sp.dma_start(nw[:], dram(head_norm_w, L).broadcast_to([P, 2 * HD])).then_inc(small, 16)

            @block.gpsimd
            def _(pool):
                pool.wait_ge(prepared, TT)
                for n in range(LEVELS):
                    for c in range(TT):
                        pool.wait_ge(t1_ready, n * TT + c)
                        m = e.k("levels")[:, n * P:(n + 1) * P].unsqueeze(1)
                        nc.gpsimd.tensor_tensor(h4(am[:, c]), h4(aT[:, c]), m.broadcast_to([P, H, P]), ALU.mult).then_inc(masked, 1)

            @block.scalar
            def _(act):
                a = nc.scalar.activation
                a(zs, zs, ACT.Silu).then_inc(z_ready, 1)
                a(beta[:], e.proj[:, :, C_GB:C_GB + H], ACT.Sigmoid).then_inc(beta_ready, 1)
                act.wait_ge(small, 32)
                a(gd[:, 0:H], gd[:, 0:H], ACT.Exp).then_inc(decay_ready, 1)
                act.wait_ge(a_exp, 1)
                a(t1b[:], t1b[:], ACT.Exp, scale=-1.0).then_inc(a_ln, 1)
                act.wait_ge(a_ln, 1)
                a(t1b[:], t1b[:], ACT.Ln, bias=1.0).then_inc(a_ln, 1)
                with act.Fori(0, TT) as c:
                    act.wait_ge(raw_turned, c)
                    a(stage[:], e.conv[:, :, bass.ds(c * P, P)], ACT.Copy).then_inc(staged, 1)
                    act.wait_ge(ssq_ready, c + 1)
                    a(rt[:], ss[:], ACT.Sqrt, bias=e.eps[:, 0:1]).then_inc(root_ready, 1)
                    act.wait_ge(gam_out, c + 1)
                    a(eg[:], gam[:], ACT.Exp)
                    a(egl[:], egl[:], ACT.Exp)
                    act.wait_ge(rows_ready, c + 1)
                    a(gl[:, bass.ds(c, 1), :].rearrange("p a h -> p (a h)"), h4(e.bank[2][0:HD])[:, :, P - 1], ACT.Exp).then_inc(gam_exp, 1)
                    for n in (1, 3):
                        act.wait_ge(kq_turned, c * 4 + n + 1)
                        dst = qkT[:, 1] if n == 1 else qgT[:, bass.ds(c, 1)].rearrange("p a h n -> p (a h) n")
                        for half in range(2):
                            last = a(odd_even(dst, half), e.bank[4 + n][half * HD:(half + 1) * HD, 0:2 * P].rearrange("p (g n) -> p g n", g=2), ACT.Copy)
                        last.then_inc(kq_out_a, 1)
                    act.wait_ge(dec_arg, c + 1)
                    a(dec[:], dec[:], ACT.Exp).then_inc(dec_ready, 1)
                with act.Fori(0, LEVELS) as n:
                    for c in range(TT):
                        act.wait_ge(t1_ready, n * TT + c + 1)
                        a(t1[:, c], e.bank[c % 2][:], ACT.Copy).then_inc(t1_out, 1)
                for c in range(TT):
                    act.wait_ge(w_ready, c + 1)
                    a(nwT[:, c].rearrange("p h n -> p (h n)"), e.bank[c % 2][0:HD], ACT.Copy, scale=-1.0).then_inc(w_out, 1)
                for c in range(TT):
                    act.wait_ge(o_ready, c + 1)
                    a(o[:, c].rearrange("p h d -> p (h d)"), e.bank[4][:, 0:H * HD], ACT.Copy).then_inc(o_out, 1)
                act.wait_ge(ssq2_ready, 1)
                a(ro[:], so[:], ACT.Sqrt, bias=e.eps[:, 0:1], scale=1.0 / HD).then_inc(root2_ready, 1)

            @block.tensor
            def _(pe):
                mm = nc.tensor.matmul
                pe.wait_ge(alpha_ready, 1)
                with pe.Fori(0, TT) as c:
                    pe.wait_ge(staged, c + 1)
                    pe.wait_ge(prepared, c)
                    for n in range(N_CONV):
                        last = nc.tensor.transpose(e.bank[n // 4][:, (n % 4) * P:(n % 4 + 1) * P], stage[:, n], ident)
                    last.then_inc(raw_turned, 1)
                    pe.wait_ge(normed, c * 3 + 1)
                    mm(e.bank[3][:, 0:H], e.k("upper"), lac[:], start=True, stop=True).then_inc(gam_ready, 1)
                    for h in range(H):
                        last = mm(h4(e.bank[2][:])[:, h], lar[:, h], e.k("upper"), start=True, stop=True)
                    last.then_inc(rows_ready, 1)
                    pe.wait_ge(normed, c * 3 + 2)
                    for n in range(3):
                        for h in range(0, H, 2):
                            last = nc.tensor.transpose(e.bank[4 + n][:, h * HD:(h + 2) * HD], qk[:, n, h:h + 2].rearrange("p h d -> p (h d)"), ident)
                        last.then_inc(kq_turned, 1)
                    pe.wait_ge(normed, c * 3 + 3)
                    for h in range(0, H, 2):
                        last = nc.tensor.transpose(e.bank[7][:, h * HD:(h + 2) * HD], qk[:, 3, h:h + 2].rearrange("p h d -> p (h d)"), ident)
                    last.then_inc(kq_turned, 1)
                    pe.wait_ge(kq_out_v, c * 2 + 2)
                    pe.wait_ge(kq_out_a, c * 2 + 2)
                    for n, b in ((1, 0), (2, 1)):
                        for h in range(H):
                            last = mm(h4(e.bank[b][:])[:, h], qkT[:, 0, h], qkT[:, n, h], start=True, stop=True)
                    last.then_inc(grams_ready, 1)
                    pe.wait_ge(gram_out, c + 1)
                    for h in range(H):
                        last = nc.tensor.transpose(e.bank[5][:, h * P:(h + 1) * P], at0[:, h], ident)
                    last.then_inc(x0_turned, 1)
                pe.wait_ge(prepared, TT)
                with pe.Fori(0, LEVELS) as n:
                    def below(c):
                        pe.wait_ge(masked, n * TT + c + 1)
                        if c >= 2:
                            pe.wait_ge(t1_out, n * TT + c - 1)
                        for h in range(H):
                            last = mm(h4(e.bank[c % 2][:])[:, h], am[:, c, h * P:(h + 1) * P], xn[:, c, h * P:(h + 1) * P], start=True, stop=True)
                        last.then_inc(t1_ready, 1)

                    def join(c):
                        pe.wait_ge(t1_out, n * TT + c + 1)
                        if c >= 2:
                            pe.wait_ge(inverted, n * TT + c - 1)
                        for h in range(H):
                            hs = slice(h * P, (h + 1) * P)
                            mm(h4(e.bank[2 + 2 * (c % 2)][:])[:, h], t1[:, c, hs], xT[:, c, hs], start=True, stop=True)
                            last = mm(h4(e.bank[3 + 2 * (c % 2)][:])[:, h], xT[:, c, hs], t1[:, c, hs], start=True, stop=True)
                        last.then_inc(dx_ready, 1)

                    pe.wait_ge(inverted, n * TT)
                    below(0)
                    below(1)
                    join(0)
                    below(2)
                    join(1)
                    below(3)
                    join(2)
                    join(3)
                pe.wait_ge(inverted, LEVELS * TT)
                for c in range(TT):
                    if c >= 2:
                        pe.wait_ge(w_out, c - 1)
                    for h in range(H):
                        last = mm(e.bank[c % 2][0:HD, h * P:(h + 1) * P], kbg[:, c, h], xT[:, c, h * P:(h + 1) * P], start=True, stop=True)
                    last.then_inc(w_ready, 1)
                for c in range(TT):
                    pe.wait_ge(w_out, c + 1)
                    pe.wait_ge(s_out, c + 1)
                    for h in range(H):
                        b = e.bank[3][:, h * HD:(h + 1) * HD]
                        mm(b, xT[:, c, h * P:(h + 1) * P], vb[:, c, h], start=True, stop=False)
                        last = mm(b, nwT[:, c, h], s[:, h], start=False, stop=True)
                    last.then_inc(u_ready, 1)
                    pe.wait_ge(u_out, c + 1)
                    if c:
                        pe.wait_ge(o_out, c)
                    for h in range(H):
                        b = e.bank[4][:, h * HD:(h + 1) * HD]
                        mm(b, qgT[:, c, h], s[:, h], start=True, stop=False)
                        last = mm(b, pT[:, c, h * P:(h + 1) * P], u[:, c % 2, h], start=False, stop=True)
                    last.then_inc(o_ready, 1)
                    for h in range(H):
                        last = mm(e.bank[5][0:HD, h * HD:(h + 1) * HD], kd[:, c, h], u[:, c % 2, h], start=True, stop=True)
                    last.then_inc(s_ready, 1)

            @block.vector
            def _(dve):
                v = nc.vector
                bh = lambda x, n=HD: bc(x.unsqueeze(2), n)
                v.memset(s[:], 0.0)
                dve.wait_ge(small, 32)
                v.tensor_tensor(t1a[:], e.proj[:, :, C_GA:C_GA + H], gd[:, H:].unsqueeze(1).broadcast_to([P, TT, H]), ALU.add)
                dve.drain()
                v.scalar_tensor_tensor(t1b[:], t1a[:], -1.0, t1a[:], ALU.mult, ALU.max).then_inc(a_exp, 1)
                v.tensor_scalar(t1a[:], t1a[:], 0.0, None, ALU.max)
                dve.drain()
                dve.wait_ge(a_ln, 2)
                v.tensor_tensor(t1a[:], t1a[:], t1b[:], ALU.add)
                dve.drain()
                dve.wait_ge(decay_ready, 1)
                v.scalar_tensor_tensor(la[:], t1a[:], -1.0, gd[:, 0:H].unsqueeze(1).broadcast_to([P, TT, H]), ALU.mult, ALU.mult).then_inc(alpha_ready, 1)
                dve.wait_ge(beta_ready, 1)
                with dve.Fori(0, TT) as c:
                    dve.drain()
                    v.tensor_copy(lac[:], la[:, bass.ds(c, 1), :].rearrange("p a h -> p (a h)"))
                    v.tensor_copy(lar[:], bc(la[:, bass.ds(c, 1), :].rearrange("p a h -> p (a h)").unsqueeze(2), P)).then_inc(normed, 1)
                    dve.wait_ge(raw_turned, c + 1)
                    v.tensor_copy(raw[:, 0:8].rearrange("p h d -> p (h d)"), e.bank[0][:])
                    v.tensor_copy(raw[:, 8:12].rearrange("p h d -> p (h d)"), e.bank[1][:, 0:H * HD])
                    dve.drain()
                    v.tensor_tensor(sq[:], raw[:, 0:8], raw[:, 0:8], ALU.mult)
                    dve.drain()
                    v.tensor_reduce(ss[:], sq[:], AX.X, ALU.add).then_inc(ssq_ready, 1)
                    dve.wait_ge(gam_ready, c + 1)
                    dve.wait_ge(rows_ready, c + 1)
                    v.tensor_copy(gam[:], e.bank[3][:, 0:H])
                    dve.drain()
                    v.tensor_tensor(egl[:], h4(e.bank[2][:])[:, :, P - 1], gam[:], ALU.subtract).then_inc(gam_out, 1)
                    dve.wait_ge(root_ready, c + 1)
                    v.reciprocal(ss[:], rt[:])
                    dve.drain()
                    k_, kb_, q_, qg_ = (qk[:, n] for n in range(4))
                    bt = beta[:, bass.ds(c, 1), :].rearrange("p a h -> p (a h)")
                    v.tensor_tensor(k_, raw[:, 4:8], bh(ss[:, 4:8]), ALU.mult)
                    v.tensor_tensor(q_, raw[:, 0:4], bh(ss[:, 0:4]), ALU.mult)
                    dve.drain()
                    v.tensor_tensor(kb_, k_, bh(bt), ALU.mult)
                    v.tensor_scalar(q_, q_, SCALE, None, ALU.mult).then_inc(normed, 1)
                    dve.drain()
                    dve.wait_ge(gam_exp, c + 1)
                    col = lambda t: t[:, bass.ds(c, 1)].rearrange("p a h n -> p (a h) n")
                    v.tensor_tensor(qg_, q_, bh(eg[:]), ALU.mult).then_inc(normed, 1)
                    v.tensor_tensor(col(kbg), kb_, bh(eg[:]), ALU.mult)
                    v.tensor_tensor(col(kd), k_, bh(egl[:]), ALU.mult)
                    v.tensor_tensor(col(vb), raw[:, 8:12], bh(bt), ALU.mult)
                    v.tensor_tensor(dec[:], h4(e.bank[2][:]), bh(gam[:], P), ALU.subtract)
                    dve.drain()
                    v.tensor_tensor(dec[:], dec[:], e.k("causal_t").unsqueeze(1).broadcast_to([P, H, P]), ALU.add).then_inc(dec_arg, 1)
                    for n in (0, 2):
                        dve.wait_ge(kq_turned, c * 4 + n + 1)
                        for half in range(2):
                            last = v.tensor_copy(odd_even(qkT[:, n], half), e.bank[4 + n][half * HD:(half + 1) * HD, 0:2 * P].rearrange("p (g n) -> p g n", g=2))
                        last.then_inc(kq_out_v, 1)
                    dve.wait_ge(dec_ready, c + 1)
                    dve.wait_ge(grams_ready, c + 1)
                    row = lambda t: h4(t[:, bass.ds(c, 1)].rearrange("p a n -> p (a n)"))
                    v.tensor_tensor(at0[:], h4(e.bank[0][:]), dec[:], ALU.mult)
                    v.tensor_tensor(row(pT), h4(e.bank[1][:]), dec[:], ALU.mult)
                    dve.drain()
                    v.tensor_copy(row(aT), at0[:])
                    dve.drain()
                    v.tensor_tensor(at0[:], at0[:], e.k("level0").unsqueeze(1).broadcast_to([P, H, P]), ALU.mult)
                    dve.drain()
                    v.tensor_tensor(at0[:], ident.unsqueeze(1).broadcast_to([P, H, P]), at0[:], ALU.subtract).then_inc(gram_out, 1)
                    dve.drain()
                    v.tensor_copy(row(xT), at0[:])
                    dve.wait_ge(x0_turned, c + 1)
                    v.tensor_copy(row(xn), h4(e.bank[5][:])).then_inc(prepared, 1)
                with dve.Fori(0, LEVELS) as n:
                    for c in range(TT):
                        dve.wait_ge(dx_ready, n * TT + c + 1)
                        v.tensor_tensor(xT[:, c], xT[:, c], e.bank[2 + 2 * (c % 2)][:], ALU.subtract)
                        v.tensor_tensor(xn[:, c], xn[:, c], e.bank[3 + 2 * (c % 2)][:], ALU.subtract).then_inc(inverted, 1)
                v.memset(so[:], 0.0).then_inc(s_out, 1)
                for c in range(TT):
                    dve.wait_ge(u_ready, c + 1)
                    v.tensor_copy(u[:, c % 2].rearrange("p h d -> p (h d)"), e.bank[3][:, 0:H * HD]).then_inc(u_out, 1)
                    dve.wait_ge(o_ready, c + 1)
                    v.tensor_tensor(s[:], s[:], bh(gl[:, c]), ALU.mult)
                    dve.drain()
                    dve.wait_ge(s_ready, c + 1)
                    v.tensor_tensor(s[:], s[:], e.bank[5][0:HD, 0:H * HD].rearrange("p (h d) -> p h d", h=H), ALU.add).then_inc(s_out, 1)
                dve.wait_ge(o_out, TT)
                v.tensor_tensor(osq, o[:], o[:], ALU.mult)
                dve.drain()
                v.tensor_reduce(so[:], osq, AX.X, ALU.add).then_inc(ssq2_ready, 1)
                dve.wait_ge(root2_ready, 1)
                v.reciprocal(ro[:], ro[:])
                dve.drain()
                v.tensor_tensor(o[:], o[:], bc(ro[:].unsqueeze(3), HD), ALU.mult)
                dve.drain()
                th = lambda x: x.rearrange("p t h d -> p (t h) d")
                v.tensor_tensor(th(osq), th(o[:]), nw[:, HD:].unsqueeze(1).broadcast_to([P, TT * H, HD]), ALU.mult)
                dve.drain()
                dve.wait_ge(z_ready, 1)
                v.tensor_tensor(e.y[:, :, M_W:M_W + H * HD], osq.rearrange("p t h d -> p t (h d)"), zs, ALU.mult)


def nsa_stage(nc, e, L, qk_norm, cmp_pos, cmp_w1, cmp_w2):
    NQ, NK = N_HEADS, 2 * N_KV
    NH = NQ + NK
    NC = N_CMP
    PAIRS = CMP_BLOCK // 2
    HT = CMP_HIDDEN // P
    with Stage(nc) as st:
        (small, w1_loaded, w2_loaded, gates_ready, ss_ready, root_ready, roped, q_turned, qk_out_v, qk_out_a, c_turned, blocks_ready,
         hid_ready, hid_out, kc_ready, kc_ss, kc_root, kc_roped, kc_turned, kc_out, vc_ready, cs_ready, cs_masked, cp_ready, cp_scaled,
         cp_turned, cp_out, co_ready, co_out, q_copied, score_ready, tile_taken, max_ready, prob_ready, turned, t_out_v, t_out_a,
         pv_ready, combined, squared, blk_zero, masked) = st.sems(
            "n_small w1_loaded w2_loaded n_gates_ready n_ss_ready n_root_ready roped q_turned qk_out_v qk_out_a c_turned blocks_ready "
            "hid_ready hid_out kc_ready kc_ss kc_root kc_roped kc_turned kc_out vc_ready cs_ready cs_masked cp_ready cp_scaled "
            "cp_turned cp_out co_ready co_out q_copied n_score_ready tile_taken max_ready prob_ready n_turned t_out_v t_out_a "
            "n_pv_ready combined n_squared blk_zero n_masked")
        sb = lambda n, s: st.sb("n_" + n, s)
        qw = sb("qk_norm", [P, 4, HD])
        wt = sb("norm_rows", [P, NH, HD])
        pos = sb("pos", [P, 2, PAIRS])
        w1 = sb("w1", [P, 2, PAIRS, CMP_HIDDEN])
        w2 = sb("w2", [P, 2, HT, HD])
        ng = sb("gates", [P, TT, 3 * NQ])
        ss, rs = sb("ss", [P, TT, NH]), sb("rs", [P, TT, NH])
        qn = e.conv[:].rearrange("p n s -> p (n s)").rearrange("p (t h d) -> p t h d", t=TT, h=NH)
        qT, kT = sb("qT", [HD, NQ, SEQ]), sb("kT", [HD, NK, SEQ])
        blk = sb("blocks", [P, 2, PAIRS, N_KV * NC])
        hidT = sb("hidT", [P, 2, HT, N_KV * NC])
        kc, kc1, kc2 = sb("kc", [NC, N_KV, HD]), sb("kc1", [NC, N_KV, HD]), sb("kc2", [NC, N_KV, HD])
        ks, kr = sb("kc_ss", [NC, N_KV]), sb("kc_rs", [NC, N_KV])
        kcT = sb("kcT", [HD, N_KV, 32])
        vcb = sb("vc_blocks", [P, N_KV, GROUP, HD])
        cp = sb("cp", [P, TT, NQ, 32])
        cm, cs = sb("cmp_max", [P, TT, NQ]), sb("cmp_sum", [P, TT, NQ])
        cpT = sb("cpT", [P, 2, P])
        qs = sb("q_head", [HD, N_KV, SEQ])
        sm = sb("masked_s", [P, 2, TT, SEQ])
        r1, r2 = (sm[:, n].rearrange("p t s -> p (t s)")[:, 0:NH * HD].rearrange("p (h d) -> p h d", h=NH) for n in range(2))
        pr = w1[:].rearrange("p a b c -> p (a b c)")[:, 0:2 * TT * SEQ].rearrange("p (a t s) -> p a t s", a=2, t=TT)
        pt = sb("probs_t", [P, 2, SEQ])
        mx, nm, rsum = sb("mx", [P, 2, TT]), sb("neg_max", [P, 2, TT]), sb("row_sum", [P, 2, TT])
        cf, om = sb("coef_o", [P, TT]), sb("o_scaled", [P, TT, HD])
        causal, ident = e.k("causal"), e.k("ident")
        Y0 = M_W + G_HEADS * HD
        prep = ((0, NQ, C_Q), (NQ, N_KV, C_KS), (NQ + N_KV, N_KV, C_KWN))
        half = HD // 2
        v_cols = (C_VS, C_VWN)

        def compressed(pe, mm, i):
            t, kv = i // N_KV, i % N_KV
            pe.wait_ge(cp_out, i + 1)
            if i >= 2:
                pe.wait_ge(co_out, i - 1)
            mm(e.bank[6 + i % 2][:, 0:GROUP * HD], cpT[:, i % 2], vcb[:, kv].rearrange("p g d -> p (g d)"), start=True, stop=True).then_inc(co_ready, 1)

        def take(dve, v, i):
            t, kv = i // N_KV, i % N_KV
            dve.wait_ge(co_ready, i + 1)
            v.tensor_copy(e.y[:, t, Y0 + kv * GROUP * HD:Y0 + (kv + 1) * GROUP * HD], e.bank[6 + i % 2][:, 0:GROUP * HD]).then_inc(co_out, 1)

        with nc.Block() as block:
            @block.sync
            def _(sp):
                sp.dma_start(qw[:].rearrange("p a d -> p (a d)"), dram(qk_norm, L).broadcast_to([P, 4 * HD])).then_inc(small, 16)
                sp.dma_start(pos[:].rearrange("p a b -> p (a b)"), dram(cmp_pos, L)).then_inc(small, 16)
                sp.dma_start(w1[:].rearrange("p a b c -> p (a b c)"), dram(cmp_w1, L)).then_inc(w1_loaded, 16)
                sp.dma_start(w2[:].rearrange("p a b c -> p (a b c)"), dram(cmp_w2, L)).then_inc(w2_loaded, 16)

            @block.gpsimd
            def _(pool):
                nc.gpsimd.memset(vcb[:], 0.0).then_inc(blk_zero, 1)
                nc.gpsimd.memset(cp[:], 0.0).then_inc(blk_zero, 1)
                pool.wait_ge(qk_out_v, NH // 2)
                pool.wait_ge(qk_out_a, NH // 2)
                with pool.Fori(0, GROUP) as g:
                    pool.wait_ge(score_ready, g * 16)
                    nc.gpsimd.tensor_copy(qs[:], qT[:].rearrange("p (k g) s -> p k g s", k=N_KV)[:, :, bass.ds(g, 1)].rearrange("p k a s -> p k (a s)")).then_inc(q_copied, 1)

            @block.scalar
            def _(act):
                a = nc.scalar.activation
                act.sem_inc(prob_ready, 8)
                a(ng[:], e.proj[:, :, C_NG:C_NG + 3 * NQ], ACT.Sigmoid).then_inc(gates_ready, 1)
                act.wait_ge(ss_ready, TT)
                a(rs[:], ss[:], ACT.Sqrt, bias=e.eps[:, 0:1], scale=1.0 / HD).then_inc(root_ready, 1)
                act.wait_ge(hid_ready, 1)
                a(hidT[:], e.bank[7][:, 0:2 * HT * 64].rearrange("p (a b n) -> p a b n", a=2, b=HT)[:, :, :, 0:N_KV * NC], ACT.Silu).then_inc(hid_out, 1)
                act.wait_ge(kc_ss, 1)
                a(kr[:], ks[:], ACT.Sqrt, bias=e.eps[0:NC, 0:1], scale=1.0 / HD).then_inc(kc_root, 1)
                for n in range(NH // 2):
                    act.wait_ge(q_turned, n + 1)
                    hh = 2 * n + 1
                    act.wait_ge(qk_out_v, n + 1)
                    a(qT[:, hh] if hh < NQ else kT[:, hh - NQ], e.bank[n % 4][HD:P], ACT.Copy).then_inc(qk_out_a, 1)
                act.wait_ge(cs_masked, 1)
                a(cp[:, :, :, 0:NC], cp[:, :, :, 0:NC], ACT.Exp, scale=SCALE).then_inc(cp_ready, 1)
                with act.Fori(0, GROUP) as g:
                    def probs(j):
                        act.wait_ge(combined, g * 4 + j + 1)
                        act.wait_ge(turned, g * 16 + j * 4 + 4)
                        act.wait_ge(max_ready, g * 4 + j + 1)
                        for t in range(TT):
                            n = (t + 1) * P
                            a(pr[:, j % 2, t, 0:n], sm[:, j % 2, t, 0:n], ACT.Exp, bias=nm[:, j % 2, t:t + 1], scale=SCALE,
                              accum_out=rsum[:, j % 2, t:t + 1]).then_inc(prob_ready, 1)

                    def last_tile(j):
                        act.wait_ge(turned, g * 16 + j * 4 + 4 + 8)
                        act.wait_ge(pv_ready, g * 16 + j * 4 + 6)
                        a(pt[:, 1], e.bank[5][:], ACT.Copy).then_inc(t_out_a, 1)

                    probs(0)
                    for j in range(1, 4):
                        probs(j)
                        last_tile(j - 1)
                    last_tile(3)

            @block.tensor
            def _(pe):
                mm, tr = nc.tensor.matmul, nc.tensor.transpose
                pe.sem_inc(turned, 8)
                pe.sem_inc(pv_ready, 4)
                for n, c0 in ((0, C_KC), (1, C_VC)):
                    for t in range(TT):
                        last = tr(e.bank[5 + n][:, t * P:(t + 1) * P], e.proj[:, t, c0:c0 + P], ident)
                    last.then_inc(c_turned, 1)
                pe.wait_ge(w1_loaded, 16)
                for n in range(2):
                    pe.wait_ge(blocks_ready, n + 1)
                    for ht in range(HT):
                        for a_ in range(PAIRS):
                            last = mm(e.bank[7][:, (n * HT + ht) * 64:(n * HT + ht) * 64 + N_KV * NC],
                                      w1[:, n, a_, ht * P:(ht + 1) * P], blk[:, n, a_], start=a_ == 0, stop=a_ == PAIRS - 1)
                last.then_inc(hid_ready, 1)
                pe.wait_ge(w2_loaded, 16)
                pe.wait_ge(hid_out, 1)
                for n in range(2):
                    for kv in range(N_KV):
                        for ht in range(HT):
                            last = mm(e.bank[4][0:NC, (n * N_KV + kv) * HD:(n * N_KV + kv + 1) * HD],
                                      hidT[:, n, ht, kv * NC:(kv + 1) * NC], w2[:, n, ht], start=ht == 0, stop=ht == HT - 1)
                last.then_inc(kc_ready, 1)
                for n in range(NH // 2):
                    pe.wait_ge(roped, TT)
                    if n >= 4:
                        pe.wait_ge(qk_out_a, n - 3)
                    for t in range(TT):
                        last = tr(e.bank[n % 4][:, t * P:(t + 1) * P], qn[:, t, 2 * n:2 * n + 2].rearrange("p h d -> p (h d)"), ident)
                    last.then_inc(q_turned, 1)
                pe.wait_ge(kc_roped, 1)
                for kv in range(N_KV):
                    last = tr(e.bank[5][0:HD, kv * 32:kv * 32 + NC], kc2[:, kv], ident[0:NC, 0:NC])
                last.then_inc(kc_turned, 1)
                pe.wait_ge(kc_out, 1)
                pe.wait_ge(qk_out_a, NH // 2)
                pe.wait_ge(qk_out_v, NH // 2)
                for t in range(TT):
                    for h in range(NQ):
                        last = mm(e.bank[t // 2][:, ((t % 2) * NQ + h) * 32:((t % 2) * NQ + h) * 32 + NC],
                                  qT[:, h, t * P:(t + 1) * P], kcT[:, h // GROUP, 0:NC], start=True, stop=True)
                last.then_inc(cs_ready, 1)
                pe.wait_ge(cp_scaled, 1)
                pe.wait_ge(vc_ready, 1)
                for i in range(TT * N_KV):
                    t, kv = i // N_KV, i % N_KV
                    if i >= 2:
                        pe.wait_ge(cp_out, i - 1)
                    tr(e.bank[2 + i % 2][:, 0:P], cp[:, t, kv * GROUP:(kv + 1) * GROUP].rearrange("p h n -> p (h n)"), ident).then_inc(cp_turned, 1)
                    if i >= 1:
                        compressed(pe, mm, i - 1)
                compressed(pe, mm, TT * N_KV - 1)
                pe.wait_ge(co_out, TT * N_KV)

                with pe.Fori(0, GROUP) as g:
                    pe.wait_ge(q_copied, g + 1)

                    def scores(j):
                        kv, br = j // 2, j % 2
                        for t in range(TT):
                            n = (t + 1) * P
                            pe.wait_ge(masked, g * 16 + j * 4 + t + 1)
                            mm(e.bank[t][:, 0:n], qs[:, kv, t * P:n], kT[:, br * N_KV + kv, 0:n], start=True, stop=True).then_inc(score_ready, 1)

                    def turn(j, t):
                        u = g * 4 + j
                        pe.wait_ge(prob_ready, g * 16 + j * 4 + t + 1 + 8)
                        if t == 1:
                            pe.wait_ge(t_out_a, u)
                        else:
                            pe.wait_ge(t_out_v, g * 12 + j * 3 + (0, 0, 1, 2)[t])
                        for b in range(t + 1):
                            last = tr(e.bank[4 + t % 2][:, b * P:(b + 1) * P], pr[:, j % 2, t, b * P:(b + 1) * P], ident)
                        last.then_inc(turned, 1)

                    def values(j, t):
                        kv, br = j // 2, j % 2
                        if t == 0:
                            pe.wait_ge(combined, g * 4 + j + 1)
                        if t == 3:
                            pe.wait_ge(t_out_a, g * 4 + j + 1)
                        else:
                            pe.wait_ge(t_out_v, g * 12 + j * 3 + t + 1)
                        for b in range(t + 1):
                            last = mm(e.bank[6 + j % 2][:, t * HD:(t + 1) * HD], pt[:, t % 2, b * P:(b + 1) * P],
                                      e.proj[:, b, v_cols[br] + kv * HD:v_cols[br] + (kv + 1) * HD], start=b == 0, stop=b == t)
                        last.then_inc(pv_ready, 1)

                    def outputs(j):
                        turn(j, 0)
                        for t in range(1, TT):
                            turn(j, t)
                            values(j, t - 1)
                        values(j, TT - 1)

                    scores(0)
                    for j in range(1, 4):
                        scores(j)
                        outputs(j - 1)
                    outputs(3)

            @block.vector
            def _(dve):
                v = nc.vector
                dve.sem_inc(masked, 4)
                dve.sem_inc(combined, 2)
                dve.wait_ge(small, 32)
                for n in range(2):
                    dve.wait_ge(c_turned, n + 1)
                    for kv in range(N_KV):
                        for par in range(2):
                            for hi in range(2):
                                rows = e.bank[5 + n][kv * HD:(kv + 1) * HD].rearrange("p (w a r) -> p r a w", r=2, a=PAIRS // 2)[:, par, :, hi:hi + NC]
                                dst = blk[par * HD:(par + 1) * HD, n, hi * 8:(hi + 1) * 8, kv * NC:(kv + 1) * NC]
                                ps_ = pos[par * HD:(par + 1) * HD, n, hi * 8:(hi + 1) * 8]
                                last = v.tensor_tensor(dst, rows, bc(ps_.unsqueeze(2), NC), ALU.add)
                    last.then_inc(blocks_ready, 1)
                for h0, nh, _c in prep:
                    row = {0: 0, NQ: 2, NQ + N_KV: 3}[h0]
                    v.tensor_copy(wt[:, h0:h0 + nh], qw[:, row].unsqueeze(1).broadcast_to([P, nh, HD]))
                with dve.Fori(0, TT) as t:
                    for h0, nh, c0 in prep:
                        x = e.proj[:, bass.ds(t, 1), c0:c0 + nh * HD].rearrange("p a n -> p (a n)").rearrange("p (h d) -> p h d", h=nh)
                        v.tensor_tensor(r1[:, h0:h0 + nh], x, x, ALU.mult)
                    dve.drain()
                    v.tensor_reduce(ss[:, bass.ds(t, 1), :].rearrange("p a h -> p (a h)"), r1, AX.X, ALU.add).then_inc(ss_ready, 1)
                    dve.drain()
                dve.wait_ge(root_ready, 1)
                v.reciprocal(rs[:], rs[:])
                with dve.Fori(0, TT) as t:
                    dve.drain()
                    for h0, nh, c0 in prep:
                        x = e.proj[:, bass.ds(t, 1), c0:c0 + nh * HD].rearrange("p a n -> p (a n)").rearrange("p (h d) -> p h d", h=nh)
                        v.tensor_tensor(r1[:, h0:h0 + nh], x, bc(rs[:, bass.ds(t, 1), h0:h0 + nh].rearrange("p a h -> p (a h)").unsqueeze(2), HD), ALU.mult)
                    dve.drain()
                    v.tensor_tensor(r1, r1, wt[:], ALU.mult)
                    dve.drain()
                    tab = lambda n: e.k(n).rearrange("p (t d) -> p t d", t=TT)[:, bass.ds(t, 1)]
                    dst = at4(qn, t)
                    v.tensor_tensor(dst, r1, tab("cos").broadcast_to([P, NH, HD]), ALU.mult)
                    v.tensor_tensor(r2[:, :, 0:half], r1[:, :, half:], tab("sin")[:, :, 0:half].broadcast_to([P, NH, half]), ALU.mult)
                    v.tensor_tensor(r2[:, :, half:], r1[:, :, 0:half], tab("sin")[:, :, half:].broadcast_to([P, NH, half]), ALU.mult)
                    dve.drain()
                    v.tensor_tensor(dst, dst, r2, ALU.add).then_inc(roped, 1)
                dve.wait_ge(kc_ready, 1)
                dve.wait_ge(blk_zero, 2)
                v.tensor_copy(kc[:].rearrange("p k d -> p (k d)"), e.bank[4][0:NC, 0:N_KV * HD])
                for kv in range(N_KV):
                    for g in range(GROUP):
                        last = v.tensor_copy(vcb[32 * g:32 * g + NC, kv, g], e.bank[4][0:NC, (N_KV + kv) * HD:(N_KV + kv + 1) * HD])
                last.then_inc(vc_ready, 1)
                dve.drain()
                v.tensor_tensor(kc1[:], kc[:], kc[:], ALU.mult)
                dve.drain()
                v.tensor_reduce(ks[:], kc1[:], AX.X, ALU.add).then_inc(kc_ss, 1)
                dve.wait_ge(kc_root, 1)
                v.reciprocal(kr[:], kr[:])
                dve.drain()
                v.tensor_tensor(kc[:], kc[:], bc(kr[:].unsqueeze(2), HD), ALU.mult)
                dve.drain()
                v.tensor_tensor(kc[:], kc[:], qw[0:NC, 1].unsqueeze(1).broadcast_to([NC, N_KV, HD]), ALU.mult)
                dve.drain()
                ctab = lambda n: e.k(n)[0:NC].unsqueeze(1)
                v.tensor_tensor(kc2[:], kc[:], ctab("cmp_cos").broadcast_to([NC, N_KV, HD]), ALU.mult)
                v.tensor_tensor(kc1[:, :, 0:half], kc[:, :, half:], ctab("cmp_sin")[:, :, 0:half].broadcast_to([NC, N_KV, half]), ALU.mult)
                v.tensor_tensor(kc1[:, :, half:], kc[:, :, 0:half], ctab("cmp_sin")[:, :, half:].broadcast_to([NC, N_KV, half]), ALU.mult)
                dve.drain()
                v.tensor_tensor(kc2[:], kc2[:], kc1[:], ALU.add).then_inc(kc_roped, 1)
                for n in range(NH // 2):
                    dve.wait_ge(q_turned, n + 1)
                    hh = 2 * n
                    v.tensor_copy(qT[:, hh] if hh < NQ else kT[:, hh - NQ], e.bank[n % 4][0:HD]).then_inc(qk_out_v, 1)
                dve.wait_ge(kc_turned, 1)
                v.tensor_copy(kcT[:, :, 0:NC], e.bank[5][0:HD, 0:64].rearrange("p (k n) -> p k n", k=N_KV)[:, :, 0:NC]).then_inc(kc_out, 1)
                dve.wait_ge(cs_ready, 1)
                for t in range(TT):
                    src = e.bank[t // 2][:].rearrange("p (u h n) -> p u h n", u=2, h=NQ)[:, t % 2, :, 0:NC]
                    v.tensor_tensor(cp[:, t, :, 0:NC], src, e.k("cmp_mask")[:, t * NC:(t + 1) * NC].unsqueeze(1).broadcast_to([P, NQ, NC]), ALU.add)
                dve.drain()
                v.tensor_reduce(cm[:], cp[:, :, :, 0:NC], AX.X, ALU.max)
                dve.drain()
                flat = cp[:].rearrange("p t h n -> p (t h) n")[:, :, 0:NC]
                v.tensor_tensor(flat, flat, bc(cm[:].rearrange("p t h -> p (t h)").unsqueeze(2), NC), ALU.subtract).then_inc(cs_masked, 1)
                dve.wait_ge(cp_ready, 1)
                v.tensor_reduce(cs[:], cp[:, :, :, 0:NC], AX.X, ALU.add)
                dve.drain()
                v.reciprocal(cs[:], cs[:])
                dve.wait_ge(gates_ready, 1)
                v.tensor_tensor(cm[:], ng[:, :, 0:NQ], bc(e.k("cmp_any").unsqueeze(2), NQ), ALU.mult)
                dve.drain()
                v.tensor_tensor(cs[:], cs[:], cm[:], ALU.mult)
                dve.drain()
                v.tensor_tensor(flat, flat, bc(cs[:].rearrange("p t h -> p (t h)").unsqueeze(2), NC), ALU.mult).then_inc(cp_scaled, 1)
                for i in range(TT * N_KV):
                    t, kv = i // N_KV, i % N_KV
                    dve.wait_ge(cp_turned, i + 1)
                    if i >= 2:
                        dve.wait_ge(co_ready, i - 1)
                    v.tensor_copy(cpT[:, i % 2], e.bank[2 + i % 2][:, 0:P]).then_inc(cp_out, 1)
                    if i >= 1:
                        take(dve, v, i - 1)
                take(dve, v, TT * N_KV - 1)

                with dve.Fori(0, GROUP) as g:
                    def mask_max(j):
                        for t in range(TT):
                            n = (t + 1) * P
                            dve.wait_ge(prob_ready, g * 16 + j * 4 + t + 1)
                            dve.wait_ge(score_ready, g * 16 + j * 4 + t + 1)
                            dve.sem_inc(tile_taken, 1)
                            v.tensor_tensor_reduce(sm[:, j % 2, t, 0:n], e.bank[t][:, 0:n], causal[:, SEQ - n:], 1.0, -3.0e38,
                                                   ALU.add, ALU.max, mx[:, j % 2, t:t + 1]).then_inc(masked, 1)
                        dve.drain()
                        v.tensor_scalar(nm[:, j % 2], mx[:, j % 2], -SCALE, None, ALU.mult).then_inc(max_ready, 1)

                    def finish(j):
                        kv, br = j // 2, j % 2
                        for t in range(3):
                            dve.wait_ge(turned, g * 16 + j * 4 + t + 1 + 8)
                            dve.wait_ge(pv_ready, g * 16 + j * 4 + 3 + t)
                            v.tensor_copy(pt[:, t % 2, 0:(t + 1) * P], e.bank[4 + t % 2][:, 0:(t + 1) * P]).then_inc(t_out_v, 1)
                        dve.wait_ge(prob_ready, g * 16 + j * 4 + 4 + 8)
                        v.reciprocal(cf[:], rsum[:, j % 2])
                        dve.drain()
                        gate = ng[:, :, bass.ds((br + 1) * NQ + kv * GROUP + g, 1)].rearrange("p t a -> p (t a)")
                        v.tensor_tensor(cf[:], cf[:], gate, ALU.mult)
                        dve.drain()
                        dve.wait_ge(pv_ready, g * 16 + j * 4 + 4 + 4)
                        v.tensor_tensor(om[:], e.bank[6 + j % 2][:, 0:TT * HD].rearrange("p (t d) -> p t d", t=TT), bc(cf[:].unsqueeze(2), HD), ALU.mult)
                        dve.drain()
                        yh = e.y[:, :, bass.ds((kv * GROUP + g) * HD + Y0, HD)]
                        v.tensor_tensor(yh, yh, om[:], ALU.add).then_inc(combined, 1)

                    mask_max(0)
                    for j in range(1, 4):
                        mask_max(j)
                        finish(j - 1)
                    finish(3)
                    dve.drain()


def at4(t, i):
    return t[:, bass.ds(i, 1)].rearrange("p a b c -> p (a b) c")


def store_stage(nc, e, out):
    with Stage(nc) as st:
        stored, = st.sems("stored")
        with nc.Block() as block:
            @block.sync
            def _(sp):
                sp.dma_start(out, e.x[:].rearrange("p k n -> p (k n)")).then_inc(stored, 16)
                sp.wait_ge(stored, 16)


def decoder_kernel(nc, x_t, c_t, const, ada_w, ada_b, norm_w, w_up, w_down, w_tok, w_conv, conv_w, w_out,
                   m_gate_b, head_norm_w, g_decay, qk_norm, cmp_pos, cmp_w1, cmp_w2, out):
    with ExitStack() as ctx:
        def sb(name, shape):
            return ctx.enter_context(nc.sbuf_tensor(name, shape, F32))

        e = Env()
        e.x = sb("x", [P, KT, SEQ])
        e.h = sb("h", [P, KT, SEQ])
        e.y = e.h[:].rearrange("p k n -> p (k n)").rearrange("p (t n) -> p t n", t=TT)
        e.base = sb("const_base", [P, BASE_W])

        def const_part(name):
            start, width = CONST_AT[name]
            return e.base[:, start:start + width] if start < BASE_W else e.const[:, start - BASE_W:start - BASE_W + width]

        e.k = const_part
        e.c, e.csil = sb("c", [P, KT]), sb("c_silu", [P, KT])
        e.mod, e.coef, e.gate = sb("mod", [P, 9 * KT]), sb("coef", [P, 3, KT]), sb("gate", [P, 3, KT])
        e.mod_b, e.nw = sb("mod_bias", [P, 9 * KT]), sb("norm_w_sb", [P, 3 * KT])
        e.eps = sb("eps", [P, 1])
        e.bank = [ctx.enter_context(nc.psum_tensor(f"bank{i}", [P, 512], F32)) for i in range(8)]
        load_stage(nc, e, x_t, c_t, const)
        with nc.Fori(0, DEPTH) as L:
            ada_stage(nc, e, L, ada_w, ada_b, norm_w)
            ffn_stage(nc, e, L, 0, w_up, w_down, ada_w)
            with ExitStack() as mix:
                e.proj = mix.enter_context(nc.sbuf_tensor("proj", [P, TT, TOK_W], F32))
                e.const = mix.enter_context(nc.sbuf_tensor("const_sb", [P, CONST_W - BASE_W], F32))
                e.conv = mix.enter_context(nc.sbuf_tensor("conv", [P, N_CONV, SEQ], F32))
                proj_stage(nc, e, L, const, w_tok, w_conv, conv_w)
                mlstm_stage(nc, e, L, m_gate_b, head_norm_w)
                delta_stage(nc, e, L, g_decay, head_norm_w)
                nsa_stage(nc, e, L, qk_norm, cmp_pos, cmp_w1, cmp_w2)
            out_stage(nc, e, L, w_out)
            ffn_stage(nc, e, L, 1, w_up, w_down, ada_w)
        store_stage(nc, e, out)


def laid_out(a):
    def kpn(w, n):
        *lead, K, N = w.shape
        v = w.reshape(*lead, K // P, P, N // n, n)
        d = len(lead)
        return v.transpose(*range(d), d + 2, d + 1, d, d + 3).reshape(*lead, N // n, P, K // P * n)

    def cols(v):
        *lead, K = v.shape
        return np.moveaxis(v.reshape(*lead, K // P, P), -1, -2)

    o = {}
    o["x_t"] = a["x"][0].T.reshape(KT, P, SEQ).transpose(1, 0, 2).reshape(P, -1)
    o["c_t"] = cols(a["c"][0])
    o["const"] = constants()
    o["ada_w"] = kpn(a["ada_w"], P)
    o["ada_b"] = cols(a["ada_b"])
    o["norm_w"] = cols(a["norm_w"].reshape(DEPTH, 3 * D_MODEL))
    up = a["ffn_w_up"].reshape(2 * DEPTH, KT, P, 2, FT, P)
    o["w_up"] = up.transpose(0, 4, 3, 2, 1, 5).reshape(2 * DEPTH, 2 * FT, P, -1)
    down = a["ffn_w_down"].reshape(2 * DEPTH, 2, FT // 2, P, KT, P)
    o["w_down"] = down.transpose(0, 4, 1, 3, 2, 5).reshape(2 * DEPTH, 2 * KT, P, -1)
    w = a["w_in"]
    m_in, g_w = 4 * M_W + 2 * M_HEADS, G_HEADS * HD
    conv_cols = w[:, :, m_in:m_in + 3 * g_w]
    tok_cols = np.concatenate([w[:, :, :m_in], w[:, :, m_in + 3 * g_w:]], 2)
    o["w_tok"] = kpn(tok_cols, PG)
    o["w_conv"] = kpn(conv_cols, P)
    o["conv_w"] = a["gdn_conv_w"].transpose(0, 2, 1).reshape(DEPTH, N_CONV, P, CONV_K).transpose(0, 2, 1, 3).reshape(DEPTH, P, -1)
    o["w_out"] = kpn(a["w_out"], P)
    o["m_gate_b"] = a["mlstm_gate_b"].reshape(DEPTH, 1, -1)
    o["head_norm_w"] = np.stack([a["mlstm_norm_w"], a["gdn_norm_w"]], 1).reshape(DEPTH, 1, -1)
    o["g_decay"] = np.concatenate([a["gdn_a_log"], a["gdn_dt_bias"]], 1).reshape(DEPTH, 1, -1)
    o["qk_norm"] = a["nsa_qk_norm"].reshape(DEPTH, 1, -1)
    pos = a["nsa_cmp_pos"].reshape(DEPTH, 2, CMP_BLOCK // 2, P)
    o["cmp_pos"] = pos.transpose(0, 3, 1, 2).reshape(DEPTH, P, -1)
    w1 = a["nsa_cmp_w1"].reshape(DEPTH, 2, CMP_BLOCK // 2, P, CMP_HIDDEN)
    o["cmp_w1"] = w1.transpose(0, 3, 1, 2, 4).reshape(DEPTH, P, -1)
    o["cmp_w2"] = a["nsa_cmp_w2"].reshape(DEPTH, 2, CMP_HIDDEN // P, P, HD).transpose(0, 3, 1, 2, 4).reshape(DEPTH, P, -1)
    return {k: np.ascontiguousarray(v) for k, v in o.items()}


def kernel(**inputs):
    import concourse.bacc as bacc
    from concourse.bass_utils import run_bass_kernel_spmd

    arrays = laid_out({k: np.asarray(v) for k, v in inputs.items()})
    nc = bacc.Bacc("TRN2", target_bir_lowering=False, num_devices=1)
    args = [nc.dram_tensor(f"in_{k}", v.shape, F32, kind="ExternalInput").ap() for k, v in arrays.items()]
    out = nc.dram_tensor("out_x", (P, KT * SEQ), F32, kind="ExternalOutput").ap()
    decoder_kernel(nc, *args, out)
    got = run_bass_kernel_spmd(nc, [{f"in_{k}": v for k, v in arrays.items()}], core_ids=[0]).results[0]["out_x"]
    return np.ascontiguousarray(got.reshape(P, KT, SEQ).transpose(1, 0, 2).reshape(D_MODEL, SEQ).T)[None]
```

```python
from contextlib import ExitStack

import numpy as np

import concourse.bass as bass
import concourse.mybir as mybir
from concourse.alu_op_type import AluOpType as ALU

F32 = mybir.dt.float32
F32R = mybir.dt.float32r
ACT = mybir.ActivationFunctionType
AX = mybir.AxisListType

P = 128
D_MODEL, SEQ, DEPTH = 1024, 512, 2
D_FF = 2816
HD = 64
KT = D_MODEL // P
TT = SEQ // P
FT = D_FF // P
EPS = 1e-6
NEG = -1e30

M_HEADS, G_HEADS, N_HEADS, N_KV = 4, 4, 8, 2
GROUP = N_HEADS // N_KV
CMP_BLOCK, CMP_STRIDE, CMP_HIDDEN = 32, 16, 256
N_CMP = (SEQ - CMP_BLOCK) // CMP_STRIDE + 1
SCALE = HD ** -0.5

M_W, KV_W = M_HEADS * HD, N_KV * HD
C_MQ, C_MK, C_MV, C_MO = 0, M_W, 2 * M_W, 3 * M_W
C_Z = 4 * M_W
C_Q = C_Z + G_HEADS * HD
C_KC = C_Q + N_HEADS * HD
C_VC = C_KC + KV_W
C_KS = C_VC + KV_W
C_VS = C_KS + KV_W
C_KWN = C_VS + KV_W
C_VWN = C_KWN + KV_W
C_MG = C_VWN + KV_W
C_GA = C_MG + 2 * M_HEADS
C_GB = C_GA + G_HEADS
C_NG = C_GB + G_HEADS
TOK_W = C_NG + 3 * N_HEADS
GATE_W = TOK_W - C_MG
PG = 512
N_PG = C_MG // PG
KH = KT // 2
N_CONV = 3 * G_HEADS * HD // P
CONV_K = 4
ROPED = N_HEADS + 2 * N_KV
FIRST_SEM = 110
LEVELS = 6

ADA_SLOTS = 4
ADA_HEAD = 2 * KT
ADA_UP, ADA_DOWN = 4, 3

CONST_PARTS = [("ident", P), ("ones", P), ("upper", P), ("decay_sel", 2 * P), ("ident2", 2 * P),
               ("causal", SEQ), ("causal_t", P), ("level0", P), ("levels", LEVELS * P),
               ("cos", TT * HD), ("sin", TT * HD), ("cmp_cos", HD), ("cmp_sin", HD),
               ("cmp_mask", TT * N_CMP), ("cmp_any", TT)]
BASE_W = 2 * P
CONST_AT, CONST_W = {}, 0
for _n, _w in CONST_PARTS:
    CONST_AT[_n] = (CONST_W, _w)
    CONST_W += _w


def constants():
    p, f = np.arange(P)[:, None], np.arange(P)[None, :]
    c = {}
    c["ident"] = (p == f)
    c["ones"] = np.ones((P, P))
    c["upper"] = (p <= f)
    c["decay_sel"] = np.concatenate([(p > f), -1.0 * (p <= f)], 1)
    c["ident2"] = np.concatenate([(p == f), (p == f)], 1)
    c["causal"] = np.concatenate([np.zeros((P, SEQ - P)), np.where(f <= p, 0.0, NEG)], 1)
    c["causal_t"] = np.where(p <= f, 0.0, NEG)

    def level(s):
        return (p // (2 * s) == f // (2 * s)) & (p % (2 * s) < s) & (f % (2 * s) >= s)

    c["level0"] = level(1)
    c["levels"] = np.concatenate([level(2 << n) for n in range(LEVELS)], 1)
    half = HD // 2
    inv = np.power(10000.0, -np.arange(half) / half).astype(np.float32)

    def tables(pos):
        ang = pos.astype(np.float32)[:, None] * inv[None, :]
        cos, sin = np.cos(ang).astype(np.float32), np.sin(ang).astype(np.float32)
        return np.concatenate([cos, cos], 1), np.concatenate([-sin, sin], 1)

    cos, sin = tables(np.arange(SEQ))
    c["cos"] = cos.reshape(TT, P, HD).transpose(1, 0, 2).reshape(P, -1)
    c["sin"] = sin.reshape(TT, P, HD).transpose(1, 0, 2).reshape(P, -1)
    end = np.arange(N_CMP) * CMP_STRIDE + CMP_BLOCK - 1
    cc, cs = tables(end)
    pad = np.zeros((P - N_CMP, HD))
    c["cmp_cos"], c["cmp_sin"] = np.concatenate([cc, pad]), np.concatenate([cs, pad])
    t = (np.arange(TT)[None, :, None] * P + np.arange(P)[:, None, None])
    valid = end[None, None, :] <= t
    c["cmp_mask"] = np.where(valid, 0.0, NEG).reshape(P, -1)
    c["cmp_any"] = valid.any(-1)
    return np.ascontiguousarray(np.concatenate([np.asarray(c[n], np.float32) for n, _ in CONST_PARTS], 1))


class Env:
    pass


def at(t, i):
    dims = " ".join("xyz"[:len(t.shape) - 2])
    return t[:, bass.ds(i, 1)].rearrange(f"p a {dims} -> p (a {dims.split()[0]}) {' '.join(dims.split()[1:])}")


def dram(t, *idx):
    n = len(idx)
    v = t[tuple(bass.ds(i, 1) for i in idx)]
    lead = " ".join("abc"[:n])
    return v.rearrange(f"{lead} p n -> ({lead} p) n")


class Stage:

    def __init__(self, nc):
        self.nc, self.ctx, self.nums = nc, ExitStack(), []

    def __enter__(self):
        self.ctx.__enter__()
        return self

    def sem(self, name):
        s = self.ctx.enter_context(self.nc.semaphore(name, num=FIRST_SEM + len(self.nums)))
        self.nums.append(s.num)
        return s

    def sems(self, names):
        return [self.sem(n) for n in names.split()]

    def sb(self, name, shape, dtype=F32):
        return self.ctx.enter_context(self.nc.sbuf_tensor(name, shape, dtype))

    def __exit__(self, *a):
        if a[0] is None:
            self.nc.all_engine_barrier(sems_to_clear=range(min(self.nums), max(self.nums) + 1))
        return self.ctx.__exit__(*a)


def load_stage(nc, e, x_t, c_t, const):
    with Stage(nc) as st:
        loaded, = st.sems("loaded")
        with nc.Block() as block:
            @block.sync
            def _(sp):
                sp.dma_start(e.x[:], x_t).then_inc(loaded, 16)
                sp.dma_start(e.base[:], const[:, 0:BASE_W]).then_inc(loaded, 16)
                sp.dma_start(e.c[:], c_t).then_inc(loaded, 16)
                sp.wait_ge(loaded, 48)

            @block.vector
            def _(dve):
                nc.vector.memset(e.eps[:], EPS)


def mod_tile(nc, dve, acc, w, csil):
    nc.vector.tensor_scalar(acc, w[:, 0], csil[:, 0:1], None, ALU.mult)
    for k in range(1, KT):
        dve.drain()
        last = nc.vector.scalar_tensor_tensor(acc, w[:, k], csil[:, k:k + 1], acc, ALU.mult, ALU.add)
    return last


def ada_stage(nc, e, L, ada_w, ada_b, norm_w):
    with Stage(nc) as st:
        N, G = ADA_HEAD, 4
        small, c_ready, acc_ready, sums_ready = st.sems("ada_small c_ready ada_acc_ready ada_sums_ready")
        loaded = [st.sem(f"ada_loaded{b}") for b in range(N // G)]
        w = st.sb("ada_w_sb", [P, N, KT, P])
        acc = st.sb("ada_acc", [P, N, P])
        with nc.Block() as block:
            @block.sync
            def _(sp):
                for n in range(0, N, 2):
                    sp.dma_start(w[:, n:n + 2].rearrange("p t k n -> p t (k n)"),
                                 ada_w[bass.ds(L, 1), n:n + 2].rearrange("a t p n -> p (a t) n")).then_inc(loaded[n // G], 16)
                sp.dma_start(e.mod_b[:], dram(ada_b, L)).then_inc(small, 16)
                sp.dma_start(e.nw[:], dram(norm_w, L)).then_inc(small, 16)

            @block.scalar
            def _(act):
                nc.scalar.activation(e.csil[:], e.c[:], ACT.Silu).then_inc(c_ready, 1)

            @block.vector
            def _(dve):
                dve.wait_ge(c_ready, 1)
                for b in range(N // G):
                    dve.wait_ge(loaded[b], G // 2 * 16)
                    tiles = slice(b * G, (b + 1) * G)
                    mod_tile(nc, dve, acc[:, tiles], w[:, tiles].rearrange("p n k m -> p k n m"), e.csil).then_inc(acc_ready, 1)
                dve.wait_ge(small, 32)
                dve.wait_ge(sums_ready, 1)
                nc.vector.tensor_tensor(e.mod[:, 0:N], e.bank[0][:, 0:N], e.mod_b[:, 0:N], ALU.add)
                dve.drain()
                nc.vector.scalar_tensor_tensor(e.coef[:, 0], e.mod[:, KT:2 * KT], 1.0, e.nw[:, 0:KT], ALU.add, ALU.mult)

            @block.tensor
            def _(pe):
                for n in range(N):
                    pe.wait_ge(acc_ready, n // G + 1)
                    last = nc.tensor.matmul(e.bank[0][:, n:n + 1], acc[:, n], e.k("ones")[:, 0:1], start=True, stop=True)
                last.then_inc(sums_ready, 1)


class SplitNorm:

    ACT_SQUARES = 6

    def __init__(self, nc, e, st, sub, tag, diag):
        self.nc, self.e, self.sub = nc, e, sub
        (self.squared, self.pair_sum, self.total, self.summed, self.rooted, self.diag_ready, self.rstd_ready, self.scaled,
         self.high, self.full, self.ready) = st.sems(" ".join(f"{n}{tag}" for n in (
             "squared pair_sum total_ready sumsq_ready root_ready diag_ready rstd_ready scaled h_hi_ready h_full_ready h_ready").split()))
        self.root, self.diag = st.sb("root" + tag, [P, TT]), diag
        self.hi = st.sb("h_hi" + tag, [P, KT, SEQ], F32R)
        self.lo = st.sb("h_lo" + tag, [P, KT, SEQ], F32R)

    def affine(self, k):
        return self.e.coef[:, self.sub, k:k + 1], self.e.mod[:, 3 * self.sub * KT + k:3 * self.sub * KT + k + 1]

    def scalar(self, act, meanwhile):
        nc, e = self.nc, self.e
        for k in range(self.ACT_SQUARES):
            nc.scalar.activation(e.h[:, k], e.x[:, k], ACT.Square).then_inc(self.squared, 1)
        meanwhile()
        act.wait_ge(self.summed, 1)
        nc.scalar.activation(self.root[:], e.bank[6][:, 0:TT], ACT.Sqrt, bias=e.eps[:, 0:1], scale=1.0 / D_MODEL).then_inc(self.rooted, 1)
        for k in range(KT):
            act.wait_ge(self.scaled, k + 1)
            coef, shift = self.affine(k)
            nc.scalar.activation(self.hi[:, k], e.h[:, k], ACT.Identity, scale=coef, bias=shift).then_inc(self.high, 1)

    def gpsimd(self, pool):
        nc, h = self.nc, self.e.h
        last = self.ACT_SQUARES - 1
        pool.wait_ge(self.squared, last + 1)
        nc.gpsimd.tensor_tensor(h[:, last], h[:, last - 1], h[:, last], ALU.add).then_inc(self.pair_sum, 1)
        for k in range(KT):
            pool.wait_ge(self.high, k + 1)
            coef, shift = self.affine(k)
            nc.gpsimd.tensor_scalar(h[:, k], h[:, k], coef, shift, ALU.mult, ALU.add).then_inc(self.full, 1)

    def tensor(self, pe):
        nc, e = self.nc, self.e
        pe.wait_ge(self.total, 1)
        for t in range(TT):
            last = nc.tensor.matmul(e.bank[6][:, t:t + 1], e.h[:, KT - 1, t * P:(t + 1) * P], e.k("ones")[:, 0:1], start=True, stop=True)
        last.then_inc(self.summed, 1)
        pe.wait_ge(self.diag_ready, 1)
        nc.tensor.matmul(e.bank[7][:], e.k("ones"), self.diag, start=True, stop=True).then_inc(self.rstd_ready, 1)

    def vector(self, dve, meanwhile):
        nc, e = self.nc, self.e
        v, h = nc.vector, e.h
        for k in range(self.ACT_SQUARES, KT):
            v.tensor_tensor(h[:, k], e.x[:, k], e.x[:, k], ALU.mult)
        pair = self.ACT_SQUARES - 1
        for k in [*range(self.ACT_SQUARES, KT - 1), *range(pair - 1), pair]:
            if k < pair:
                dve.wait_ge(self.squared, k + 1)
            if k == pair:
                dve.wait_ge(self.pair_sum, 1)
            dve.drain()
            last = v.tensor_tensor(h[:, KT - 1], h[:, KT - 1], h[:, k], ALU.add)
        last.then_inc(self.total, 1)
        meanwhile()
        dve.wait_ge(self.rooted, 1)
        v.reciprocal(self.root[:], self.root[:])
        dve.drain()
        v.tensor_tensor(self.diag.rearrange("p (t n) -> p t n", t=TT), e.k("ident").unsqueeze(1).broadcast_to([P, TT, P]),
                        self.root[:].unsqueeze(2).broadcast_to([P, TT, P]), ALU.mult).then_inc(self.diag_ready, 1)
        dve.wait_ge(self.rstd_ready, 1)
        for k in range(KT + 2):
            if k < KT:
                v.tensor_tensor(h[:, k], e.x[:, k], e.bank[7][:], ALU.mult).then_inc(self.scaled, 1)
            if k >= 2:
                dve.wait_ge(self.full, k - 1)
                v.tensor_tensor(self.lo[:, k - 2], h[:, k - 2], self.hi[:, k - 2].bitcast(F32), ALU.subtract).then_inc(self.ready, 1)


def product(nc, out, w_hi, w_lo, x_hi, x_lo, first, last):
    nc.tensor.matmul(out, w_hi, x_hi, start=first, stop=False)
    nc.tensor.matmul(out, w_hi, x_lo, start=False, stop=False)
    return nc.tensor.matmul(out, w_lo, x_hi, start=False, stop=last)


def ffn_stage(nc, e, L, which, w_up, w_down, ada_w):
    sub, tag = 2 * which, f"_f{which}"
    names = lambda text: " ".join(n + tag for n in text.split())
    FH = FT // 2
    ada = which == 0
    UP, DOWN = FT // 2, KT // 2
    MOD_REST = 9 * KT - ADA_HEAD
    assert UP * ADA_UP + DOWN * ADA_DOWN == MOD_REST
    with Stage(nc) as st:
        raw_loaded = [st.sem(f"raw_loaded{b}{tag}") for b in range(2)]
        (high_ready, split_ready, gate_ready, up_ready, silu_ready, product_ready, hidden_high, hidden_ready,
         down_high, down_split, half_ready, down_ready) = st.sems(
            names("high_ready split_ready gate_ready up_ready silu_ready product_ready hidden_high hidden_ready "
                  "down_high down_split half_ready down_ready"))
        down_free = st.sem("down_free" + tag)
        if ada:
            mod_loaded = [st.sem(f"mod_loaded{b}") for b in range(ADA_SLOTS)]
            mod_acc, mod_sums = st.sems("mod_acc mod_sums")
            acc = st.sb("mod_acc_sb", [P, ADA_SLOTS, P])
        sg = st.sb("silu_sb" + tag, [P, 2, SEQ])
        norm = SplitNorm(nc, e, st, sub, tag, sg[:, 0])
        prod = st.sb("product_sb" + tag, [P, 2, SEQ])
        hid_hi = st.sb("hidden_hi" + tag, [P, FT, SEQ], F32R)
        hid_lo = st.sb("hidden_lo" + tag, [P, FT, SEQ], F32R)
        raw = st.sb("w_raw" + tag, [P, 2, FH * P])
        parts = st.sb("w_parts" + tag, [P, 4 * 2 * KT * P], F32R)
        up = parts[:].rearrange("p (b s h n) -> p b s h n", b=2, s=2, h=2)
        down = parts[:, 0:4 * FH * P].rearrange("p (b h n) -> p b h n", b=2, h=2)
        aw = e.h[:].rearrange("p k n -> p (k n)").rearrange("p (b k m) -> p b k m", b=ADA_SLOTS, k=KT)
        with nc.Block() as block:
            @block.sync
            def _(sp):
                def load_up(n, b):
                    sp.dma_start(raw[:, b, 0:KT * P], dram(w_up, L * 2 + which, n)).then_inc(raw_loaded[b], 16)

                def load_down(n, b):
                    sp.dma_start(raw[:, b], dram(w_down, L * 2 + which, n)).then_inc(raw_loaded[b], 16)

                def load_mod(n, b):
                    sp.dma_start(aw[:, b].rearrange("p k m -> p (k m)"), dram(ada_w, L, n + ADA_HEAD)).then_inc(mod_loaded[b], 16)

                for q in range(2):
                    load_up(q, q)
                for q in range(2):
                    sp.wait_ge(split_ready, q + 1)
                    load_up(2 + q, q)
                if ada:
                    sp.wait_ge(norm.ready, KT)
                    for b in range(ADA_SLOTS):
                        load_mod(b, b)
                with sp.Fori(1, UP) as i:
                    for q in range(4):
                        sp.wait_ge(split_ready, i * 4 + q - 1)
                        load_up(i * 4 + q, q % 2)
                        if ada:
                            sp.wait_ge(mod_acc, (i - 1) * ADA_UP + q + 1)
                            load_mod(i * ADA_UP + q, q)
                for q in range(2):
                    sp.wait_ge(split_ready, 4 * UP - 1 + q)
                    load_down(q, q)
                for q in range(2):
                    sp.wait_ge(down_split, q + 1)
                    load_down(2 + q, q)
                if ada:
                    for q in range(ADA_DOWN):
                        sp.wait_ge(mod_acc, UP * ADA_UP - ADA_UP + q + 1)
                        load_mod(UP * ADA_UP + q, q)
                with sp.Fori(1, DOWN) as i:
                    for q in range(4):
                        sp.wait_ge(down_split, i * 4 + q - 1)
                        load_down(i * 4 + q, q % 2)
                        if ada and q < ADA_DOWN:
                            sp.wait_ge(mod_acc, UP * ADA_UP + (i - 1) * ADA_DOWN + q + 1)
                            load_mod(UP * ADA_UP + i * ADA_DOWN + q, q)

            @block.gpsimd
            def _(pool):
                norm.gpsimd(pool)

            @block.tensor
            def _(pe):
                def mod_sum(bank, col, n, s):
                    pe.wait_ge(mod_acc, n + 1)
                    nc.tensor.matmul(bank[:, bass.ds(col, 1)], acc[:, s], e.k("ones")[:, 0:1],
                                     start=True, stop=True).then_inc(mod_sums, 1)

                pe.sem_inc(gate_ready, 2)
                pe.sem_inc(up_ready, 2)
                pe.sem_inc(half_ready, 1)
                pe.sem_inc(down_ready, 1)
                if ada:
                    pe.sem_inc(mod_sums, ADA_SLOTS)
                norm.tensor(pe)
                with pe.Fori(0, UP) as i:
                    for b in range(2):
                        n = i * 2 + b
                        pe.wait_ge(product_ready, n + 1)
                        for side, done in ((0, gate_ready), (1, up_ready)):
                            pe.wait_ge(split_ready, n * 2 + side + 1)
                            for k in range(KT):
                                if b == 0 and side == 0:
                                    pe.wait_ge(norm.ready, k + 1)
                                ks = slice(k * P, (k + 1) * P)
                                last = product(nc, e.bank[2 * b + side][:], up[:, b, side, 0, ks], up[:, b, side, 1, ks],
                                               norm.hi[:, k], norm.lo[:, k], k == 0, k == KT - 1)
                            last.then_inc(done, 1)
                        if ada:
                            for q in (2 * b, 2 * b + 1):
                                mod_sum(e.bank[6], i * ADA_UP + q, i * ADA_UP + q, q)
                with pe.Fori(0, DOWN) as i:
                    for b in range(2):
                        m = i * 2 + b
                        pe.wait_ge(down_free, m + 1)
                        for half in range(2):
                            pe.wait_ge(down_split, m * 2 + half + 1)
                            pe.wait_ge(hidden_ready, (half + 1) * FH)
                            for f in range(FH):
                                fs, ff = slice(f * P, (f + 1) * P), half * FH + f
                                last = product(nc, e.bank[4 + b][:], down[:, half, 0, fs], down[:, half, 1, fs],
                                               hid_hi[:, ff], hid_lo[:, ff], ff == 0, ff == FT - 1)
                            last.then_inc(down_ready if half else half_ready, 1)
                    if ada:
                        for q in range(ADA_DOWN):
                            mod_sum(e.bank[7], i * ADA_DOWN + q, i * ADA_DOWN + q + UP * ADA_UP, q)

            @block.scalar
            def _(act):
                def round_up(n, b):
                    for side, used in ((0, gate_ready), (1, up_ready)):
                        act.wait_ge(raw_loaded[side], n * 16 + 16)
                        act.wait_ge(used, n + 1)
                        nc.scalar.activation(up[:, b, side, 0], raw[:, side, 0:KT * P], ACT.Copy).then_inc(high_ready, 1)

                def silu(n, b, hi):
                    act.wait_ge(gate_ready, n + 1 + 2)
                    act.wait_ge(product_ready, n + 1)
                    nc.scalar.activation(sg[:, b], e.bank[2 * b][:], ACT.Silu).then_inc(silu_ready, 1)
                    act.wait_ge(product_ready, n + 1 + 2)
                    nc.scalar.activation(hi, prod[:, b], ACT.Copy).then_inc(hidden_high, 1)

                def round_down(n, half, m):
                    act.wait_ge(raw_loaded[half], (m + FT + 1) * 16)
                    act.wait_ge(down_ready if half else half_ready, m + 1)
                    nc.scalar.activation(down[:, half, 0], raw[:, half], ACT.Copy).then_inc(down_high, 1)

                act.sem_inc(hidden_high, 2)
                norm.scalar(act, lambda: round_up(0, 0))
                with act.Fori(0, UP - 1) as i:
                    round_up(i * 2 + 1, 1)
                    silu(i * 2, 0, at(hid_hi, i * 2))
                    round_up(i * 2 + 2, 0)
                    silu(i * 2 + 1, 1, at(hid_hi, i * 2 + 1))
                round_up(FT - 1, 1)
                for b in range(2):
                    silu(FT - 2 + b, b, hid_hi[:, FT - 2 + b])
                act.wait_ge(up_ready, FT + 2)
                with act.Fori(0, KT) as m:
                    for half in range(2):
                        round_down(m * 2 + half, half, m)

            @block.vector
            def _(dve):
                dve.sem_inc(product_ready, 2)
                dve.sem_inc(down_free, 2)
                v = nc.vector

                def split_up(n, b):
                    for side in range(2):
                        dve.wait_ge(high_ready, n * 2 + side + 1)
                        v.tensor_tensor(up[:, b, side, 1], raw[:, side, 0:KT * P], up[:, b, side, 0].bitcast(F32), ALU.subtract).then_inc(split_ready, 1)

                def hidden(n, b, hi, lo):
                    dve.wait_ge(up_ready, n + 1 + 2)
                    dve.wait_ge(silu_ready, n + 1)
                    dve.wait_ge(hidden_high, n + 1)
                    v.tensor_tensor(prod[:, b], e.bank[2 * b + 1][:], sg[:, b], ALU.mult).then_inc(product_ready, 1)
                    dve.wait_ge(hidden_high, n + 1 + 2)
                    v.tensor_tensor(lo, prod[:, b], hi.bitcast(F32), ALU.subtract).then_inc(hidden_ready, 1)

                def mod(n, s, turn):
                    if ada:
                        dve.wait_ge(mod_loaded[s], turn * 16 + 16)
                        dve.wait_ge(mod_sums, n + 1)
                        mod_tile(nc, dve, acc[:, s], aw[:, s], e.csil).then_inc(mod_acc, 1)

                def split_down(n, half):
                    dve.wait_ge(down_high, n + 1)
                    v.tensor_tensor(down[:, half, 1], raw[:, half], down[:, half, 0].bitcast(F32), ALU.subtract).then_inc(down_split, 1)

                def add_to_x(m, b, xm, gate):
                    dve.wait_ge(down_ready, m + 1 + 1)
                    v.scalar_tensor_tensor(xm, e.bank[4 + b][:], gate, xm, ALU.mult, ALU.add).then_inc(down_free, 1)

                norm.vector(dve, lambda: split_up(0, 0))
                with dve.Fori(0, UP - 1) as i:
                    for b in range(2):
                        n = i * 2 + b
                        split_up(n + 1, 1 - b)
                        for q in (2 * b, 2 * b + 1):
                            mod(i * ADA_UP + q, q, i)
                        hidden(n, b, at(hid_hi, n), at(hid_lo, n))
                split_up(FT - 1, 1)
                for b in range(2):
                    for q in (2 * b, 2 * b + 1):
                        mod((UP - 1) * ADA_UP + q, q, UP - 1)
                    n = FT - 2 + b
                    hidden(n, b, hid_hi[:, n], hid_lo[:, n])
                if ada:
                    done = UP * ADA_UP
                    dve.wait_ge(mod_sums, done + ADA_SLOTS)
                    v.tensor_tensor(e.mod[:, ADA_HEAD:ADA_HEAD + done], e.bank[6][:, 0:done], e.mod_b[:, ADA_HEAD:ADA_HEAD + done], ALU.add)
                    dve.drain()
                    v.tensor_scalar(e.gate[:, 0], e.mod[:, 2 * KT:3 * KT], 0.5, None, ALU.mult)
                    dve.drain()
                for half in range(2):
                    split_down(half, half)
                with dve.Fori(0, DOWN - 1) as i:
                    for b in range(2):
                        m = i * 2 + b
                        split_down(m * 2 + 2, 0)
                        add_to_x(m, b, at(e.x, m), e.gate[:, sub, bass.ds(m, 1)])
                        if b:
                            mod(i * ADA_DOWN + 1 + UP * ADA_UP + 1, 1, i + UP)
                        split_down(m * 2 + 3, 1)
                        mod(i * ADA_DOWN + 2 * b + UP * ADA_UP + 1, 2 * b, i + UP)
                m = KT - 2
                split_down(m * 2 + 2, 0)
                add_to_x(m, 0, e.x[:, m], e.gate[:, sub, m:m + 1])
                split_down(m * 2 + 3, 1)
                for q in range(ADA_DOWN):
                    mod((DOWN - 1) * ADA_DOWN + q + UP * ADA_UP + 1, q, DOWN - 1 + UP)
                add_to_x(KT - 1, 1, e.x[:, KT - 1], e.gate[:, sub, KT - 1:KT])
                if ada:
                    done = UP * ADA_UP
                    dve.wait_ge(mod_sums, MOD_REST + ADA_SLOTS)
                    v.tensor_tensor(e.mod[:, ADA_HEAD + done:], e.bank[7][:, 0:MOD_REST - done], e.mod_b[:, ADA_HEAD + done:], ALU.add)
                    dve.drain()
                    for s in (1, 2):
                        vec = lambda j: e.mod[:, (3 * s + j) * KT:(3 * s + j + 1) * KT]
                        v.scalar_tensor_tensor(e.coef[:, s], vec(1), 1.0, e.nw[:, s * KT:(s + 1) * KT], ALU.add, ALU.mult)
                        v.tensor_scalar(e.gate[:, s], vec(2), 1.0 if s == 1 else 0.5, None, ALU.mult)


def proj_stage(nc, e, L, const, w_tok, w_gate, w_conv, conv_w):
    with Stage(nc) as st:
        tok_loaded = [st.sem(f"tok_loaded{b}") for b in range(2)]
        ch_loaded = [st.sem(f"ch_loaded{b}") for b in range(2)]
        (const_loaded, small, high_ready, split_ready, half_used, tok_ready, even_free, odd_free, gates_ready,
         ch_high, ch_split, ch_ready, padded, convolved, pad_zero) = st.sems(
            "const_loaded p_small p_high_ready p_split_ready half_used tok_ready even_free odd_free p_gates_ready "
            "ch_high ch_split ch_ready padded convolved pad_zero")
        pad = st.sb("conv_pad", [P, 2, SEQ + CONV_K - 1])
        norm = SplitNorm(nc, e, st, 1, "_p", st.sb("diag_p", [P, SEQ])[:])
        raw = st.sb("w_raw_p", [P, 2, KH * PG])
        parts = st.sb("w_parts_p", [P, 2, 2, KH * PG], F32R)
        wg = st.sb("w_gate_sb", [P, KT, GATE_W])
        taps = st.sb("taps", [P, N_CONV, CONV_K])
        CH = KT * P
        with nc.Block() as block:
            @block.sync
            def _(sp):
                def load_tok(g, half):
                    sp.dma_start(raw[:, half], dram(w_tok, L, g * 2 + half)).then_inc(tok_loaded[half], 16)

                def load_ch(n, b):
                    sp.dma_start(raw[:, b, 0:CH], dram(w_conv, L, n)).then_inc(ch_loaded[b], 16)

                for half in range(2):
                    load_tok(0, half)
                sp.dma_start(wg[:].rearrange("p k n -> p (k n)"), dram(w_gate, L)).then_inc(small, 16)
                sp.dma_start(taps[:].rearrange("p n k -> p (n k)"), dram(conv_w, L)).then_inc(small, 16)
                sp.dma_start(e.const[:], const[:, BASE_W:]).then_inc(const_loaded, 16)
                with sp.Fori(1, N_PG) as g:
                    for half in range(2):
                        sp.wait_ge(split_ready, g * 2 + half - 1)
                        load_tok(g, half)
                for b in range(2):
                    sp.wait_ge(split_ready, 2 * N_PG - 1 + b)
                    load_ch(b, b)
                with sp.Fori(1, N_CONV // 2) as i:
                    for b in range(2):
                        sp.wait_ge(ch_split, i * 2 + b - 1)
                        load_ch(i * 2 + b, b)
                sp.wait_ge(const_loaded, 16)

            @block.gpsimd
            def _(pool):
                norm.gpsimd(pool)

            @block.tensor
            def _(pe):
                norm.tensor(pe)
                with pe.Fori(0, N_PG) as g:
                    for half in range(2):
                        pe.wait_ge(norm.ready, (half + 1) * KH)
                        pe.wait_ge(split_ready, g * 2 + half + 1)
                        for t in range(TT):
                            if half == 0:
                                pe.wait_ge(odd_free if t % 2 else even_free, g * 2 + t // 2 + 1)
                            ts = slice(t * P, (t + 1) * P)
                            for k in range(KH):
                                kk, ks = half * KH + k, slice(k * PG, (k + 1) * PG)
                                last = product(nc, e.bank[t][:], norm.hi[:, kk, ts], norm.lo[:, kk, ts],
                                               parts[:, half, 0, ks], parts[:, half, 1, ks], kk == 0, kk == KT - 1)
                            if half:
                                last.then_inc(tok_ready, 1)
                        if half == 0:
                            last.then_inc(half_used, 1)
                pe.wait_ge(small, 32)
                for t in range(TT):
                    for k in range(KT):
                        last = nc.tensor.matmul(e.bank[6][:, t * GATE_W:(t + 1) * GATE_W], e.h[:, k, t * P:(t + 1) * P], wg[:, k],
                                                start=k == 0, stop=k == KT - 1)
                last.then_inc(gates_ready, 1)
                with pe.Fori(0, N_CONV // 2) as i:
                    for b in range(2):
                        pe.wait_ge(ch_split, i * 2 + b + 1)
                        pe.wait_ge(padded, i * 2 + b + 1)
                        for k in range(KT):
                            ks = slice(k * P, (k + 1) * P)
                            last = product(nc, e.bank[4 + b][:], parts[:, b, 0, ks], parts[:, b, 1, ks], norm.hi[:, k], norm.lo[:, k],
                                           k == 0, k == KT - 1)
                        last.then_inc(ch_ready, 1)

            @block.scalar
            def _(act):
                act.sem_inc(even_free, 2)
                act.sem_inc(padded, 2)
                def high(g, half):
                    act.wait_ge(tok_loaded[half], g * 16 + 16)
                    nc.scalar.activation(parts[:, half, 0], raw[:, half], ACT.Copy).then_inc(high_ready, 1)

                def high_ch(n, b, turn):
                    act.wait_ge(ch_loaded[b], turn * 16 + 16)
                    nc.scalar.activation(parts[:, b, 0, 0:CH], raw[:, b, 0:CH], ACT.Copy).then_inc(ch_high, 1)

                def take(g, t):
                    act.wait_ge(tok_ready, g * TT + t + 1)
                    nc.scalar.activation(e.proj[:, t, bass.ds(g * PG, PG)], e.bank[t][:], ACT.Copy).then_inc(even_free, 1)

                def channel(i, b):
                    n = i * 2 + b
                    act.wait_ge(ch_ready, n + 1)
                    act.wait_ge(convolved, n + 1)
                    nc.scalar.activation(pad[:, b, CONV_K - 1:], e.bank[4 + b][:], ACT.Copy).then_inc(padded, 1)

                norm.scalar(act, lambda: high(0, 0))
                high(0, 1)
                with act.Fori(0, N_PG - 1) as g:
                    act.wait_ge(half_used, g + 1)
                    high(g + 1, 0)
                    take(g, 0)
                    take(g, 2)
                    act.wait_ge(tok_ready, g * TT + TT)
                    high(g + 1, 1)
                act.wait_ge(half_used, N_PG)
                high_ch(0, 0, 0)
                take(N_PG - 1, 0)
                take(N_PG - 1, 2)
                act.wait_ge(tok_ready, N_PG * TT)
                high_ch(1, 1, 0)
                act.wait_ge(pad_zero, 1)
                with act.Fori(0, N_CONV // 2 - 1) as i:
                    for b in range(2):
                        channel(i, b)
                        high_ch(i * 2 + b + 2, b, i + 1)
                for b in range(2):
                    channel(N_CONV // 2 - 1, b)

            @block.vector
            def _(dve):
                v = nc.vector
                dve.sem_inc(odd_free, 2)
                dve.sem_inc(convolved, 2)
                v.memset(pad[:, :, 0:CONV_K - 1], 0.0).then_inc(pad_zero, 1)
                def low(g, half):
                    dve.wait_ge(high_ready, g * 2 + half + 1)
                    v.tensor_tensor(parts[:, half, 1], raw[:, half], parts[:, half, 0].bitcast(F32), ALU.subtract).then_inc(split_ready, 1)

                def low_ch(n, b):
                    dve.wait_ge(ch_high, n + 1)
                    v.tensor_tensor(parts[:, b, 1, 0:CH], raw[:, b, 0:CH], parts[:, b, 0, 0:CH].bitcast(F32), ALU.subtract).then_inc(ch_split, 1)

                def take(g, t):
                    dve.wait_ge(tok_ready, g * TT + t + 1)
                    v.tensor_copy(e.proj[:, t, bass.ds(g * PG, PG)], e.bank[t][:]).then_inc(odd_free, 1)

                def convolve(i, b):
                    n = i * 2 + b
                    dve.wait_ge(padded, n + 3)
                    tap, out = at(taps, n), at(e.conv, n)
                    v.tensor_scalar(out, pad[:, b, 0:SEQ], tap[:, 0:1], None, ALU.mult)
                    for j in range(1, CONV_K):
                        dve.drain()
                        last = v.scalar_tensor_tensor(out, pad[:, b, j:j + SEQ], tap[:, j:j + 1], out, ALU.mult, ALU.add)
                    last.then_inc(convolved, 1)

                norm.vector(dve, lambda: low(0, 0))
                low(0, 1)
                with dve.Fori(0, N_PG - 1) as g:
                    low(g + 1, 0)
                    take(g, 1)
                    take(g, 3)
                    low(g + 1, 1)
                low_ch(0, 0)
                take(N_PG - 1, 1)
                take(N_PG - 1, 3)
                low_ch(1, 1)
                dve.wait_ge(gates_ready, 1)
                v.tensor_copy(e.proj[:, :, C_MG:], e.bank[6][:, 0:TT * GATE_W].rearrange("p (t n) -> p t n", t=TT))
                with dve.Fori(0, N_CONV // 2 - 1) as i:
                    for b in range(2):
                        low_ch(i * 2 + b + 2, b)
                        convolve(i, b)
                for b in range(2):
                    convolve(N_CONV // 2 - 1, b)


def out_stage(nc, e, L, w_out):
    with Stage(nc) as st:
        w_loaded = [st.sem(f"wo_loaded{b}") for b in range(2)]
        turned, y_high, y_low, w_high, w_split, out_ready, out_free = st.sems("turned y_high y_low wo_high wo_split out_ready out_free")
        raw = st.sb("w_raw_o", [P, 2, KT * P])
        parts = st.sb("w_parts_o", [P, 2, 2, KT * P], F32R)
        y_hi = st.sb("y_hi", [P, KT, SEQ], F32R)
        y_lo = st.sb("y_lo", [P, KT, SEQ], F32R)
        with nc.Block() as block:
            @block.sync
            def _(sp):
                for b in range(2):
                    sp.dma_start(raw[:, b], dram(w_out, L, b)).then_inc(w_loaded[b], 16)
                with sp.Fori(1, KT // 2) as i:
                    for b in range(2):
                        sp.wait_ge(w_split, i * 2 + b - 1)
                        sp.dma_start(raw[:, b], dram(w_out, L, i * 2 + b)).then_inc(w_loaded[b], 16)

            @block.tensor
            def _(pe):
                for k in range(KT):
                    if k >= 4:
                        pe.wait_ge(y_low, k - 3)
                    for t in range(TT):
                        last = nc.tensor.transpose(e.bank[k % 4][:, t * P:(t + 1) * P], e.y[:, t, k * P:(k + 1) * P], e.k("ident"))
                    last.then_inc(turned, 1)
                pe.wait_ge(y_low, KT)
                with pe.Fori(0, KT // 2) as i:
                    for b in range(2):
                        pe.wait_ge(w_split, i * 2 + b + 1)
                        pe.wait_ge(out_free, i * 2 + b + 1)
                        for k in range(KT):
                            ks = slice(k * P, (k + 1) * P)
                            last = product(nc, e.bank[4 + b][:], parts[:, b, 0, ks], parts[:, b, 1, ks], y_hi[:, k], y_lo[:, k],
                                           k == 0, k == KT - 1)
                        last.then_inc(out_ready, 1)

            @block.scalar
            def _(act):
                def high(b, turn):
                    act.wait_ge(w_loaded[b], turn * 16 + 16)
                    nc.scalar.activation(parts[:, b, 0], raw[:, b], ACT.Copy).then_inc(w_high, 1)

                for k in range(KT):
                    act.wait_ge(turned, k + 1)
                    nc.scalar.activation(y_hi[:, k], e.bank[k % 4][:], ACT.Copy).then_inc(y_high, 1)
                    if k >= KT - 2:
                        high(k - (KT - 2), 0)
                with act.Fori(1, KT // 2) as i:
                    for b in range(2):
                        act.wait_ge(out_ready, i * 2 + b - 1)
                        high(b, i)

            @block.vector
            def _(dve):
                v = nc.vector

                def low(m, b):
                    dve.wait_ge(w_high, m + 1)
                    v.tensor_tensor(parts[:, b, 1], raw[:, b], parts[:, b, 0].bitcast(F32), ALU.subtract).then_inc(w_split, 1)

                def add_to_x(m, b):
                    dve.wait_ge(out_ready, m + 1)
                    xm = at(e.x, m)
                    v.scalar_tensor_tensor(xm, e.bank[4 + b][:], e.gate[:, 1, bass.ds(m, 1)], xm, ALU.mult, ALU.add).then_inc(out_free, 1)

                dve.sem_inc(out_free, 2)
                for k in range(KT):
                    dve.wait_ge(y_high, k + 1)
                    v.tensor_tensor(y_lo[:, k], e.bank[k % 4][:], y_hi[:, k].bitcast(F32), ALU.subtract).then_inc(y_low, 1)
                    if k >= KT - 2:
                        low(k - (KT - 2), k - (KT - 2))
                with dve.Fori(0, KT // 2 - 1) as i:
                    for b in range(2):
                        low(i * 2 + b + 2, b)
                        add_to_x(i * 2 + b, b)
                for b in range(2):
                    add_to_x(KT - 2 + b, b)


def bc(ap, n):
    return ap.broadcast_to(list(ap.shape[:-1]) + [n])


def attention_rows(t, w):
    for h0, n, c0 in ((0, N_HEADS, C_Q), (N_HEADS, N_KV, C_KS), (N_HEADS + N_KV, N_KV, C_KWN)):
        yield h0, n, w(t, c0, n)


def all_tiles(proj, c0, n):
    return proj[:, :, c0:c0 + n * HD].rearrange("p t (h d) -> p t h d", h=n)


def one_tile(t):
    return lambda proj, c0, n: proj[:, bass.ds(t, 1), c0:c0 + n * HD].rearrange("p a (h d) -> p (a h) d", h=n)


def mlstm_stage(nc, e, L, gate_b, head_norm_w):
    H = M_HEADS
    with Stage(nc) as st:
        (small, gates_in, absed, e_ready, ln_ready, forget_ready, cum_ready, cum_out, offsets_ready,
         qk_turned, qk_act, qk_dve, bcast_ready, head_copied, e_rows, e_out, rows_done, w_ready, score_ready, weighted,
         w_turned, w_copied_a, w_copied_v, pv_ready, head_done, exp_m, ssq_ready, root_ready, o_ready, qk_sums, qk_root) = st.sems(
            "m_small gates_in absed e_ready ln_ready forget_ready cum_ready cum_out offsets_ready "
            "qk_turned qk_act qk_dve bcast_ready head_copied e_rows e_out rows_done w_ready score_ready weighted "
            "w_turned w_copied_a w_copied_v pv_ready head_done exp_m ssq_ready root_ready o_ready qk_sums qk_root")
        sb = lambda n, s: st.sb("m_" + n, s)
        gb = sb("gate_b", [P, 2 * H])
        nw = sb("norm_w", [P, 2 * HD])
        g = sb("gates", [P, TT, 2 * H])
        ga, ge = sb("gate_abs", [P, TT, H]), sb("gate_exp", [P, TT, H])
        lf = sb("log_f", [P, TT, H])
        cum, tot = sb("cum", [P, TT, H]), sb("tot", [P, TT, H])
        off = sb("off", [P, H, TT, TT])
        start = sb("start", [P, H, TT])
        qT, kT = sb("qT", [HD, H, SEQ]), sb("kT", [HD, H, SEQ])
        qs = sb("q_head", [HD, SEQ])
        lfb, lib = sb("lf_rows", [P, TT, P]), sb("li_rows", [P, TT, P])
        eo, ed = sb("e_off", [P, TT, P]), sb("e_diag", [P, TT, P])
        emax, dmax, cand = sb("emax", [P, TT]), sb("dmax", [P, TT]), sb("cand", [P, TT, TT])
        m1, rows = sb("m1", [P, TT]), sb("rows", [P, TT])
        nb, nd = sb("neg_b", [P, TT, TT]), sb("neg_d", [P, TT])
        w = sb("w", [P, TT, SEQ])
        sw = sb("sw", [P, TT, SEQ])
        swT = sb("swT", [P, 2, SEQ])
        num, den, mm = sb("num", [P, H, TT, HD]), sb("den", [P, H, TT]), sb("m", [P, H, TT])
        sq = sb("sq", [P, H, TT, HD])
        ss, rs = sb("ss", [P, H, TT]), sb("rs", [P, H, TT])
        og = sb("og", [P, TT, H * HD])
        squares = sb("qk_squares", [P, TT, ROPED, HD])
        causal = e.k("causal")
        tri = causal[:, SEQ - P:]
        with nc.Block() as block:
            @block.sync
            def _(sp):
                sp.dma_start(gb[:], dram(gate_b, L).broadcast_to([P, 2 * H])).then_inc(small, 16)
                sp.dma_start(nw[:], dram(head_norm_w, L).broadcast_to([P, 2 * HD])).then_inc(small, 16)

            @block.gpsimd
            def _(pool):
                nc.gpsimd.memset(off[:], 0.0)
                nc.gpsimd.memset(start[:], 0.0)
                pool.drain()
                for b in range(TT):
                    for i in range(b + 1):
                        nc.gpsimd.memset(off[:, :, i, b], NEG)
                for h0, n, rows_ in attention_rows(e.proj, all_tiles):
                    last = nc.gpsimd.tensor_tensor(squares[:, :, h0:h0 + n], rows_, rows_, ALU.mult)
                last.then_inc(qk_sums, 1)
                pool.wait_ge(cum_out, 1)
                pool.drain()
                T = lambda u: tot[:, u, :]
                nc.gpsimd.tensor_copy(off[:, :, 2, 0], T(1))
                nc.gpsimd.tensor_copy(off[:, :, 3, 1], T(2))
                nc.gpsimd.tensor_tensor(off[:, :, 3, 0], T(1), T(2), ALU.add)
                nc.gpsimd.tensor_copy(start[:, :, 1], T(0))
                nc.gpsimd.tensor_tensor(start[:, :, 2], T(0), T(1), ALU.add)
                pool.drain()
                nc.gpsimd.tensor_tensor(start[:, :, 3], start[:, :, 2], T(2), ALU.add).then_inc(offsets_ready, 1)
                pool.wait_ge(qk_act, H)
                pool.wait_ge(qk_dve, H)
                with pool.Fori(0, H) as h:
                    pool.wait_ge(e_rows, h + 1)
                    nc.gpsimd.tensor_copy(lfb[:], bc(lf[:, :, bass.ds(h, 1)], P))
                    nc.gpsimd.tensor_copy(lib[:], bc(g[:, :, bass.ds(h, 1)], P)).then_inc(bcast_ready, 1)
                    pool.wait_ge(head_done, h + 1)
                    nc.gpsimd.tensor_copy(qs[:], at(qT, h)).then_inc(head_copied, 1)


            @block.scalar
            def _(act):
                nc.scalar.activation(og[:], e.proj[:, :, C_MO:C_MO + H * HD], ACT.Sigmoid).then_inc(o_ready, 1)
                act.wait_ge(absed, 1)
                nc.scalar.activation(ge[:], ga[:], ACT.Exp, scale=-1.0).then_inc(e_ready, 1)
                act.wait_ge(e_ready, 1)
                nc.scalar.activation(ga[:], ge[:], ACT.Ln, bias=1.0).then_inc(ln_ready, 1)
                for h in range(H):
                    act.wait_ge(qk_turned, 2 * h + 1)
                    nc.scalar.activation(qT[:, h], e.bank[(2 * h) % 8][0:HD], ACT.Copy).then_inc(qk_act, 1)
                nc.scalar.activation(e.conv[:], e.conv[:], ACT.Silu)
                act.drain()
                with act.Fori(0, H) as h:
                    act.wait_ge(rows_done, h + 1)
                    act.wait_ge(head_done, h + 1)
                    for i in range(TT):
                        for b in range(i):
                            nc.scalar.activation(w[:, i, b * P:(b + 1) * P], eo[:, b], ACT.Exp, bias=nb[:, i, b:b + 1])
                        nc.scalar.activation(w[:, i, i * P:(i + 1) * P], ed[:, i], ACT.Exp, bias=nd[:, i:i + 1]).then_inc(w_ready, 1)
                    for i in (1, 3):
                        act.wait_ge(w_turned, h * TT + i + 1)
                        if i == 3:
                            act.wait_ge(pv_ready, h * TT + 2)
                        nc.scalar.activation(swT[:, 1, 0:(i + 1) * P], e.bank[5][:, 0:(i + 1) * P], ACT.Copy).then_inc(w_copied_a, 1)
                act.wait_ge(qk_sums, 2)
                nc.scalar.activation(e.qk_rms[:], e.qk_rms[:], ACT.Sqrt, bias=e.eps[:, 0:1], scale=1.0 / HD).then_inc(qk_root, 1)
                act.wait_ge(absed, 2)
                nc.scalar.activation(ss[:], mm[:], ACT.Exp, scale=-1.0).then_inc(exp_m, 1)
                act.wait_ge(ssq_ready, 1)
                nc.scalar.activation(rs[:], ss[:], ACT.Sqrt, bias=e.eps[:, 0:1], scale=1.0 / HD).then_inc(root_ready, 1)

            @block.tensor
            def _(pe):
                for h in range(H):
                    for n, c0 in ((0, C_MQ), (1, C_MK)):
                        for t in range(TT):
                            last = nc.tensor.transpose(e.bank[2 * h + n][0:HD, t * P:(t + 1) * P],
                                                       e.proj[:, t, c0 + h * HD:c0 + (h + 1) * HD], e.k("ident"))
                        last.then_inc(qk_turned, 1)
                pe.wait_ge(qk_act, 1)
                pe.wait_ge(forget_ready, 1)
                nc.tensor.matmul(e.bank[0][:, 0:TT * H], e.k("upper"), lf[:], start=True, stop=True)
                nc.tensor.matmul(e.bank[0][:, TT * H:2 * TT * H], e.k("ones"), lf[:], start=True, stop=True).then_inc(cum_ready, 1)
                pe.wait_ge(cum_out, 1)
                pe.sem_inc(e_rows, 1)
                with pe.Fori(0, H) as h:
                    pe.wait_ge(bcast_ready, h + 1)
                    for b in range(TT):
                        r = e.bank[6 + b // 2][:, (b % 2) * 2 * P:(b % 2 + 1) * 2 * P]
                        nc.tensor.matmul(r, lfb[:, b], e.k("decay_sel"), start=True, stop=False)
                        last = nc.tensor.matmul(r, lib[:, b], e.k("ident2"), start=False, stop=True)
                    last.then_inc(e_rows, 1)
                    pe.wait_ge(head_copied, h + 1)
                    for i in range(TT):
                        n = (i + 1) * P
                        nc.tensor.matmul(e.bank[i][:, 0:n], qs[:, i * P:n], kT[:, bass.ds(h, 1), 0:n].rearrange("p a n -> p (a n)"),
                                         start=True, stop=True).then_inc(score_ready, 1)

                    def turn(i):
                        pe.wait_ge(weighted, h * TT + i + 1)
                        if i >= 2:
                            pe.wait_ge(w_copied_a if i % 2 else w_copied_v, h * 2 + 1)
                        for b in range(i + 1):
                            last = nc.tensor.transpose(e.bank[4 + i % 2][:, b * P:(b + 1) * P], sw[:, i, b * P:(b + 1) * P], e.k("ident"))
                        last.then_inc(w_turned, 1)

                    def values(i):
                        pe.wait_ge(w_copied_a if i % 2 else w_copied_v, h * 2 + i // 2 + 1)
                        if i == 0:
                            pe.wait_ge(e_out, h + 1)
                        for b in range(i + 1):
                            last = nc.tensor.matmul(e.bank[6][:, i * HD:(i + 1) * HD], swT[:, i % 2, b * P:(b + 1) * P],
                                                    e.proj[:, b, bass.ds(h * HD + C_MV, HD)], start=b == 0, stop=b == i)
                        last.then_inc(pv_ready, 1)

                    turn(0)
                    turn(1)
                    values(0)
                    turn(2)
                    values(1)
                    turn(3)
                    values(2)
                    values(3)
                    pe.wait_ge(head_done, h + 2)

            @block.vector
            def _(dve):
                v = nc.vector
                dve.wait_ge(small, 32)
                v.tensor_tensor(g[:], e.proj[:, :, C_MG:C_MG + 2 * H], gb[:].unsqueeze(1).broadcast_to([P, TT, 2 * H]), ALU.add)
                dve.drain()
                v.tensor_scalar(lf[:], g[:, :, H:], 0.0, None, ALU.min)
                v.scalar_tensor_tensor(ga[:], g[:, :, H:], -1.0, g[:, :, H:], ALU.mult, ALU.max).then_inc(absed, 1)
                for h in range(H):
                    dve.wait_ge(qk_turned, 2 * h + 2)
                    v.tensor_copy(kT[:, h], e.bank[2 * h + 1][0:HD]).then_inc(qk_dve, 1)
                dve.wait_ge(ln_ready, 1)
                v.tensor_tensor(lf[:], lf[:], ga[:], ALU.subtract).then_inc(forget_ready, 1)
                dve.wait_ge(qk_sums, 1)
                v.tensor_reduce(e.qk_rms[:].rearrange("p t h -> p (t h)"), squares[:].rearrange("p t h d -> p (t h) d"), AX.X, ALU.add).then_inc(qk_sums, 1)
                dve.wait_ge(cum_ready, 1)
                v.tensor_copy(cum[:].rearrange("p t h -> p (t h)"), e.bank[0][:, 0:TT * H])
                v.tensor_copy(tot[:].rearrange("p t h -> p (t h)"), e.bank[0][:, TT * H:2 * TT * H]).then_inc(cum_out, 1)
                dve.wait_ge(offsets_ready, 1)
                dve.sem_inc(head_done, 1)
                with dve.Fori(0, H) as h:
                    dve.wait_ge(e_rows, h + 2)
                    for b in range(TT):
                        v.tensor_tensor(ed[:, b], e.bank[6 + b // 2][:, (b % 2) * 256 + P:(b % 2) * 256 + 2 * P], tri, ALU.add)
                        last = v.tensor_copy(eo[:, b], e.bank[6 + b // 2][:, (b % 2) * 256:(b % 2) * 256 + P])
                    last.then_inc(e_out, 1)
                    dve.drain()
                    v.tensor_reduce(emax[:], eo[:], AX.X, ALU.max)
                    v.tensor_reduce(dmax[:], ed[:], AX.X, ALU.max)
                    dve.drain()
                    oh = at(off, h)
                    v.tensor_tensor(cand[:], oh, emax[:].unsqueeze(1).broadcast_to([P, TT, TT]), ALU.add)
                    v.tensor_tensor(dmax[:], dmax[:], start[:, bass.ds(h, 1), :].rearrange("p a t -> p (a t)"), ALU.max)
                    dve.drain()
                    v.tensor_reduce(m1[:], cand[:], AX.X, ALU.max)
                    dve.drain()
                    v.tensor_tensor(m1[:], m1[:], dmax[:], ALU.max)
                    dve.drain()
                    v.tensor_tensor(nb[:], oh, bc(m1[:].unsqueeze(2), TT), ALU.subtract)
                    v.tensor_tensor(mm[:, bass.ds(h, 1), :].rearrange("p a t -> p (a t)"), m1[:],
                                    cum[:, :, bass.ds(h, 1)].rearrange("p t a -> p (t a)"), ALU.add)
                    v.tensor_scalar(nd[:], m1[:], -1.0, None, ALU.mult).then_inc(rows_done, 1)
                    for i in range(TT):
                        n = (i + 1) * P
                        dve.wait_ge(score_ready, h * TT + i + 1)
                        dve.wait_ge(w_ready, h * TT + i + 1)
                        v.tensor_tensor_reduce(sw[:, i, 0:n], e.bank[i][:, 0:n], w[:, i, 0:n], SCALE, 0.0, ALU.mult, ALU.add,
                                               rows[:, i:i + 1]).then_inc(weighted, 1)
                    dve.drain()
                    v.tensor_copy(den[:, bass.ds(h, 1), :].rearrange("p a t -> p (a t)"), rows[:])
                    for i in (0, 2):
                        dve.wait_ge(w_turned, h * TT + i + 1)
                        if i == 2:
                            dve.wait_ge(pv_ready, h * TT + 1)
                        v.tensor_copy(swT[:, 0, 0:(i + 1) * P], e.bank[4][:, 0:(i + 1) * P]).then_inc(w_copied_v, 1)
                    dve.wait_ge(pv_ready, h * TT + TT)
                    v.tensor_copy(at(num, h), e.bank[6][:, 0:TT * HD].rearrange("p (t d) -> p t d", t=TT)).then_inc(head_done, 1)
                dve.drain()
                dve.wait_ge(qk_root, 1)
                v.reciprocal(e.qk_rms[:], e.qk_rms[:])
                v.scalar_tensor_tensor(den[:], den[:], -1.0, den[:], ALU.mult, ALU.max).then_inc(absed, 1)
                dve.wait_ge(exp_m, 1)
                dve.drain()
                v.tensor_tensor(den[:], den[:], ss[:], ALU.max)
                dve.drain()
                v.reciprocal(den[:], den[:])
                dve.drain()
                v.tensor_tensor(num[:], num[:], bc(den[:].unsqueeze(3), HD), ALU.mult)
                dve.drain()
                v.tensor_tensor(sq[:], num[:], num[:], ALU.mult)
                dve.drain()
                v.tensor_reduce(ss[:], sq[:], AX.X, ALU.add).then_inc(ssq_ready, 1)
                dve.wait_ge(root_ready, 1)
                v.reciprocal(rs[:], rs[:])
                dve.drain()
                v.tensor_tensor(num[:], num[:], bc(rs[:].unsqueeze(3), HD), ALU.mult)
                dve.drain()
                v.tensor_tensor(sq[:].rearrange("p h t d -> p (h t) d"), num[:].rearrange("p h t d -> p (h t) d"),
                                nw[:, 0:HD].unsqueeze(1).broadcast_to([P, H * TT, HD]), ALU.mult)
                dve.wait_ge(o_ready, 1)
                dve.drain()
                for h in range(H):
                    v.tensor_tensor(e.y[:, :, h * HD:(h + 1) * HD], sq[:, h], og[:, :, h * HD:(h + 1) * HD], ALU.mult)


def delta_stage(nc, e, L, g_decay, head_norm_w, qk_norm):
    H = G_HEADS
    W = H * P
    with Stage(nc) as st:
        (small, decay_ready, beta_ready, a_exp, a_ln, alpha_ready, staged, raw_turned, ssq_ready, root_ready, gam_ready, gam_out,
         gam_exp, normed, kq_turned, kq_out_v, kq_out_a, grams_ready, dec_arg, dec_ready, gram_out, x0_turned, prepared,
         masked, t1_ready, t1_out, dx_ready, inverted, w_ready, w_out, u_ready, u_out, o_ready, o_out, s_ready, z_ready,
         ssq2_ready, root2_ready, rows_ready, qw_loaded, s_out) = st.sems(
            "g_small decay_ready beta_ready a_exp a_ln alpha_ready staged raw_turned g_ssq_ready g_root_ready gam_ready gam_out "
            "gam_exp normed kq_turned kq_out_v kq_out_a grams_ready dec_arg dec_ready gram_out x0_turned prepared "
            "masked t1_ready t1_out dx_ready inverted wt_ready wt_out u_ready u_out g_o_ready g_o_out s_ready z_ready "
            "ssq2_ready root2_ready gam_rows_ready qw_loaded s_out")
        sb = lambda n, s: st.sb("g_" + n, s)
        gd = sb("decay", [P, 2 * H])
        nw = sb("norm_w", [P, 2 * HD])
        beta = sb("beta", [P, TT, H])
        la = sb("log_alpha", [P, TT, H])
        t1a, t1b = sb("t1a", [P, TT, H]), sb("t1b", [P, TT, H])
        stage = sb("stage", [P, N_CONV, P])
        raw = sb("raw", [P, 3 * H, HD])
        sq = sb("sq", [P, 2 * H, HD])
        ss, rt = sb("ss", [P, 2 * H]), sb("rt", [P, 2 * H])
        lac = sb("la_c", [P, H])
        lar = sb("la_rows", [P, H, P])
        gam, eg, egl = sb("gam", [P, H]), sb("eg", [P, H]), sb("egl", [P, H])
        qk = sb("qk", [P, 4, H, HD])
        qkT = sb("qkT", [HD, 3, H, P])
        dec = sb("dec", [P, H, P])
        at0 = sb("at0", [P, H, P])
        qgT = sb("qgT", [HD, TT, H, P])
        vb, kbg, kd = sb("vb", [P, TT, H, HD]), sb("kbg", [P, TT, H, HD]), sb("kd", [P, TT, H, HD])
        gl = sb("gl", [HD, TT, H])
        aT, pT = sb("aT", [P, TT, W]), sb("pT", [P, TT, W])
        xT, xn = sb("xT", [P, TT, W]), sb("xn", [P, TT, W])
        am, t1 = sb("am", [P, TT, W]), sb("t1", [P, TT, W])
        nwT = sb("nwT", [HD, TT, H, P])
        u = sb("u", [P, 2, H, HD])
        s = sb("s", [HD, H, HD])
        decayed = dec[0:HD, :, 0:HD]
        o = sb("o", [P, TT, H, HD])
        osq = am[:].rearrange("p t n -> p (t n)")[:, 0:TT * H * HD].rearrange("p (t h d) -> p t h d", t=TT, h=H)
        so, ro = sb("so", [P, TT, H]), sb("ro", [P, TT, H])
        zs = e.proj[:, :, C_Z:C_Z + H * HD]
        rows_of = lambda buf, n: buf[:].rearrange("p t n -> p (t n)")[:, n * ROPED * HD:(n + 1) * ROPED * HD].rearrange("p (h d) -> p h d", h=ROPED)
        row, turned_row, norm_rows = rows_of(am, 0), rows_of(am, 1), rows_of(t1, 0)
        h4 = lambda b: b.rearrange("p (h n) -> p h n", h=H)
        odd_even = lambda t, half: t.rearrange("p (g b) n -> p g b n", b=2)[:, :, half]
        ident = e.k("ident")
        with nc.Block() as block:
            @block.sync
            def _(sp):
                sp.dma_start(e.qk_w[:].rearrange("p a d -> p (a d)"), dram(qk_norm, L).broadcast_to([P, 4 * HD])).then_inc(qw_loaded, 16)
                sp.dma_start(gd[:], dram(g_decay, L).broadcast_to([P, 2 * H])).then_inc(small, 16)
                sp.dma_start(nw[:], dram(head_norm_w, L).broadcast_to([P, 2 * HD])).then_inc(small, 16)

            @block.gpsimd
            def _(pool):
                g, half = nc.gpsimd, HD // 2
                pool.wait_ge(qw_loaded, 16)
                for h0, nh, norm in ((0, N_HEADS, 0), (N_HEADS, N_KV, 2), (N_HEADS + N_KV, N_KV, 3)):
                    g.tensor_copy(norm_rows[:, h0:h0 + nh], e.qk_w[:, norm].unsqueeze(1).broadcast_to([P, nh, HD]))
                with pool.Fori(0, TT) as t:
                    scale = e.qk_rms[:, bass.ds(t, 1), :].rearrange("p a h -> p (a h)").unsqueeze(2)
                    tab = lambda n: e.k(n).rearrange("p (t d) -> p t d", t=TT)[:, bass.ds(t, 1)]
                    pool.drain()
                    for h0, nh, x in attention_rows(e.proj, one_tile(t)):
                        g.tensor_tensor(row[:, h0:h0 + nh], x, bc(scale[:, h0:h0 + nh], HD), ALU.mult)
                    pool.drain()
                    g.tensor_tensor(row, row, norm_rows, ALU.mult)
                    pool.drain()
                    g.tensor_tensor(turned_row[:, :, 0:half], row[:, :, half:], tab("sin")[:, :, 0:half].broadcast_to([P, ROPED, half]), ALU.mult)
                    g.tensor_tensor(turned_row[:, :, half:], row[:, :, 0:half], tab("sin")[:, :, half:].broadcast_to([P, ROPED, half]), ALU.mult)
                    pool.drain()
                    g.tensor_tensor(row, row, tab("cos").broadcast_to([P, ROPED, HD]), ALU.mult)
                    pool.drain()
                    for h0, nh, x in attention_rows(e.proj, one_tile(t)):
                        g.tensor_tensor(x, row[:, h0:h0 + nh], turned_row[:, h0:h0 + nh], ALU.add)
                pool.drain()
                pool.wait_ge(prepared, TT)
                for n in range(LEVELS):
                    for c in range(TT):
                        if n:
                            pool.wait_ge(t1_ready, (n - 1) * TT + c + 1)
                        m = e.k("levels")[:, n * P:(n + 1) * P].unsqueeze(1)
                        nc.gpsimd.tensor_tensor(h4(am[:, c]), h4(aT[:, c]), m.broadcast_to([P, H, P]), ALU.mult).then_inc(masked, 1)

            @block.scalar
            def _(act):
                a = nc.scalar.activation
                a(zs, zs, ACT.Silu).then_inc(z_ready, 1)
                a(beta[:], e.proj[:, :, C_GB:C_GB + H], ACT.Sigmoid).then_inc(beta_ready, 1)
                act.wait_ge(small, 32)
                a(gd[:, 0:H], gd[:, 0:H], ACT.Exp).then_inc(decay_ready, 1)
                act.wait_ge(a_exp, 1)
                a(t1b[:], t1b[:], ACT.Exp, scale=-1.0).then_inc(a_ln, 1)
                act.wait_ge(a_ln, 1)
                a(t1b[:], t1b[:], ACT.Ln, bias=1.0).then_inc(a_ln, 1)
                with act.Fori(0, TT) as c:
                    act.wait_ge(raw_turned, c + 1)
                    a(stage[:], e.conv[:, :, bass.ds(c * P, P)], ACT.Copy).then_inc(staged, 1)
                    act.wait_ge(ssq_ready, c + 1)
                    a(rt[:], ss[:], ACT.Sqrt, bias=e.eps[:, 0:1]).then_inc(root_ready, 1)
                    act.wait_ge(gam_out, c + 1)
                    a(eg[:], gam[:], ACT.Exp)
                    a(egl[:], egl[:], ACT.Exp)
                    act.wait_ge(rows_ready, c + 1)
                    a(gl[:, bass.ds(c, 1), :].rearrange("p a h -> p (a h)"), h4(e.bank[2][0:HD])[:, :, P - 1], ACT.Exp).then_inc(gam_exp, 1)
                    for n in (1, 3):
                        act.wait_ge(kq_turned, c * 4 + n + 1)
                        dst = qkT[:, 1] if n == 1 else qgT[:, bass.ds(c, 1)].rearrange("p a h n -> p (a h) n")
                        for half in range(2):
                            last = a(odd_even(dst, half), e.bank[4 + n][half * HD:(half + 1) * HD, 0:2 * P].rearrange("p (g n) -> p g n", g=2), ACT.Copy)
                        last.then_inc(kq_out_a, 1)
                    act.wait_ge(dec_arg, c + 1)
                    a(dec[:], dec[:], ACT.Exp).then_inc(dec_ready, 1)
                with act.Fori(0, LEVELS) as n:
                    for c in range(TT):
                        act.wait_ge(t1_ready, n * TT + c + 1)
                        a(t1[:, c], e.bank[c % 2][:], ACT.Copy).then_inc(t1_out, 1)
                for c in range(TT):
                    act.wait_ge(w_ready, c + 1)
                    a(nwT[:, c].rearrange("p h n -> p (h n)"), e.bank[c % 2][0:HD], ACT.Copy, scale=-1.0).then_inc(w_out, 1)
                for c in range(TT):
                    act.wait_ge(o_ready, c + 1)
                    a(o[:, c].rearrange("p h d -> p (h d)"), e.bank[4][:, 0:H * HD], ACT.Copy).then_inc(o_out, 1)
                act.wait_ge(ssq2_ready, 1)
                a(ro[:], so[:], ACT.Sqrt, bias=e.eps[:, 0:1], scale=1.0 / HD).then_inc(root2_ready, 1)

            @block.tensor
            def _(pe):
                mm = nc.tensor.matmul
                pe.wait_ge(alpha_ready, 1)
                pe.sem_inc(raw_turned, 1)
                with pe.Fori(0, TT) as c:
                    pe.wait_ge(staged, c + 1)
                    for n in range(N_CONV):
                        last = nc.tensor.transpose(e.bank[n // 4][:, (n % 4) * P:(n % 4 + 1) * P], stage[:, n], ident)
                    last.then_inc(raw_turned, 1)
                    pe.wait_ge(normed, c * 3 + 1)
                    mm(e.bank[3][:, 0:H], e.k("upper"), lac[:], start=True, stop=True).then_inc(gam_ready, 1)
                    for h in range(H):
                        last = mm(h4(e.bank[2][:])[:, h], lar[:, h], e.k("upper"), start=True, stop=True)
                    last.then_inc(rows_ready, 1)
                    pe.wait_ge(normed, c * 3 + 2)
                    for n in range(3):
                        for h in range(0, H, 2):
                            last = nc.tensor.transpose(e.bank[4 + n][:, h * HD:(h + 2) * HD], qk[:, n, h:h + 2].rearrange("p h d -> p (h d)"), ident)
                        last.then_inc(kq_turned, 1)
                    pe.wait_ge(normed, c * 3 + 3)
                    for h in range(0, H, 2):
                        last = nc.tensor.transpose(e.bank[7][:, h * HD:(h + 2) * HD], qk[:, 3, h:h + 2].rearrange("p h d -> p (h d)"), ident)
                    last.then_inc(kq_turned, 1)
                    pe.wait_ge(kq_out_v, c * 2 + 2)
                    pe.wait_ge(kq_out_a, c * 2 + 2)
                    for n, b in ((1, 0), (2, 1)):
                        for h in range(H):
                            last = mm(h4(e.bank[b][:])[:, h], qkT[:, 0, h], qkT[:, n, h], start=True, stop=True)
                    last.then_inc(grams_ready, 1)
                    pe.wait_ge(gram_out, c + 1)
                    for h in range(H):
                        last = nc.tensor.transpose(e.bank[5][:, h * P:(h + 1) * P], at0[:, h], ident)
                    last.then_inc(x0_turned, 1)
                pe.wait_ge(prepared, TT)
                with pe.Fori(0, LEVELS) as n:
                    def below(c):
                        pe.wait_ge(masked, n * TT + c + 1)
                        pe.wait_ge(inverted, n * TT + c + 1)
                        if c >= 2:
                            pe.wait_ge(t1_out, n * TT + c - 1)
                        for h in range(H):
                            last = mm(h4(e.bank[c % 2][:])[:, h], am[:, c, h * P:(h + 1) * P], xn[:, c, h * P:(h + 1) * P], start=True, stop=True)
                        last.then_inc(t1_ready, 1)

                    def join(c):
                        pe.wait_ge(t1_out, n * TT + c + 1)
                        pe.wait_ge(inverted, n * TT + c - 1 + TT)
                        for h in range(H):
                            hs = slice(h * P, (h + 1) * P)
                            mm(h4(e.bank[2 + 2 * (c % 2)][:])[:, h], t1[:, c, hs], xT[:, c, hs], start=True, stop=True)
                            last = mm(h4(e.bank[3 + 2 * (c % 2)][:])[:, h], xT[:, c, hs], t1[:, c, hs], start=True, stop=True)
                        last.then_inc(dx_ready, 1)

                    below(0)
                    below(1)
                    join(0)
                    below(2)
                    join(1)
                    below(3)
                    join(2)
                    join(3)
                pe.wait_ge(inverted, LEVELS * TT + TT)
                for c in range(TT):
                    if c >= 2:
                        pe.wait_ge(w_out, c - 1)
                    for h in range(H):
                        last = mm(e.bank[c % 2][0:HD, h * P:(h + 1) * P], kbg[:, c, h], xT[:, c, h * P:(h + 1) * P], start=True, stop=True)
                    last.then_inc(w_ready, 1)
                for c in range(TT):
                    bank = lambda i, h, n=P: e.bank[i][0:n, h * HD:(h + 1) * HD]
                    for h in range(H):
                        mm(bank(3, h), xT[:, c, h * P:(h + 1) * P], vb[:, c, h], start=h == 0, stop=False)
                    pe.wait_ge(w_out, c + 1)
                    pe.wait_ge(s_out, c + 1)
                    for h in range(H):
                        last = mm(bank(3, h), nwT[:, c, h], s[:, h], start=False, stop=h == H - 1)
                    last.then_inc(u_ready, 1)
                    if c:
                        pe.wait_ge(o_out, c)
                    for h in range(H):
                        mm(bank(4, h), qgT[:, c, h], s[:, h], start=h == 0, stop=False)
                    pe.wait_ge(u_out, c + 1)
                    for h in range(H):
                        last = mm(bank(5, h, HD), kd[:, c, h], u[:, c % 2, h], start=True, stop=True)
                    last.then_inc(s_ready, 1)
                    for h in range(H):
                        last = mm(bank(4, h), pT[:, c, h * P:(h + 1) * P], u[:, c % 2, h], start=False, stop=h == H - 1)
                    last.then_inc(o_ready, 1)

            @block.vector
            def _(dve):
                v = nc.vector
                bh = lambda x, n=HD: bc(x.unsqueeze(2), n)
                v.memset(s[:], 0.0)
                dve.wait_ge(small, 32)
                v.tensor_tensor(t1a[:], e.proj[:, :, C_GA:C_GA + H], gd[:, H:].unsqueeze(1).broadcast_to([P, TT, H]), ALU.add)
                dve.drain()
                v.scalar_tensor_tensor(t1b[:], t1a[:], -1.0, t1a[:], ALU.mult, ALU.max).then_inc(a_exp, 1)
                v.tensor_scalar(t1a[:], t1a[:], 0.0, None, ALU.max)
                dve.drain()
                dve.wait_ge(a_ln, 2)
                v.tensor_tensor(t1a[:], t1a[:], t1b[:], ALU.add)
                dve.drain()
                dve.wait_ge(decay_ready, 1)
                v.scalar_tensor_tensor(la[:], t1a[:], -1.0, gd[:, 0:H].unsqueeze(1).broadcast_to([P, TT, H]), ALU.mult, ALU.mult).then_inc(alpha_ready, 1)
                dve.wait_ge(beta_ready, 1)
                with dve.Fori(0, TT) as c:
                    dve.drain()
                    v.tensor_copy(lac[:], la[:, bass.ds(c, 1), :].rearrange("p a h -> p (a h)"))
                    v.tensor_copy(lar[:], bc(la[:, bass.ds(c, 1), :].rearrange("p a h -> p (a h)").unsqueeze(2), P)).then_inc(normed, 1)
                    dve.wait_ge(raw_turned, c + 2)
                    v.tensor_copy(raw[:, 0:8].rearrange("p h d -> p (h d)"), e.bank[0][:])
                    v.tensor_copy(raw[:, 8:12].rearrange("p h d -> p (h d)"), e.bank[1][:, 0:H * HD])
                    dve.drain()
                    v.tensor_tensor(sq[:], raw[:, 0:8], raw[:, 0:8], ALU.mult)
                    dve.drain()
                    v.tensor_reduce(ss[:], sq[:], AX.X, ALU.add).then_inc(ssq_ready, 1)
                    dve.wait_ge(gam_ready, c + 1)
                    dve.wait_ge(rows_ready, c + 1)
                    v.tensor_copy(gam[:], e.bank[3][:, 0:H])
                    dve.drain()
                    v.tensor_tensor(egl[:], h4(e.bank[2][:])[:, :, P - 1], gam[:], ALU.subtract).then_inc(gam_out, 1)
                    dve.wait_ge(root_ready, c + 1)
                    v.reciprocal(ss[:], rt[:])
                    dve.drain()
                    k_, kb_, q_, qg_ = (qk[:, n] for n in range(4))
                    bt = beta[:, bass.ds(c, 1), :].rearrange("p a h -> p (a h)")
                    v.tensor_tensor(k_, raw[:, 4:8], bh(ss[:, 4:8]), ALU.mult)
                    v.tensor_tensor(q_, raw[:, 0:4], bh(ss[:, 0:4]), ALU.mult)
                    dve.drain()
                    v.tensor_tensor(kb_, k_, bh(bt), ALU.mult)
                    v.tensor_scalar(q_, q_, SCALE, None, ALU.mult).then_inc(normed, 1)
                    dve.drain()
                    dve.wait_ge(gam_exp, c + 1)
                    col = lambda t: t[:, bass.ds(c, 1)].rearrange("p a h n -> p (a h) n")
                    v.tensor_tensor(qg_, q_, bh(eg[:]), ALU.mult).then_inc(normed, 1)
                    v.tensor_tensor(dec[:], h4(e.bank[2][:]), bh(gam[:], P), ALU.subtract)
                    dve.drain()
                    v.tensor_tensor(dec[:], dec[:], e.k("causal_t").unsqueeze(1).broadcast_to([P, H, P]), ALU.add).then_inc(dec_arg, 1)
                    for n in (0, 2):
                        dve.wait_ge(kq_turned, c * 4 + n + 1)
                        for half in range(2):
                            last = v.tensor_copy(odd_even(qkT[:, n], half), e.bank[4 + n][half * HD:(half + 1) * HD, 0:2 * P].rearrange("p (g n) -> p g n", g=2))
                        last.then_inc(kq_out_v, 1)
                    v.tensor_tensor(col(kbg), kb_, bh(eg[:]), ALU.mult)
                    v.tensor_tensor(col(kd), k_, bh(egl[:]), ALU.mult)
                    v.tensor_tensor(col(vb), raw[:, 8:12], bh(bt), ALU.mult)
                    dve.wait_ge(dec_ready, c + 1)
                    dve.wait_ge(grams_ready, c + 1)
                    rows = lambda t: h4(t[:, bass.ds(c, 1)].rearrange("p a n -> p (a n)"))
                    v.tensor_tensor(at0[:], h4(e.bank[0][:]), dec[:], ALU.mult)
                    v.tensor_tensor(rows(pT), h4(e.bank[1][:]), dec[:], ALU.mult)
                    dve.drain()
                    v.tensor_copy(rows(aT), at0[:])
                    dve.drain()
                    v.tensor_tensor(at0[:], at0[:], e.k("level0").unsqueeze(1).broadcast_to([P, H, P]), ALU.mult)
                    dve.drain()
                    v.tensor_tensor(at0[:], ident.unsqueeze(1).broadcast_to([P, H, P]), at0[:], ALU.subtract).then_inc(gram_out, 1)
                    dve.drain()
                    v.tensor_copy(rows(xT), at0[:])
                    dve.wait_ge(x0_turned, c + 1)
                    v.tensor_copy(rows(xn), h4(e.bank[5][:])).then_inc(prepared, 1)
                dve.sem_inc(inverted, TT)
                with dve.Fori(0, LEVELS) as n:
                    for c in range(TT):
                        dve.wait_ge(dx_ready, n * TT + c + 1)
                        v.tensor_tensor(xT[:, c], xT[:, c], e.bank[2 + 2 * (c % 2)][:], ALU.subtract)
                        v.tensor_tensor(xn[:, c], xn[:, c], e.bank[3 + 2 * (c % 2)][:], ALU.subtract).then_inc(inverted, 1)
                v.memset(so[:], 0.0).then_inc(s_out, 1)
                for c in range(TT):
                    dve.wait_ge(u_ready, c + 1)
                    v.tensor_copy(u[:, c % 2].rearrange("p h d -> p (h d)"), e.bank[3][:, 0:H * HD]).then_inc(u_out, 1)
                    v.tensor_tensor(decayed, s[:], bh(gl[:, c]), ALU.mult)
                    dve.drain()
                    dve.wait_ge(s_ready, c + 1)
                    v.tensor_tensor(s[:], decayed, e.bank[5][0:HD, 0:H * HD].rearrange("p (h d) -> p h d", h=H), ALU.add).then_inc(s_out, 1)
                dve.wait_ge(o_out, TT)
                v.tensor_tensor(osq, o[:], o[:], ALU.mult)
                dve.drain()
                v.tensor_reduce(so[:], osq, AX.X, ALU.add).then_inc(ssq2_ready, 1)
                dve.wait_ge(root2_ready, 1)
                v.reciprocal(ro[:], ro[:])
                dve.drain()
                v.tensor_tensor(o[:], o[:], bc(ro[:].unsqueeze(3), HD), ALU.mult)
                dve.drain()
                th = lambda x: x.rearrange("p t h d -> p (t h) d")
                v.tensor_tensor(th(osq), th(o[:]), nw[:, HD:].unsqueeze(1).broadcast_to([P, TT * H, HD]), ALU.mult)
                dve.drain()
                dve.wait_ge(z_ready, 1)
                v.tensor_tensor(e.y[:, :, M_W:M_W + H * HD], osq.rearrange("p t h d -> p t (h d)"), zs, ALU.mult)


def nsa_stage(nc, e, L, cmp_pos, cmp_w1, cmp_w2):
    NQ, NK = N_HEADS, 2 * N_KV
    NH = NQ + NK
    NC = N_CMP
    PAIRS = CMP_BLOCK // 2
    HT = CMP_HIDDEN // P
    with Stage(nc) as st:
        (small, w1_loaded, w2_loaded, gates_ready, q_turned, qk_out_v, qk_out_a, c_turned, blocks_ready,
         hid_ready, hid_act, hid_turned, hid_out, kc_ready, kc_ss, kc_root, kc_roped, kc_turned, kc_out, vc_ready, cs_ready, cs_masked, cp_ready, cp_scaled,
         cp_turned, cp_out, co_ready, co_out, q_copied, score_ready, tile_taken, max_ready, prob_ready, turned, t_out_v, t_out_a,
         pv_ready, combined, added, output_taken, blk_zero, masked) = st.sems(
            "n_small w1_loaded w2_loaded n_gates_ready q_turned qk_out_v qk_out_a c_turned blocks_ready "
            "hid_ready hid_act hid_turned hid_out kc_ready kc_ss kc_root kc_roped kc_turned kc_out vc_ready cs_ready cs_masked cp_ready cp_scaled "
            "cp_turned cp_out co_ready co_out q_copied n_score_ready tile_taken max_ready prob_ready n_turned t_out_v t_out_a "
            "n_pv_ready combined added output_taken blk_zero n_masked")
        sb = lambda n, s: st.sb("n_" + n, s)
        pos = sb("pos", [P, 2, PAIRS])
        w1 = sb("w1", [P, 2, PAIRS, CMP_HIDDEN])
        w2 = sb("w2", [P, 2, HT, HD])
        ng = sb("gates", [P, TT, 3 * NQ])
        qT, kT = sb("qT", [HD, NQ, SEQ]), sb("kT", [HD, NK, SEQ])
        blk = sb("blocks", [P, 2, PAIRS, N_KV * NC])
        hidT = sb("hidT", [P, 2, HT, N_KV * NC])
        hid = sb("hid", [N_KV * NC, 2, HT, P])
        kc, kc1, kc2 = sb("kc", [NC, N_KV, HD]), sb("kc1", [NC, N_KV, HD]), sb("kc2", [NC, N_KV, HD])
        ks, kr = sb("kc_ss", [NC, N_KV]), sb("kc_rs", [NC, N_KV])
        kcT = sb("kcT", [HD, N_KV, 32])
        vcb = sb("vc_blocks", [P, N_KV, GROUP, HD])
        cp = sb("cp", [P, TT, NQ, 32])
        cm, cs = sb("cmp_max", [P, TT, NQ]), sb("cmp_sum", [P, TT, NQ])
        cpT = sb("cpT", [P, 2, P])
        qs = sb("q_head", [HD, N_KV, SEQ])
        sm = sb("masked_s", [P, 2, TT, SEQ])
        pr = w1[:].rearrange("p a b c -> p (a b c)")[:, 0:2 * TT * SEQ].rearrange("p (a t s) -> p a t s", a=2, t=TT)
        pt = sb("probs_t", [P, 2, SEQ])
        mx, nm, rsum = sb("mx", [P, 2, TT]), sb("neg_max", [P, 2, TT]), sb("row_sum", [P, 2, TT])
        cf, om = sb("coef_o", [P, TT]), sb("o_scaled", [P, 2, TT, HD])
        causal, ident = e.k("causal"), e.k("ident")
        Y0 = M_W + G_HEADS * HD
        half = HD // 2
        v_cols = (C_VS, C_VWN)

        def compressed(pe, mm, i):
            t, kv = i // N_KV, i % N_KV
            pe.wait_ge(cp_out, i + 1)
            if i >= 2:
                pe.wait_ge(co_out, i - 1)
            mm(e.bank[6 + i % 2][:, 0:GROUP * HD], cpT[:, i % 2], vcb[:, kv].rearrange("p g d -> p (g d)"), start=True, stop=True).then_inc(co_ready, 1)

        def take(dve, v, i):
            t, kv = i // N_KV, i % N_KV
            dve.wait_ge(co_ready, i + 1)
            v.tensor_copy(e.y[:, t, Y0 + kv * GROUP * HD:Y0 + (kv + 1) * GROUP * HD], e.bank[6 + i % 2][:, 0:GROUP * HD]).then_inc(co_out, 1)

        with nc.Block() as block:
            @block.sync
            def _(sp):
                sp.dma_start(pos[:].rearrange("p a b -> p (a b)"), dram(cmp_pos, L)).then_inc(small, 16)
                sp.dma_start(w1[:].rearrange("p a b c -> p (a b c)"), dram(cmp_w1, L)).then_inc(w1_loaded, 16)
                sp.dma_start(w2[:].rearrange("p a b c -> p (a b c)"), dram(cmp_w2, L)).then_inc(w2_loaded, 16)

            @block.gpsimd
            def _(pool):
                nc.gpsimd.memset(vcb[:], 0.0).then_inc(blk_zero, 1)
                nc.gpsimd.memset(cp[:], 0.0).then_inc(blk_zero, 1)
                pool.sem_inc(added, 2)
                pool.wait_ge(co_out, TT * N_KV)
                with pool.Fori(0, GROUP) as g:
                    for j in range(4):
                        kv = j // 2
                        pool.drain()
                        pool.wait_ge(combined, g * 4 + j + 3)
                        pool.sem_inc(output_taken, 1)
                        yh = e.y[:, :, bass.ds((kv * GROUP + g) * HD + Y0, HD)]
                        nc.gpsimd.tensor_tensor(yh, yh, om[:, j % 2], ALU.add).then_inc(added, 1)

            @block.scalar
            def _(act):
                a = nc.scalar.activation
                act.sem_inc(prob_ready, 8)
                act.sem_inc(t_out_a, 2)
                a(ng[:], e.proj[:, :, C_NG:C_NG + 3 * NQ], ACT.Sigmoid).then_inc(gates_ready, 1)
                for n in range(NH // 2):
                    act.wait_ge(q_turned, n + 1)
                    hh = 2 * n + 1
                    act.wait_ge(qk_out_v, n + 1)
                    a(qT[:, hh] if hh < NQ else kT[:, hh - NQ], e.bank[n % 4][HD:P], ACT.Copy).then_inc(qk_out_a, 1)
                act.wait_ge(hid_ready, 1)
                a(hid[:].rearrange("p n h m -> p (n h m)"), e.bank[7][0:N_KV * NC], ACT.Silu).then_inc(hid_act, 1)
                act.wait_ge(kc_ss, 1)
                a(kr[:], ks[:], ACT.Sqrt, bias=e.eps[0:NC, 0:1], scale=1.0 / HD).then_inc(kc_root, 1)
                act.wait_ge(cs_masked, 1)
                a(cp[:, :, :, 0:NC], cp[:, :, :, 0:NC], ACT.Exp, scale=SCALE).then_inc(cp_ready, 1)

                def take_q(g, kv):
                    a(qs[:, kv], at(qT, kv * GROUP + g), ACT.Copy).then_inc(q_copied, 1)

                def probs(g, j):
                    act.wait_ge(combined, g * 4 + j + 1)
                    act.wait_ge(turned, g * 16 + j * 4 + 4)
                    act.wait_ge(max_ready, g * 4 + j + 1)
                    for t in range(TT):
                        n = (t + 1) * P
                        a(pr[:, j % 2, t, 0:n], sm[:, j % 2, t, 0:n], ACT.Exp, bias=nm[:, j % 2, t:t + 1], scale=SCALE,
                          accum_out=rsum[:, j % 2, t:t + 1]).then_inc(prob_ready, 1)

                def late_tiles(g, j):
                    for t in (2, 3):
                        act.wait_ge(turned, g * 16 + j * 4 + t + 1 + 8)
                        act.wait_ge(pv_ready, g * 16 + j * 4 + t + 3)
                        a(pt[:, t % 2, 0:(t + 1) * P], e.bank[4 + t % 2][:, 0:(t + 1) * P], ACT.Copy).then_inc(t_out_a, 1)

                def group(g, last):
                    for j in range(4):
                        late_tiles(g, j)
                        if not (last and j == 3):
                            probs(g, j + 1)
                        if j in (1, 2) and not last:
                            take_q(g + 1, j - 1)

                act.wait_ge(qk_out_v, NH // 2)
                act.drain()
                for kv in range(N_KV):
                    take_q(0, kv)
                probs(0, 0)
                with act.Fori(0, GROUP - 1) as g:
                    group(g, False)
                group(GROUP - 1, True)

            @block.tensor
            def _(pe):
                mm, tr = nc.tensor.matmul, nc.tensor.transpose
                pe.sem_inc(turned, 8)
                pe.sem_inc(pv_ready, 4)
                for n, c0 in ((0, C_KC), (1, C_VC)):
                    for t in range(TT):
                        last = tr(e.bank[5 + n][:, t * P:(t + 1) * P], e.proj[:, t, c0:c0 + P], ident)
                    last.then_inc(c_turned, 1)
                for n in range(NH // 2):
                    c0 = C_Q + n * P if 2 * n < NQ else (C_KS, C_KWN)[n - NQ // 2]
                    if n >= 4:
                        pe.wait_ge(qk_out_a, n - 3)
                    for t in range(TT):
                        last = tr(e.bank[n % 4][:, t * P:(t + 1) * P], e.proj[:, t, c0:c0 + P], ident)
                    last.then_inc(q_turned, 1)
                pe.wait_ge(w1_loaded, 16)
                for n in range(2):
                    pe.wait_ge(blocks_ready, n + 1)
                    for a_ in range(PAIRS):
                        last = mm(e.bank[7][0:N_KV * NC, n * CMP_HIDDEN:(n + 1) * CMP_HIDDEN], blk[:, n, a_], w1[:, n, a_],
                                  start=a_ == 0, stop=a_ == PAIRS - 1)
                last.then_inc(hid_ready, 1)
                pe.wait_ge(hid_act, 1)
                for n in range(2):
                    for ht in range(HT):
                        last = tr(e.bank[5][:, (n * HT + ht) * 64:(n * HT + ht) * 64 + N_KV * NC], hid[:, n, ht], ident[0:N_KV * NC, 0:N_KV * NC])
                last.then_inc(hid_turned, 1)
                pe.wait_ge(w2_loaded, 16)
                pe.wait_ge(hid_out, 1)
                for n in range(2):
                    for kv in range(N_KV):
                        for ht in range(HT):
                            last = mm(e.bank[4][0:NC, (n * N_KV + kv) * HD:(n * N_KV + kv + 1) * HD],
                                      hidT[:, n, ht, kv * NC:(kv + 1) * NC], w2[:, n, ht], start=ht == 0, stop=ht == HT - 1)
                last.then_inc(kc_ready, 1)
                pe.wait_ge(kc_roped, 1)
                for kv in range(N_KV):
                    last = tr(e.bank[5][0:HD, kv * 32:kv * 32 + NC], kc2[:, kv], ident[0:NC, 0:NC])
                last.then_inc(kc_turned, 1)
                pe.wait_ge(kc_out, 1)
                pe.wait_ge(qk_out_a, NH // 2)
                pe.wait_ge(qk_out_v, NH // 2)
                for t in range(TT):
                    for h in range(NQ):
                        last = mm(e.bank[t // 2][:, ((t % 2) * NQ + h) * 32:((t % 2) * NQ + h) * 32 + NC],
                                  qT[:, h, t * P:(t + 1) * P], kcT[:, h // GROUP, 0:NC], start=True, stop=True)
                last.then_inc(cs_ready, 1)
                pe.wait_ge(cp_scaled, 1)
                pe.wait_ge(vc_ready, 1)
                for i in range(TT * N_KV):
                    t, kv = i // N_KV, i % N_KV
                    if i >= 2:
                        pe.wait_ge(cp_out, i - 1)
                    tr(e.bank[2 + i % 2][:, 0:P], cp[:, t, kv * GROUP:(kv + 1) * GROUP].rearrange("p h n -> p (h n)"), ident).then_inc(cp_turned, 1)
                    if i >= 1:
                        compressed(pe, mm, i - 1)
                compressed(pe, mm, TT * N_KV - 1)
                pe.wait_ge(co_out, TT * N_KV)

                def scores(g, j):
                    kv, br = j // 2 % 2, j % 2
                    if br == 0:
                        pe.wait_ge(q_copied, g * 2 + j // 2 + 1)
                    for t in range(TT):
                        n = (t + 1) * P
                        pe.wait_ge(masked, g * 16 + j * 4 + t + 1)
                        mm(e.bank[t][:, 0:n], qs[:, kv, t * P:n], kT[:, br * N_KV + kv, 0:n], start=True, stop=True).then_inc(score_ready, 1)

                def turn(g, j, t):
                    pe.wait_ge(prob_ready, g * 16 + j * 4 + t + 1 + 8)
                    if t < 2:
                        pe.wait_ge(t_out_a, g * 8 + j * 2 + t + 1)
                    else:
                        pe.wait_ge(t_out_v, g * 8 + j * 2 + t - 1)
                    for b in range(t + 1):
                        last = tr(e.bank[4 + t % 2][:, b * P:(b + 1) * P], pr[:, j % 2, t, b * P:(b + 1) * P], ident)
                    last.then_inc(turned, 1)

                def values(g, j, t):
                    kv, br = j // 2, j % 2
                    if t == 0:
                        pe.wait_ge(combined, g * 4 + j + 1)
                    if t < 2:
                        pe.wait_ge(t_out_v, g * 8 + j * 2 + t + 1)
                    else:
                        pe.wait_ge(t_out_a, g * 8 + j * 2 + t + 1)
                    for b in range(t + 1):
                        last = mm(e.bank[6 + j % 2][:, t * HD:(t + 1) * HD], pt[:, t % 2, b * P:(b + 1) * P],
                                  e.proj[:, b, v_cols[br] + kv * HD:v_cols[br] + (kv + 1) * HD], start=b == 0, stop=b == t)
                    last.then_inc(pv_ready, 1)

                def group(g, final):
                    for j in range(4):
                        turn(g, j, 0)
                        turn(g, j, 1)
                        if not (final and j == 3):
                            scores(g, j + 1)
                        values(g, j, 0)
                        turn(g, j, 2)
                        values(g, j, 1)
                        turn(g, j, 3)
                        values(g, j, 2)
                        values(g, j, 3)

                scores(0, 0)
                with pe.Fori(0, GROUP - 1) as g:
                    group(g, False)
                group(GROUP - 1, True)

            @block.vector
            def _(dve):
                v = nc.vector
                dve.sem_inc(masked, 4)
                dve.sem_inc(combined, 2)
                dve.wait_ge(small, 16)
                for n in range(2):
                    dve.wait_ge(c_turned, n + 1)
                    for kv in range(N_KV):
                        for par in range(2):
                            for hi in range(2):
                                rows = e.bank[5 + n][kv * HD:(kv + 1) * HD].rearrange("p (w a r) -> p r a w", r=2, a=PAIRS // 2)[:, par, :, hi:hi + NC]
                                dst = blk[par * HD:(par + 1) * HD, n, hi * 8:(hi + 1) * 8, kv * NC:(kv + 1) * NC]
                                ps_ = pos[par * HD:(par + 1) * HD, n, hi * 8:(hi + 1) * 8]
                                last = v.tensor_tensor(dst, rows, bc(ps_.unsqueeze(2), NC), ALU.add)
                    last.then_inc(blocks_ready, 1)
                for n in range(NH // 2):
                    dve.wait_ge(q_turned, n + 1)
                    hh = 2 * n
                    v.tensor_copy(qT[:, hh] if hh < NQ else kT[:, hh - NQ], e.bank[n % 4][0:HD]).then_inc(qk_out_v, 1)
                dve.wait_ge(hid_turned, 1)
                v.tensor_copy(hidT[:], e.bank[5][:, 0:2 * HT * 64].rearrange("p (a b n) -> p a b n", a=2, b=HT)[:, :, :, 0:N_KV * NC]).then_inc(hid_out, 1)
                dve.wait_ge(kc_ready, 1)
                dve.wait_ge(blk_zero, 2)
                v.tensor_copy(kc[:].rearrange("p k d -> p (k d)"), e.bank[4][0:NC, 0:N_KV * HD])
                for kv in range(N_KV):
                    for g in range(GROUP):
                        last = v.tensor_copy(vcb[32 * g:32 * g + NC, kv, g], e.bank[4][0:NC, (N_KV + kv) * HD:(N_KV + kv + 1) * HD])
                last.then_inc(vc_ready, 1)
                dve.drain()
                v.tensor_tensor(kc1[:], kc[:], kc[:], ALU.mult)
                dve.drain()
                v.tensor_reduce(ks[:], kc1[:], AX.X, ALU.add).then_inc(kc_ss, 1)
                dve.wait_ge(kc_root, 1)
                v.reciprocal(kr[:], kr[:])
                dve.drain()
                v.tensor_tensor(kc[:], kc[:], bc(kr[:].unsqueeze(2), HD), ALU.mult)
                dve.drain()
                v.tensor_tensor(kc[:], kc[:], e.qk_w[0:NC, 1].unsqueeze(1).broadcast_to([NC, N_KV, HD]), ALU.mult)
                dve.drain()
                ctab = lambda n: e.k(n)[0:NC].unsqueeze(1)
                v.tensor_tensor(kc2[:], kc[:], ctab("cmp_cos").broadcast_to([NC, N_KV, HD]), ALU.mult)
                v.tensor_tensor(kc1[:, :, 0:half], kc[:, :, half:], ctab("cmp_sin")[:, :, 0:half].broadcast_to([NC, N_KV, half]), ALU.mult)
                v.tensor_tensor(kc1[:, :, half:], kc[:, :, 0:half], ctab("cmp_sin")[:, :, half:].broadcast_to([NC, N_KV, half]), ALU.mult)
                dve.drain()
                v.tensor_tensor(kc2[:], kc2[:], kc1[:], ALU.add).then_inc(kc_roped, 1)
                dve.wait_ge(kc_turned, 1)
                v.tensor_copy(kcT[:, :, 0:NC], e.bank[5][0:HD, 0:64].rearrange("p (k n) -> p k n", k=N_KV)[:, :, 0:NC]).then_inc(kc_out, 1)
                dve.wait_ge(cs_ready, 1)
                for t in range(TT):
                    src = e.bank[t // 2][:].rearrange("p (u h n) -> p u h n", u=2, h=NQ)[:, t % 2, :, 0:NC]
                    v.tensor_tensor(cp[:, t, :, 0:NC], src, e.k("cmp_mask")[:, t * NC:(t + 1) * NC].unsqueeze(1).broadcast_to([P, NQ, NC]), ALU.add)
                dve.drain()
                v.tensor_reduce(cm[:], cp[:, :, :, 0:NC], AX.X, ALU.max)
                dve.drain()
                flat = cp[:].rearrange("p t h n -> p (t h) n")[:, :, 0:NC]
                v.tensor_tensor(flat, flat, bc(cm[:].rearrange("p t h -> p (t h)").unsqueeze(2), NC), ALU.subtract).then_inc(cs_masked, 1)
                dve.wait_ge(cp_ready, 1)
                v.tensor_reduce(cs[:], cp[:, :, :, 0:NC], AX.X, ALU.add)
                dve.drain()
                v.reciprocal(cs[:], cs[:])
                dve.wait_ge(gates_ready, 1)
                v.tensor_tensor(cm[:], ng[:, :, 0:NQ], bc(e.k("cmp_any").unsqueeze(2), NQ), ALU.mult)
                dve.drain()
                v.tensor_tensor(cs[:], cs[:], cm[:], ALU.mult)
                dve.drain()
                v.tensor_tensor(flat, flat, bc(cs[:].rearrange("p t h -> p (t h)").unsqueeze(2), NC), ALU.mult).then_inc(cp_scaled, 1)
                for i in range(TT * N_KV):
                    t, kv = i // N_KV, i % N_KV
                    dve.wait_ge(cp_turned, i + 1)
                    if i >= 2:
                        dve.wait_ge(co_ready, i - 1)
                    v.tensor_copy(cpT[:, i % 2], e.bank[2 + i % 2][:, 0:P]).then_inc(cp_out, 1)
                    if i >= 1:
                        take(dve, v, i - 1)
                take(dve, v, TT * N_KV - 1)

                def mask_max(g, j):
                    for t in range(TT):
                        n = (t + 1) * P
                        dve.wait_ge(prob_ready, g * 16 + j * 4 + t + 1)
                        dve.wait_ge(score_ready, g * 16 + j * 4 + t + 1)
                        dve.sem_inc(tile_taken, 1)
                        v.tensor_tensor_reduce(sm[:, j % 2, t, 0:n], e.bank[t][:, 0:n], causal[:, SEQ - n:], 1.0, -3.0e38,
                                               ALU.add, ALU.max, mx[:, j % 2, t:t + 1]).then_inc(masked, 1)
                    dve.drain()
                    v.tensor_scalar(nm[:, j % 2], mx[:, j % 2], -SCALE, None, ALU.mult).then_inc(max_ready, 1)

                def early_tiles(g, j):
                    for t in range(2):
                        dve.wait_ge(turned, g * 16 + j * 4 + t + 1 + 8)
                        dve.wait_ge(pv_ready, g * 16 + j * 4 + 3 + t)
                        v.tensor_copy(pt[:, t, 0:(t + 1) * P], e.bank[4 + t][:, 0:(t + 1) * P]).then_inc(t_out_v, 1)

                def finish(g, j):
                    kv, br = j // 2, j % 2
                    dve.drain()
                    dve.wait_ge(prob_ready, g * 16 + j * 4 + 4 + 8)
                    v.reciprocal(cf[:], rsum[:, j % 2])
                    dve.drain()
                    gate = ng[:, :, bass.ds((br + 1) * NQ + kv * GROUP + g, 1)].rearrange("p t a -> p (t a)")
                    v.tensor_tensor(cf[:], cf[:], gate, ALU.mult)
                    dve.drain()
                    dve.wait_ge(added, g * 4 + j + 1)
                    dve.wait_ge(pv_ready, g * 16 + j * 4 + 4 + 4)
                    v.tensor_tensor(om[:, j % 2], e.bank[6 + j % 2][:, 0:TT * HD].rearrange("p (t d) -> p t d", t=TT), bc(cf[:].unsqueeze(2), HD),
                                    ALU.mult).then_inc(combined, 1)

                def group(g, last):
                    for j in range(4):
                        early_tiles(g, j)
                        if not (last and j == 3):
                            mask_max(g, j + 1)
                        finish(g, j)

                mask_max(0, 0)
                with dve.Fori(0, GROUP - 1) as g:
                    group(g, False)
                group(GROUP - 1, True)


def at4(t, i):
    return t[:, bass.ds(i, 1)].rearrange("p a b c -> p (a b) c")


def store_stage(nc, e, out):
    with Stage(nc) as st:
        stored, = st.sems("stored")
        with nc.Block() as block:
            @block.sync
            def _(sp):
                sp.dma_start(out, e.x[:].rearrange("p k n -> p (k n)")).then_inc(stored, 16)
                sp.wait_ge(stored, 16)


def decoder_kernel(nc, x_t, c_t, const, ada_w, ada_b, norm_w, w_up, w_down, w_tok, w_gate, w_conv, conv_w, w_out,
                   m_gate_b, head_norm_w, g_decay, qk_norm, cmp_pos, cmp_w1, cmp_w2, out):
    with ExitStack() as ctx:
        def sb(name, shape):
            return ctx.enter_context(nc.sbuf_tensor(name, shape, F32))

        e = Env()
        e.x = sb("x", [P, KT, SEQ])
        e.h = sb("h", [P, KT, SEQ])
        e.y = e.h[:].rearrange("p k n -> p (k n)").rearrange("p (t n) -> p t n", t=TT)
        e.base = sb("const_base", [P, BASE_W])

        def const_part(name):
            start, width = CONST_AT[name]
            return e.base[:, start:start + width] if start < BASE_W else e.const[:, start - BASE_W:start - BASE_W + width]

        e.k = const_part
        e.c, e.csil = sb("c", [P, KT]), sb("c_silu", [P, KT])
        e.mod, e.coef, e.gate = sb("mod", [P, 9 * KT]), sb("coef", [P, 3, KT]), sb("gate", [P, 3, KT])
        e.mod_b, e.nw = sb("mod_bias", [P, 9 * KT]), sb("norm_w_sb", [P, 3 * KT])
        e.eps = sb("eps", [P, 1])
        e.bank = [ctx.enter_context(nc.psum_tensor(f"bank{i}", [P, 512], F32)) for i in range(8)]
        load_stage(nc, e, x_t, c_t, const)
        with nc.Fori(0, DEPTH) as L:
            ada_stage(nc, e, L, ada_w, ada_b, norm_w)
            ffn_stage(nc, e, L, 0, w_up, w_down, ada_w)
            with ExitStack() as mix:
                e.proj = mix.enter_context(nc.sbuf_tensor("proj", [P, TT, TOK_W], F32))
                e.const = mix.enter_context(nc.sbuf_tensor("const_sb", [P, CONST_W - BASE_W], F32))
                e.conv = mix.enter_context(nc.sbuf_tensor("conv", [P, N_CONV, SEQ], F32))
                e.qk_rms = mix.enter_context(nc.sbuf_tensor("qk_rms", [P, TT, ROPED], F32))
                e.qk_w = mix.enter_context(nc.sbuf_tensor("qk_norm_sb", [P, 4, HD], F32))
                proj_stage(nc, e, L, const, w_tok, w_gate, w_conv, conv_w)
                mlstm_stage(nc, e, L, m_gate_b, head_norm_w)
                delta_stage(nc, e, L, g_decay, head_norm_w, qk_norm)
                nsa_stage(nc, e, L, cmp_pos, cmp_w1, cmp_w2)
            out_stage(nc, e, L, w_out)
            ffn_stage(nc, e, L, 1, w_up, w_down, ada_w)
        store_stage(nc, e, out)


def laid_out(a):
    def kpn(w, n):
        *lead, K, N = w.shape
        v = w.reshape(*lead, K // P, P, N // n, n)
        d = len(lead)
        return v.transpose(*range(d), d + 2, d + 1, d, d + 3).reshape(*lead, N // n, P, K // P * n)

    def cols(v):
        *lead, K = v.shape
        return np.moveaxis(v.reshape(*lead, K // P, P), -1, -2)

    o = {}
    o["x_t"] = a["x"][0].T.reshape(KT, P, SEQ).transpose(1, 0, 2).reshape(P, -1)
    o["c_t"] = cols(a["c"][0])
    o["const"] = constants()
    o["ada_w"] = kpn(a["ada_w"], P)
    o["ada_b"] = cols(a["ada_b"])
    o["norm_w"] = cols(a["norm_w"].reshape(DEPTH, 3 * D_MODEL))
    up = a["ffn_w_up"].reshape(2 * DEPTH, KT, P, 2, FT, P)
    o["w_up"] = up.transpose(0, 4, 3, 2, 1, 5).reshape(2 * DEPTH, 2 * FT, P, -1)
    down = a["ffn_w_down"].reshape(2 * DEPTH, 2, FT // 2, P, KT, P)
    o["w_down"] = down.transpose(0, 4, 1, 3, 2, 5).reshape(2 * DEPTH, 2 * KT, P, -1)
    w = a["w_in"]
    m_in, g_w, mg, gg = 4 * M_W + 2 * M_HEADS, G_HEADS * HD, 2 * M_HEADS, 2 * G_HEADS
    m, g, n = w[:, :, :m_in], w[:, :, m_in:m_in + 4 * g_w + gg], w[:, :, m_in + 4 * g_w + gg:]
    conv_cols = g[:, :, :3 * g_w]
    tok_cols = np.concatenate([m[:, :, :-mg], g[:, :, 3 * g_w:4 * g_w], n[:, :, :-3 * N_HEADS]], 2)
    gate_cols = np.concatenate([m[:, :, -mg:], g[:, :, 4 * g_w:], n[:, :, -3 * N_HEADS:]], 2)
    tok = tok_cols.reshape(DEPTH, 2, KH, P, N_PG, PG)
    o["w_tok"] = tok.transpose(0, 4, 1, 3, 2, 5).reshape(DEPTH, 2 * N_PG, P, -1)
    o["w_gate"] = kpn(gate_cols, GATE_W)[:, 0]
    o["w_conv"] = kpn(conv_cols, P)
    o["conv_w"] = a["gdn_conv_w"].transpose(0, 2, 1).reshape(DEPTH, N_CONV, P, CONV_K).transpose(0, 2, 1, 3).reshape(DEPTH, P, -1)
    o["w_out"] = kpn(a["w_out"], P)
    o["m_gate_b"] = a["mlstm_gate_b"].reshape(DEPTH, 1, -1)
    o["head_norm_w"] = np.stack([a["mlstm_norm_w"], a["gdn_norm_w"]], 1).reshape(DEPTH, 1, -1)
    o["g_decay"] = np.concatenate([a["gdn_a_log"], a["gdn_dt_bias"]], 1).reshape(DEPTH, 1, -1)
    o["qk_norm"] = a["nsa_qk_norm"].reshape(DEPTH, 1, -1)
    pos = a["nsa_cmp_pos"].reshape(DEPTH, 2, CMP_BLOCK // 2, P)
    o["cmp_pos"] = pos.transpose(0, 3, 1, 2).reshape(DEPTH, P, -1)
    w1 = a["nsa_cmp_w1"].reshape(DEPTH, 2, CMP_BLOCK // 2, P, CMP_HIDDEN)
    o["cmp_w1"] = w1.transpose(0, 3, 1, 2, 4).reshape(DEPTH, P, -1)
    o["cmp_w2"] = a["nsa_cmp_w2"].reshape(DEPTH, 2, CMP_HIDDEN // P, P, HD).transpose(0, 3, 1, 2, 4).reshape(DEPTH, P, -1)
    return {k: np.ascontiguousarray(v) for k, v in o.items()}


def kernel(**inputs):
    import concourse.bacc as bacc
    from concourse.bass_utils import run_bass_kernel_spmd

    arrays = laid_out({k: np.asarray(v) for k, v in inputs.items()})
    nc = bacc.Bacc("TRN2", target_bir_lowering=False, num_devices=1)
    args = [nc.dram_tensor(f"in_{k}", v.shape, F32, kind="ExternalInput").ap() for k, v in arrays.items()]
    out = nc.dram_tensor("out_x", (P, KT * SEQ), F32, kind="ExternalOutput").ap()
    decoder_kernel(nc, *args, out)
    got = run_bass_kernel_spmd(nc, [{f"in_{k}": v for k, v in arrays.items()}], core_ids=[0]).results[0]["out_x"]
    return np.ascontiguousarray(got.reshape(P, KT, SEQ).transpose(1, 0, 2).reshape(D_MODEL, SEQ).T)[None]
```
